# Optimizing a Trainium2 kernel written in Bass

```python
import math
import jax, jax.numpy as jnp
from jax import lax
import numpy as np

D_MODEL = 1024
BATCH = 1
SEQ = 256
DEPTH = 2

CHUNK = 64
N_MIXERS = 2
N_A_LAYERS = (DEPTH + 1) // 2
N_B_LAYERS = DEPTH // 2
EPS = 1e-6

RET_HEADS = 4
RET_QK_DIM = D_MODEL // RET_HEADS
RET_V_DIM = 2 * RET_QK_DIM
RET_V_WIDTH = RET_HEADS * RET_V_DIM
RET_IN_WIDTH = 2 * D_MODEL + 2 * RET_V_WIDTH
ROPE_BASE = 10000.0

SGU_BLOCK = 128
SGU_GROUPS = 8
SGU_FFN = 6 * D_MODEL
SGU_HALF = SGU_FFN // 2
SGU_GROUP_DIM = SGU_HALF // SGU_GROUPS

PEER_HEADS = 8
PEER_NKEYS = 128
PEER_EXPERTS = PEER_NKEYS * PEER_NKEYS
PEER_KEY_DIM = 256
PEER_HALF = PEER_KEY_DIM // 2
PEER_TOPK = 16
PEER_TOKEN_BLOCK = 128


def rmsnorm(x, gain):
    x32 = x.astype(jnp.float32)
    y = x32 * lax.rsqrt(jnp.mean(x32 * x32, axis=-1, keepdims=True) + EPS)
    return (y * gain.astype(jnp.float32)).astype(x.dtype)

def layernorm(x, gain, bias):
    x32 = x.astype(jnp.float32)
    mu = jnp.mean(x32, axis=-1, keepdims=True)
    xc = x32 - mu
    y = xc * lax.rsqrt(jnp.mean(xc * xc, axis=-1, keepdims=True) + EPS)
    return (y * gain.astype(jnp.float32) + bias.astype(jnp.float32)).astype(x.dtype)

def modulate(h, shift, scale):
    return h * (1 + scale[:, None, :]) + shift[:, None, :]

def rotary(x, positions):
    half = x.shape[-1] // 2
    inv_freq = 1.0 / (ROPE_BASE ** (jnp.arange(half, dtype=jnp.float32) / half))
    ang = positions.astype(jnp.float32)[..., None] * inv_freq
    cos = jnp.cos(ang)[:, :, None, :]
    sin = jnp.sin(ang)[:, :, None, :]
    x32 = x.astype(jnp.float32)
    x1, x2 = x32[..., :half], x32[..., half:]
    return jnp.concatenate([x1 * cos - x2 * sin, x1 * sin + x2 * cos], axis=-1)

def retention_mixer(h, positions, w_in, w_out):
    B, S, _ = h.shape
    nc = S // CHUNK
    H, Dk, Dv = RET_HEADS, RET_QK_DIM, RET_V_DIM
    proj = h @ w_in
    q, k, v, g = jnp.split(proj, [D_MODEL, 2 * D_MODEL, 2 * D_MODEL + RET_V_WIDTH], axis=-1)
    q = rotary(q.reshape(B, S, H, Dk), positions)
    k = rotary(k.reshape(B, S, H, Dk), positions) * (Dk ** -0.5)
    v = v.reshape(B, S, H, Dv).astype(jnp.float32)
    log_gamma = jnp.log(1.0 - 2.0 ** (-5.0 - jnp.arange(H, dtype=jnp.float32)))
    idx = jnp.arange(CHUNK, dtype=jnp.float32)
    d_intra = jnp.exp(log_gamma[:, None, None] * jnp.abs(idx[:, None] - idx[None, :]))
    xi = jnp.exp(log_gamma[None, :] * (idx[:, None] + 1.0))
    zeta = jnp.exp(log_gamma[None, :] * (CHUNK - 1.0 - idx[:, None]))
    gamma_chunk = jnp.exp(log_gamma * CHUNK)

    def to_chunks(t):
        return jnp.moveaxis(t.reshape(B, nc, CHUNK, H, t.shape[-1]), 1, 0)

    def step(state, inp):
        qi, ki, vi = inp
        scores = jnp.einsum('bihd,bjhd->bhij', qi, ki) * d_intra[None]
        intra = jnp.einsum('bhij,bjhe->bihe', scores, vi)
        cross = jnp.einsum('bihd,bhde->bihe', qi * xi[None, :, :, None], state)
        state = state * gamma_chunk[None, :, None, None] + jnp.einsum(
            'bjhd,bjhe->bhde', ki * zeta[None, :, :, None], vi)
        return state, intra + cross

    state0 = jnp.zeros((B, H, Dk, Dv), jnp.float32)
    _, y = lax.scan(step, state0, (to_chunks(q), to_chunks(k), to_chunks(v)))
    y = jnp.moveaxis(y, 0, 1).reshape(B, S, H, Dv)
    y = y * lax.rsqrt(jnp.mean(y * y, axis=-1, keepdims=True) + EPS)
    y = y.reshape(B, S, RET_V_WIDTH).astype(h.dtype)
    return (jax.nn.silu(g) * y) @ w_out

def sgu_mixer(h, w_in, b_in, ln_g, ln_b, w_s, b_s, w_out):
    B, S, _ = h.shape
    nb = S // SGU_BLOCK
    z = jax.nn.gelu(h @ w_in + b_in)
    u, v = jnp.split(z, 2, axis=-1)
    v = layernorm(v, ln_g, ln_b)
    pos_chunk = jnp.arange(SGU_BLOCK) // CHUNK
    mask = (pos_chunk[None, :] <= pos_chunk[:, None]).astype(w_s.dtype)
    vb = v.reshape(B, nb, SGU_BLOCK, SGU_GROUPS, SGU_GROUP_DIM)
    s = jnp.einsum('gij,bnjgc->bnigc', w_s * mask[None], vb) + b_s.T[None, None, :, :, None]
    s = s.reshape(B, S, SGU_HALF)
    return (u * s) @ w_out

def peer_ffn(h, w_query, sub_keys, expert_u, expert_v):
    B, S, D = h.shape
    T = B * S
    Hh, K = PEER_HEADS, PEER_TOPK
    ht = h.reshape(T, D)
    q = (ht @ w_query).reshape(T, Hh, 2, PEER_HALF).astype(jnp.float32)
    scores = jnp.einsum('thpd,hpkd->thpk', q, sub_keys.astype(jnp.float32))
    s_top, i_top = lax.top_k(scores, K)
    cand = (s_top[:, :, 0, :, None] + s_top[:, :, 1, None, :]).reshape(T, Hh, K * K)
    cand_idx = (i_top[:, :, 0, :, None] * PEER_NKEYS + i_top[:, :, 1, None, :]).reshape(T, Hh, K * K)
    best, pos = lax.top_k(cand, K)
    expert_idx = jnp.take_along_axis(cand_idx, pos, axis=-1)
    gates = jax.nn.softmax(best, axis=-1).astype(h.dtype)
    nb = T // PEER_TOKEN_BLOCK

    def block(args):
        xb, idx, g = args
        u = expert_u[idx]
        a = jax.nn.gelu(jnp.einsum('tkd,td->tk', u, xb)) * g
        return jnp.einsum('tk,tkd->td', a, expert_v[idx])

    out = lax.map(block, (ht.reshape(nb, PEER_TOKEN_BLOCK, D),
                          expert_idx.reshape(nb, PEER_TOKEN_BLOCK, Hh * K),
                          gates.reshape(nb, PEER_TOKEN_BLOCK, Hh * K)))
    return out.reshape(B, S, D)

def first_inputs(seed: int = 0) -> dict:
    key = jax.random.key(seed)
    ks = jax.random.split(key, 24)
    f32 = jnp.float32
    D = D_MODEL

    def nrm(k, shape, scale):
        return jax.random.normal(k, shape, f32) * scale

    return {
        "x": nrm(ks[0], (BATCH, SEQ, D), 1.0),
        "c": nrm(ks[1], (BATCH, D), 1.0),
        "positions": jnp.broadcast_to(jnp.arange(SEQ, dtype=jnp.int32), (BATCH, SEQ)),
        "norm_mix": 1.0 + nrm(ks[2], (DEPTH, D), 0.05),
        "norm_ffn": 1.0 + nrm(ks[3], (DEPTH, D), 0.05),
        "ada_w": nrm(ks[4], (DEPTH, D, 6 * D), 0.5 * D ** -0.5),
        "ada_b": nrm(ks[5], (DEPTH, 6 * D), 0.02),
        "ret_w_in": nrm(ks[6], (N_A_LAYERS, D, RET_IN_WIDTH), D ** -0.5),
        "ret_w_out": nrm(ks[7], (N_A_LAYERS, RET_V_WIDTH, D), RET_V_WIDTH ** -0.5),
        "sgu_w_in": nrm(ks[8], (N_B_LAYERS, D, SGU_FFN), D ** -0.5),
        "sgu_b_in": nrm(ks[9], (N_B_LAYERS, SGU_FFN), 0.02),
        "sgu_ln_g": 1.0 + nrm(ks[10], (N_B_LAYERS, SGU_HALF), 0.05),
        "sgu_ln_b": nrm(ks[11], (N_B_LAYERS, SGU_HALF), 0.02),
        "sgu_w_s": nrm(ks[12], (N_B_LAYERS, SGU_GROUPS, SGU_BLOCK, SGU_BLOCK), SGU_BLOCK ** -0.5),
        "sgu_b_s": 1.0 + nrm(ks[13], (N_B_LAYERS, SGU_GROUPS, SGU_BLOCK), 0.1),
        "sgu_w_out": nrm(ks[14], (N_B_LAYERS, SGU_HALF, D), SGU_HALF ** -0.5),
        "peer_w_query": nrm(ks[15], (DEPTH, D, PEER_HEADS * PEER_KEY_DIM), D ** -0.5),
        "peer_sub_keys": nrm(ks[16], (DEPTH, PEER_HEADS, 2, PEER_NKEYS, PEER_HALF), PEER_HALF ** -0.5),
        "peer_u": nrm(ks[17], (DEPTH, PEER_EXPERTS, D), D ** -0.5),
        "peer_v": nrm(ks[18], (DEPTH, PEER_EXPERTS, D), 0.5),
        "norm_final": 1.0 + nrm(ks[19], (D,), 0.05),
    }

def first_block(x, c, positions, norm_mix, norm_ffn, ada_w, ada_b, ret_w_in, ret_w_out,
              sgu_w_in, sgu_b_in, sgu_ln_g, sgu_ln_b, sgu_w_s, sgu_b_s, sgu_w_out,
              peer_w_query, peer_sub_keys, peer_u, peer_v, norm_final):
    c_act = jax.nn.silu(c)
    for layer in range(DEPTH):
        mod = c_act @ ada_w[layer] + ada_b[layer]
        sh1, sc1, g1, sh2, sc2, g2 = jnp.split(mod, 6, axis=-1)
        h = modulate(rmsnorm(x, norm_mix[layer]), sh1, sc1)
        j = layer // N_MIXERS
        if layer % N_MIXERS == 0:
            y = retention_mixer(h, positions, ret_w_in[j], ret_w_out[j])
        else:
            y = sgu_mixer(h, sgu_w_in[j], sgu_b_in[j], sgu_ln_g[j], sgu_ln_b[j],
                          sgu_w_s[j], sgu_b_s[j], sgu_w_out[j])
        x = x + g1[:, None, :] * y
        h = modulate(rmsnorm(x, norm_ffn[layer]), sh2, sc2)
        x = x + g2[:, None, :] * peer_ffn(h, peer_w_query[layer], peer_sub_keys[layer],
                                          peer_u[layer], peer_v[layer])
    return rmsnorm(x, norm_final)


N_META = 16
ATT_BLOCK = 128
ATT_HEADS = 16
ATT_HEAD_DIM = 64
DN_HEADS = 8
DN_HEAD_DIM = 128
DN_CONV = 4
DN_CHUNK = 64
FFN_DIM = 2816
FFN_CONV = 3
N_ATTN_LAYERS = (DEPTH + 1) // 2
N_DN_LAYERS = DEPTH // 2
ATT_HD = ATT_HEADS * ATT_HEAD_DIM
DN_HD = DN_HEADS * DN_HEAD_DIM
ATT_IN = 4 * ATT_HD + ATT_HEADS
DN_IN = 4 * DN_HD + 2 * DN_HEADS
NEG = -1e30


def rmsnorm_2(x, g):
    xf = x.astype(jnp.float32)
    y = xf * lax.rsqrt(jnp.mean(xf * xf, axis=-1, keepdims=True) + EPS)
    return (y * g.astype(jnp.float32)).astype(x.dtype)

def l2norm(x):
    xf = x.astype(jnp.float32)
    return xf * lax.rsqrt(jnp.sum(xf * xf, axis=-1, keepdims=True) + EPS)

def causal_dwconv(x, w):
    K, C = w.shape
    return lax.conv_general_dilated(
        x, w[:, None, :].astype(x.dtype), window_strides=(1,), padding=[(K - 1, 0)],
        dimension_numbers=('NWC', 'WIO', 'NWC'), feature_group_count=C)

def forgetting_attention(h, w_in, b_forget, q_gain, k_gain, w_out):
    B, L, _ = h.shape
    pad = (-L) % ATT_BLOCK
    hp = jnp.pad(h, ((0, 0), (pad, 0), (0, 0)))
    Lp = L + pad
    proj = hp @ w_in
    q, k, v, og, fl = jnp.split(proj, [ATT_HD, 2 * ATT_HD, 3 * ATT_HD, 4 * ATT_HD], axis=-1)
    q = rmsnorm_2(q.reshape(B, Lp, ATT_HEADS, ATT_HEAD_DIM), q_gain).transpose(0, 2, 1, 3)
    k = rmsnorm_2(k.reshape(B, Lp, ATT_HEADS, ATT_HEAD_DIM), k_gain).transpose(0, 2, 1, 3)
    v = v.reshape(B, Lp, ATT_HEADS, ATT_HEAD_DIM).transpose(0, 2, 1, 3)
    logf = jax.nn.log_sigmoid(fl.astype(jnp.float32) + b_forget.astype(jnp.float32))
    c = jnp.cumsum(logf, axis=1).transpose(0, 2, 1)
    pos = jnp.arange(Lp)
    n_blk = Lp // ATT_BLOCK
    qb = q.reshape(B, ATT_HEADS, n_blk, ATT_BLOCK, ATT_HEAD_DIM).transpose(2, 0, 1, 3, 4)
    cb = c.reshape(B, ATT_HEADS, n_blk, ATT_BLOCK).transpose(2, 0, 1, 3)
    pb = pos.reshape(n_blk, ATT_BLOCK)
    scale = ATT_HEAD_DIM ** -0.5

    def one_block(args):
        q_i, c_i, p_i = args
        s = jnp.einsum('bhqd,bhkd->bhqk', q_i, k).astype(jnp.float32) * scale
        s = s + c_i[..., :, None] - c[:, :, None, :]
        mask = (pos[None, :] <= p_i[:, None]) & (pos[None, :] >= pad)
        p = jax.nn.softmax(jnp.where(mask, s, NEG), axis=-1)
        return jnp.einsum('bhqk,bhkd->bhqd', p.astype(v.dtype), v)

    o = lax.map(one_block, (qb, cb, pb))
    o = o.transpose(1, 0, 3, 2, 4).reshape(B, Lp, ATT_HD)
    o = o * jax.nn.sigmoid(og)
    return (o @ w_out)[:, pad:]

def gated_deltanet(h, w_in, conv_w, a_log, dt_bias, o_gain, w_out):
    B, L, _ = h.shape
    H, Dh, C = DN_HEADS, DN_HEAD_DIM, DN_CHUNK
    pad = (-L) % C
    hp = jnp.pad(h, ((0, 0), (pad, 0), (0, 0)))
    Lp = L + pad
    N = Lp // C
    proj = hp @ w_in
    qkv, og, b_logit, a_logit = jnp.split(proj, [3 * DN_HD, 4 * DN_HD, 4 * DN_HD + H], axis=-1)
    qkv = jax.nn.silu(causal_dwconv(qkv, conv_w))
    q, k, v = jnp.split(qkv, [DN_HD, 2 * DN_HD], axis=-1)
    q = l2norm(q.reshape(B, Lp, H, Dh)) * (Dh ** -0.5)
    k = l2norm(k.reshape(B, Lp, H, Dh))
    v = v.reshape(B, Lp, H, Dh).astype(jnp.float32)
    beta = jax.nn.sigmoid(b_logit.astype(jnp.float32))
    g = -jnp.exp(a_log.astype(jnp.float32)) * jax.nn.softplus(
        a_logit.astype(jnp.float32) + dt_bias.astype(jnp.float32))

    def chunk(t):
        return t.reshape(B, N, C, H, Dh).transpose(0, 3, 1, 2, 4)
    qc, kc, vc = chunk(q), chunk(k), chunk(v)
    bc = beta.reshape(B, N, C, H).transpose(0, 3, 1, 2)
    gc = jnp.cumsum(g.reshape(B, N, C, H).transpose(0, 3, 1, 2), axis=-1)
    idx = jnp.arange(C)
    strict = idx[:, None] > idx[None, :]
    incl = idx[:, None] >= idx[None, :]
    dec = jnp.exp(jnp.where(incl, gc[..., :, None] - gc[..., None, :], -jnp.inf))
    kk = jnp.einsum('bhnid,bhnjd->bhnij', kc, kc)
    A = jnp.where(strict, kk * dec * bc[..., :, None], 0.0)
    lhs = A + jnp.eye(C, dtype=jnp.float32)
    rhs = jnp.concatenate([kc * (bc * jnp.exp(gc))[..., None], vc * bc[..., None]], axis=-1)
    sol = lax.linalg.triangular_solve(lhs, rhs, left_side=True, lower=True, unit_diagonal=True)
    W, U0 = sol[..., :Dh], sol[..., Dh:]
    qk = jnp.einsum('bhnid,bhnjd->bhnij', qc, kc) * dec
    q_dec = qc * jnp.exp(gc)[..., None]
    k_dec = kc * jnp.exp(gc[..., -1:] - gc)[..., None]
    g_last = jnp.exp(gc[..., -1])

    def to_n(t):
        return jnp.moveaxis(t, 2, 0)

    def step(S, xs):
        W_n, U0_n, qk_n, qd_n, kd_n, gl_n = xs
        U = U0_n - jnp.einsum('bhcd,bhvd->bhcv', W_n, S)
        O = jnp.einsum('bhcd,bhvd->bhcv', qd_n, S) + jnp.einsum('bhij,bhjv->bhiv', qk_n, U)
        S = gl_n[..., None, None] * S + jnp.einsum('bhcv,bhcd->bhvd', U, kd_n)
        return S, O

    S0 = jnp.zeros((B, H, Dh, Dh), jnp.float32)
    _, O = lax.scan(step, S0, (to_n(W), to_n(U0), to_n(qk), to_n(q_dec), to_n(k_dec), to_n(g_last)))
    O = O.transpose(1, 0, 3, 2, 4).reshape(B, Lp, H, Dh)
    O = rmsnorm_2(O, o_gain) * jax.nn.silu(og.reshape(B, Lp, H, Dh).astype(jnp.float32))
    return (O.reshape(B, Lp, DN_HD).astype(h.dtype) @ w_out)[:, pad:]

def conv_ffn(h, w_up, conv_w, w_down):
    u = causal_dwconv(h @ w_up, conv_w)
    gate, up = jnp.split(u, [FFN_DIM], axis=-1)
    return (jax.nn.gelu(gate, approximate=True) * up) @ w_down

def second_inputs(seed: int = 0) -> dict:
    key = jax.random.key(seed)
    ks = jax.random.split(key, 24)
    D = D_MODEL
    nrm = lambda k, shape, s: jax.random.normal(k, shape, jnp.float32) * s
    gain = lambda k, shape: 1.0 + 0.1 * jax.random.normal(k, shape, jnp.float32)
    dt = jnp.exp(jax.random.uniform(ks[12], (N_DN_LAYERS, DN_HEADS), jnp.float32,
                                    np.log(1e-3), np.log(1e-1)))
    return {
        "x": nrm(ks[0], (BATCH, SEQ, D), 1.0),
        "meta_tokens": nrm(ks[1], (N_META, D), 1.0),
        "norm_mix_pre": gain(ks[2], (DEPTH, D)),
        "norm_mix_post": gain(ks[3], (DEPTH, D)),
        "norm_ffn_pre": gain(ks[4], (DEPTH, D)),
        "norm_ffn_post": gain(ks[5], (DEPTH, D)),
        "attn_w_in": nrm(ks[6], (N_ATTN_LAYERS, D, ATT_IN), D ** -0.5),
        "attn_b_forget": jax.random.uniform(ks[7], (N_ATTN_LAYERS, ATT_HEADS), jnp.float32, 2.0, 6.0),
        "attn_q_norm": gain(ks[8], (N_ATTN_LAYERS, ATT_HEAD_DIM)),
        "attn_k_norm": gain(ks[9], (N_ATTN_LAYERS, ATT_HEAD_DIM)),
        "attn_w_out": nrm(ks[10], (N_ATTN_LAYERS, ATT_HD, D), ATT_HD ** -0.5),
        "dn_w_in": nrm(ks[11], (N_DN_LAYERS, D, DN_IN), D ** -0.5),
        "dn_conv": nrm(ks[13], (N_DN_LAYERS, DN_CONV, 3 * DN_HD), DN_CONV ** -0.5),
        "dn_a_log": jnp.log(jax.random.uniform(ks[14], (N_DN_LAYERS, DN_HEADS), jnp.float32, 1.0, 16.0)),
        "dn_dt_bias": dt + jnp.log(-jnp.expm1(-dt)),
        "dn_o_norm": gain(ks[15], (N_DN_LAYERS, DN_HEAD_DIM)),
        "dn_w_out": nrm(ks[16], (N_DN_LAYERS, DN_HD, D), DN_HD ** -0.5),
        "ffn_w_up": nrm(ks[17], (DEPTH, D, 2 * FFN_DIM), D ** -0.5),
        "ffn_conv": nrm(ks[18], (DEPTH, FFN_CONV, 2 * FFN_DIM), FFN_CONV ** -0.5),
        "ffn_w_down": nrm(ks[19], (DEPTH, FFN_DIM, D), FFN_DIM ** -0.5),
    }

def second_block(x, meta_tokens, norm_mix_pre, norm_mix_post, norm_ffn_pre, norm_ffn_post,
              attn_w_in, attn_b_forget, attn_q_norm, attn_k_norm, attn_w_out,
              dn_w_in, dn_conv, dn_a_log, dn_dt_bias, dn_o_norm, dn_w_out,
              ffn_w_up, ffn_conv, ffn_w_down):
    B = x.shape[0]
    meta = jnp.broadcast_to(meta_tokens[None].astype(x.dtype), (B, N_META, x.shape[-1]))
    h = jnp.concatenate([meta, x], axis=1)
    for i in range(DEPTH):
        j = i // 2
        a = rmsnorm_2(h, norm_mix_pre[i])
        if i % 2 == 0:
            m = forgetting_attention(a, attn_w_in[j], attn_b_forget[j], attn_q_norm[j],
                                     attn_k_norm[j], attn_w_out[j])
        else:
            m = gated_deltanet(a, dn_w_in[j], dn_conv[j], dn_a_log[j], dn_dt_bias[j],
                               dn_o_norm[j], dn_w_out[j])
        h = h + rmsnorm_2(m, norm_mix_post[i])
        f = conv_ffn(rmsnorm_2(h, norm_ffn_pre[i]), ffn_w_up[i], ffn_conv[i], ffn_w_down[i])
        h = h + rmsnorm_2(f, norm_ffn_post[i])
    return h[:, N_META:]


def setup_inputs(seed=0):
    out = dict(first_inputs(seed))
    for name, value in second_inputs(seed + 1).items():
        if name != "x":
            out[name + "_2"] = value
    return out


def reference(
    x, c, positions, norm_mix, norm_ffn, ada_w, ada_b, ret_w_in, ret_w_out, sgu_w_in, sgu_b_in,
    sgu_ln_g, sgu_ln_b, sgu_w_s, sgu_b_s, sgu_w_out, peer_w_query, peer_sub_keys, peer_u,
    peer_v, norm_final, meta_tokens_2, norm_mix_pre_2, norm_mix_post_2, norm_ffn_pre_2,
    norm_ffn_post_2, attn_w_in_2, attn_b_forget_2, attn_q_norm_2, attn_k_norm_2, attn_w_out_2,
    dn_w_in_2, dn_conv_2, dn_a_log_2, dn_dt_bias_2, dn_o_norm_2, dn_w_out_2, ffn_w_up_2,
    ffn_conv_2, ffn_w_down_2,
):
    x = first_block(
        x, c, positions, norm_mix, norm_ffn, ada_w, ada_b, ret_w_in, ret_w_out, sgu_w_in,
        sgu_b_in, sgu_ln_g, sgu_ln_b, sgu_w_s, sgu_b_s, sgu_w_out, peer_w_query, peer_sub_keys,
        peer_u, peer_v, norm_final,
    )
    return second_block(
        x, meta_tokens_2, norm_mix_pre_2, norm_mix_post_2, norm_ffn_pre_2, norm_ffn_post_2,
        attn_w_in_2, attn_b_forget_2, attn_q_norm_2, attn_k_norm_2, attn_w_out_2, dn_w_in_2,
        dn_conv_2, dn_a_log_2, dn_dt_bias_2, dn_o_norm_2, dn_w_out_2, ffn_w_up_2, ffn_conv_2,
        ffn_w_down_2,
    )


_drawn_inputs = setup_inputs


def setup_inputs(seed=0):
    import zlib

    import numpy as np

    out = dict(_drawn_inputs(seed))
    spreads = {}
    factors = {'sgu_ln_b': 4.659}
    for name, (base, spread) in spreads.items():
        noise = np.random.default_rng([zlib.crc32(name.encode()), seed]).standard_normal(out[name].shape)
        drawn = base * np.exp(spread * noise) if base else spread * noise
        out[name] = __import__('jax').numpy.asarray(drawn.astype(out[name].dtype))
    for name, factor in factors.items():
        out[name] = (out[name] * factor).astype(out[name].dtype)
    return out
```

```python
from contextlib import ExitStack, contextmanager

import numpy as np

P = 128
D = 1024
KT = D // P
SEQ = 256
META = 16
TOK = SEQ + META
T0 = META
RAW = 4
ADA_UNITS = 96
ROUND = 8
BANK = 512
EPS = 1e-6
NEG = -1e30
TWO_PI_PARTS = (6.28125, 1.9350051879882812e-03, 3.0199159819567e-07)
RH, RDK, RDV = 4, 256, 512
CHUNK = 64
HH, TOPK, NKEYS = 8, 16, 128
SG, SH = 8, 3072
ST_ = SH // P
AH, ADH = 16, 64
DH = 8
FFT = 2816 // P
TILES = [(0, META), (META, P), (META + P, P)]
LEVELS = 7

PCOLS = [("c", 8), ("ada_b", 96), ("norm_mix", 16), ("norm_ffn", 16), ("norm_final", 8), ("sgu_b_in", 48),
         ("sgu_ln_g", 24), ("sgu_ln_b", 24), ("mix_pre", 16), ("mix_post", 16), ("ffn_pre", 16), ("ffn_post", 16),
         ("q_gain", 1), ("k_gain", 1), ("o_gain", 1), ("ffn_conv", 2 * 44 * 3), ("dn_conv", 24 * 4),
         ("b_forget", 16), ("a_log", 8), ("dt_bias", 8)]
PO, _o = {}, 0
for _n, _w in PCOLS:
    PO[_n] = _o
    _o += _w
PW = _o
C1COLS = [("ident", 128), ("iota", 128), ("inv_freq", 1)]
C2COLS = [("tri", 3 * TOK), ("causal", 128), ("mneg", 128), ("levels", LEVELS * 128), ("colsel", 64), ("colsel1", 32),
          ("rowsel", 16 * 128), ("rowsel1", 16 * 128), ("half", 2), ("selbot", 16), ("seltop", 16)]


def offsets(cols):
    out, at = {}, 0
    for name, width in cols:
        out[name] = (at, width)
        at += width
    return out, at


C1O, C1W = offsets(C1COLS)
C2O, C2W = offsets(C2COLS)


def shape_constants():
    c1 = np.zeros((P, C1W), np.float32)
    c2 = np.zeros((P, C2W), np.float32)

    def put(c, o, name, v):
        a, w = o[name]
        v = np.asarray(v, np.float32).reshape(v.shape[0], w)
        c[:v.shape[0], a:a + w] = v

    put(c1, C1O, "ident", np.eye(P))
    put(c1, C1O, "iota", np.tile(np.arange(P, dtype=np.float32), (P, 1)))
    half = RDK // 2
    put(c1, C1O, "inv_freq", (np.float32(1.0) / (np.float32(10000.0) ** (
        np.arange(half, dtype=np.float32) / np.float32(half)))).reshape(P, 1))
    tri = np.zeros((P, 3, TOK))
    for t, (s, n) in enumerate(TILES):
        for j in range(n):
            tri[j, t, s + j:] = 1.0
    put(c2, C2O, "tri", tri)
    i = np.arange(P)
    put(c2, C2O, "causal", np.where(i[None, :] > i[:, None], NEG, 0.0))
    put(c2, C2O, "mneg", np.where(i[None, :] < i[:, None], NEG, 0.0))
    lv = np.zeros((P, LEVELS, P))
    for n in range(LEVELS):
        b = 1 << n
        lv[:, n, :] = ((i[None, :] // b) % 2 == 1) & (i[:, None] // b == i[None, :] // b - 1)
    put(c2, C2O, "levels", lv)
    cs = np.zeros((P, 64))
    cs[:64, 32] = 1
    cs[64:, 33] = 1
    put(c2, C2O, "colsel", cs)
    cs = np.zeros((P, 32))
    cs[:, 16] = 1
    put(c2, C2O, "colsel1", cs)
    rs = np.zeros((32, 16, P))
    rs1 = np.zeros((16, 16, P))
    for b in range(16):
        rs[2 * b, b, :64] = 1
        rs[2 * b + 1, b, 64:] = 1
        rs1[b, b, :] = 1
    put(c2, C2O, "rowsel", rs)
    put(c2, C2O, "rowsel1", rs1)
    hf = np.zeros((32, 2))
    hf[:16, 0] = 1
    hf[16:, 1] = 1
    put(c2, C2O, "half", hf)
    sb = np.zeros((32, 16))
    stp = np.zeros((32, 16))
    for h in range(16):
        stp[h, h] = 1
        sb[16 + h, h] = 1
    put(c2, C2O, "selbot", sb)
    put(c2, C2O, "seltop", stp)
    ret = np.zeros((P, 2, RH, SEQ))
    pos = np.arange(SEQ)
    for h in range(RH):
        lg = np.log(1.0 - 2.0 ** (-5.0 - h))
        dist = np.abs(pos[None, :] - pos[:, None]).astype(np.float64)
        d = np.exp(lg * dist) * (pos[None, :] // CHUNK >= pos[:, None] // CHUNK)
        ret[:, :, h, :] = (d * RDK ** -0.5).reshape(2, P, SEQ).transpose(1, 0, 2)
    return c1, c2, ret.astype(np.float32).reshape(P, -1)


class At:

    def __init__(self, unit, b=None, step=ROUND):
        self.unit, self.b, self.step = unit, b, step
        self.raw = unit % RAW

    def plus(self, n):
        return At(self.unit + n, self.b, self.step)

    def number(self, k=0):
        return self.unit + k if self.b is None else self.b * self.step + (self.unit + k)

    def fill(self):
        n = self.unit // RAW + 1
        return n if self.b is None else self.b * (self.step // RAW) + n

    def halves(self, k):
        n = 2 * (self.unit - ADA_UNITS) + k
        return n if self.b is None else self.b * (2 * self.step) + n

    def slot(self, half):
        return (2 * self.unit + half) % 4


class Counts:

    def __init__(self, engine, own=None):
        self.engine, self.own, self.n, self.reg, self.per = engine, own, {}, None, {}

    def value(self, sem):
        v = self.n.get(sem.name, 0)
        return self.reg * self.per.get(sem.name, 0) + v if self.reg is not None else v

    def next(self, sem, k=1):
        self.n[sem.name] = self.n.get(sem.name, 0) + k
        return self.value(sem)

    def link(self, instruction):
        instruction.then_inc(self.own, 1)
        self.engine.wait_ge(self.own, self.next(self.own))

    @contextmanager
    def loop(self, count, **per):
        with self.engine.Fori(0, count) as i:
            before = dict(self.n)
            self.reg, self.per = i, per
            yield i
            self.reg = None
        for name in self.n:
            grew = self.n[name] - before.get(name, 0)
            assert grew == per.get(name, 0), (name, grew, per.get(name, 0))
            self.n[name] += grew * (count - 1)


def build_program(nc, t, out, until=None, taps=None):
    from concourse import mybir
    f32, bf16, u32, i32 = mybir.dt.float32, mybir.dt.bfloat16, mybir.dt.uint32, mybir.dt.int32
    ALU, ACT = mybir.AluOpType, mybir.ActivationFunctionType
    AX = mybir.AxisListType.X
    MUL, ADD, SUB = ALU.mult, ALU.add, ALU.subtract

    ctx = ExitStack()
    with ctx:
        def sb(name, shape, dt=f32):
            return ctx.enter_context(nc.sbuf_tensor(name, shape, dt))

        f32r = mybir.dt.float32r
        raw = sb("raw", [P, RAW, KT, P])
        w_hi = sb("w_hi", [P, 4, KT // 2, P], f32r)
        w_lo = sb("w_lo", [P, 4, KT // 2, P], f32r)
        x = sb("x", [P, KT, TOK])
        h_hi = sb("h_hi", [P, KT, TOK], f32r)
        h_lo = sb("h_lo", [P, KT, TOK], f32r)
        params = sb("params", [P, PW])
        const1 = sb("const1", [P, C1W])
        ones = sb("ones", [P, P])
        zeros_b = sb("zeros_b", [P, P], bf16)
        small = sb("small", [P, 4])
        mods = sb("mods", [P, 96])
        gains = sb("gains", [P, 4, KT])
        rstd = sb("rstd", [P, TOK])
        mixed_hi = sb("mixed_hi", [P, 2, SEQ], f32r)
        mixed_lo = sb("mixed_lo", [P, 2, SEQ], f32r)
        pick_i = sb("pick_i", [P, 2, 4, P])
        pick_j = sb("pick_j", [P, 2, 4, P])
        chosen = sb("chosen", [P, 3, SEQ])
        mixin = chosen[:, 0:2, :]
        arena = sb("arena", [P, 32768])
        ps = ctx.enter_context(nc.psum_tensor("ps", [P, 8, BANK], f32))

        def view(at, *shape):
            n = int(np.prod(shape))
            a = arena[:, at:at + n]
            if len(shape) == 1:
                return a
            names = " ".join(f"d{k}" for k in range(len(shape)))
            return a.rearrange(f"p ({names}) -> p {names}", **{f"d{k}": s for k, s in enumerate(shape[:-1])})

        ident = const1[:, 0:128]
        iota = const1[:, 128:256]
        inv_freq = const1[:, 256:257]
        eps, half_pi = small[:, 0:1], small[:, 1:2]

        def par(name, k=0, n=1):
            return params[:, PO[name] + k:PO[name] + k + n]

        def bc(ap, axis, shape):
            return ap.unsqueeze(axis).to_broadcast(list(shape))

        def sem(name):
            return ctx.enter_context(nc.semaphore(name))

        s_consts_in = sem("consts_in")
        s_ret_in = sem("ret_in")
        s_keys_in = sem("keys_in")
        s_sgu_in = sem("sgu_in")
        s_tabs_in = sem("tabs_in")
        s_row_out = sem("row_out")
        s_row_in = sem("row_in")
        s_out_done = sem("out_done")
        s_result_ready = sem("result_ready")
        s_memsets = sem("memsets")
        s_met = sem("met")
        s_half_used = sem("half_used")
        s_hi_ready = sem("hi_ready")
        s_raw_free = sem("raw_free")
        s_bank_free = sem("bank_free")
        s_act_own = sem("act_own")
        s_dve_own = sem("dve_own")
        s_c_act = sem("c_act")
        s_rope_args = sem("rope_args")
        s_rope_ready = sem("rope_ready")
        s_ada_row = sem("ada_row")
        s_ada_t = sem("ada_t")
        s_squares = sem("squares")
        s_sums = sem("sums")
        s_mean_sum = sem("mean_sum")
        s_root = sem("root")
        s_inv = sem("inv")
        s_tap_done = sem("tap_done")
        s_h_scaled = sem("h_scaled")
        s_h_whole = sem("h_whole")
        s_act_hi = sem("act_hi")
        s_h_ready = sem("h_ready")
        s_acc_done = sem("acc_done")
        s_out_ready = sem("out_ready")
        s_x_ready = sem("x_ready")
        s_vt_ready = sem("vt_ready")
        s_vt_copied = sem("vt_copied")
        s_scores_ready = sem("scores_ready")
        s_decayed = sem("decayed")
        s_y_ready = sem("y_ready")
        s_y_copied = sem("y_copied")
        s_key_scores = sem("key_scores")
        s_key_copied = sem("key_copied")
        s_gate_in = sem("gate_in")
        s_gate_exp = sem("gate_exp")
        s_picks_ready = sem("picks_ready")
        s_tables_ready = sem("tables_ready")
        s_g_banks = sem("g_banks")
        s_g_copied = sem("g_copied")
        s_gelu_done = sem("gelu_done")
        s_mix_done = sem("mix_done")
        s_sgu_centred = sem("sgu_centred")
        s_sgu_ready = sem("sgu_ready")
        s_spatial_ready = sem("spatial_ready")
        s_sgu_s = sem("sgu_s")
        s_norms = sem("norms")
        s_scaled = sem("scaled")
        s_heads_prep = sem("heads_prep")
        s_cum_ready = sem("cum_ready")
        s_att_s = sem("att_s")
        s_att_m = sem("att_m")
        s_att_p = sem("att_p")
        s_att_pn = sem("att_pn")
        s_att_t = sem("att_t")
        s_att_tc = sem("att_tc")
        s_att_o = sem("att_o")
        s_att_od = sem("att_od")
        s_logit_in = sem("logit_in")
        s_logit_exp = sem("logit_exp")
        s_ffn_gelu = sem("ffn_gelu")
        s_dn_silu = sem("dn_silu")
        s_dn_p = sem("dn_p")
        s_dn_v = sem("dn_v")
        s_fo_copied = sem("fo_copied")
        full = [ctx.enter_context(nc.semaphore(f"raw_full{k}")) for k in range(RAW)]

        ada_row = arena[0:1, 0:12288]
        ada_sq = arena[0:96, 12288:12416]
        rope = view(16384, 8, SEQ)
        posn = view(18432, SEQ).bitcast(i32)
        qk = view(0, 16, SEQ)
        vT = view(4096, 16, SEQ)
        gT = view(8192, 16, SEQ)
        vtok = view(12288, 2, 2048)
        cosT, sinT = rope[:, 6, :], rope[:, 7, :]
        ropet = view(18688, 4, 2048)
        yT = view(0, 16, SEQ)
        sT = view(4096, RH, 2, SEQ)
        ysq = view(18688, 16, SEQ)
        yrs = view(22784, RH, SEQ)
        ret_dec = view(26880, 2, RH, SEQ)
        sq = view(22400, KT, TOK)
        h = sq
        qT = view(0, 16, SEQ)
        keysT = view(4096, 16, P)
        sc = view(6144, 2, 16, P)
        sc2 = view(10240, 2, 16, P)
        tv = view(14336, 2, 16, TOPK)
        ti = view(14848, 2, 16, TOPK).bitcast(u32)
        tif = view(15360, 2, 16, TOPK)
        cand = view(15872, 2, HH, TOPK * TOPK)
        cand2 = view(19968, 2, HH, TOPK * TOPK)
        bv = view(24064, 2, HH, TOPK)
        bp = view(24320, 2, HH, TOPK).bitcast(u32)
        bq = view(24576, 2, 2, HH * TOPK).bitcast(u32)
        bqf = view(25088, 2, 2, HH * TOPK)
        picked = view(25600, 2, 3, P)
        gsum = view(26368, 2, HH)
        G = view(0, P, SEQ)
        uT = view(0, ST_, SEQ)
        sv = view(6144, ST_, SEQ)
        ssq = view(12288, ST_, SEQ)
        svtok = view(12288, 2, SH)
        smean = view(18432, SEQ)
        srstd = view(18688, SEQ)
        sws = view(20000, SG, P)
        sbs = view(21024, SG, P)
        tabs = view(24576, C2W)
        T2 = 24576 + C2W
        dwf = view(T2, KT, 16)
        awf = view(T2 + 128, KT, 16)
        row_rstd = arena[0:32, T2 + 256:T2 + 256 + TOK]
        dsm = view(T2 + 528, 3, 6, 16)
        assert T2 + 528 + 288 <= 32768
        fo = view(20224, KT, TOK)

        def tab(name, rows=P):
            a, w = C2O[name]
            return tabs[0:rows, a:a + w]

        aqk = view(0, 16, TOK)
        aqkv = view(0, 24, TOK)
        avT = view(4352, 8, TOK)
        aog = view(6528, 8, TOK)
        asq = view(8704, 16, TOK)
        avtok = view(13056, 3, D)
        alf = view(16528, 3, 32)
        awork = view(16640, 4, 3, 16)
        acum = arena[0:32, 16832:16832 + TOK]
        aL = view(17104, 2, TOK)
        aR = view(17648, 2, TOK)
        asm = view(18192, 2, 6)
        ap_ = view(18208, 2, 3, TOK)
        qgain = view(19840, 1)
        apT = view(8704, 2, 3, 3, P)
        ay = view(4352, 8, TOK)
        dqkv = view(0, 24, TOK)
        dog = view(6528, 8, TOK)
        dsq = view(8704, 16, TOK)
        dwork = view(8704, 2, TOK)
        (dER, ddec, dLT, dQK, dkb, dkd, dvb, dX, dXT, dMT, dT1, dqd, dW, dU, dST) = (
            view(8704 + 1024 * k, 8, P) for k in range(15))
        dOT = dqkv[:, 16:24, :]
        fact = view(0, 24, TOK)
        fconv = view(6528, 2, 4, TOK)
        cact = mixin[:, 0, 0:8]
        one, two = slice(T0, TOK), slice(0, TOK)

        def heads8(bank, rows, cols):
            return ps[0:rows, bank:bank + 2, :].rearrange("p b (g c) -> p (b g) c", c=P)[:, :, 0:cols]

        def trin(n):
            return tab("tri")[0:n, TOK + META:TOK + META + n]

        block = ctx.enter_context(nc.Block())

        parts = [("ada", 96), ("ret_in", 48), ("ret_out", 16), ("query0", 16), ("peer0", 256), ("sgu_in", 48),
                 ("sgu_out", 24), ("query1", 16), ("peer1", 256), ("att_in", 32), ("att_out", 8), ("up0", 44),
                 ("down0", 24), ("dn_in", 32), ("dn_out", 8), ("up1", 44), ("down1", 24)]
        first, n = {}, 0
        for name, units in parts:
            first[name] = n
            n += units
        n_units = n
        stages = ["ada", "ret", "peer0", "sgu", "peer1", "final1", "att", "ffn0", "dn", "ffn1"]
        on = {s: until is None or stages.index(s) <= stages.index(until) for s in stages}
        last_part = {None: "down1", "ada": "ada", "ret": "ret_out", "peer0": "peer0", "sgu": "sgu_out", "peer1": "peer1",
                     "final1": "peer1", "att": "att_out", "ffn0": "down0", "dn": "dn_out", "ffn1": "down1"}[until]

        limit = first[last_part] + dict(parts)[last_part]
        blocks_before, nb = {}, 0
        for name, units in parts:
            blocks_before[name] = nb
            if name in ("ret_in", "query0", "query1", "sgu_in", "att_in", "up0", "up1", "dn_in"):
                nb += units

        def meet(c, sem):
            c.engine.drain().then_inc(sem, 1)
            c.engine.wait_ge(sem, c.next(sem, 4))

        @block.sync
        def _(sp):
            sp.dma_start(params[:], t["params"]).then_inc(s_consts_in, 16)
            sp.dma_start(const1[:], t["const1"]).then_inc(s_consts_in, 16)
            sp.dma_start(x[:, :, T0:TOK], t["xT"]).then_inc(s_consts_in, 16)
            sp.dma_start(posn, t["positions"]).then_inc(s_consts_in, 16)

            def load(src, at):
                if not (at.b is None and at.unit < RAW):
                    sp.wait_ge(s_raw_free, at.number(1 - RAW) * 2)
                sp.dma_start(raw[:, at.raw, :, :], src).then_inc(full[at.raw], 16)

            def stream(src, base, count):
                done = 0
                if base == 0:
                    for k in range(ROUND):
                        load(src[k], At(k))
                    done = ROUND
                rounds = (count - done) // ROUND
                with sp.Fori(0, rounds) as b:
                    for k in range(ROUND):
                        load(src[b * ROUND + (done + k)], At(base + done + k, b))
                for k in range(done + rounds * ROUND, count):
                    load(src[k], At(base + k))

            def stream_peer(u, v, base):
                load(u[0], At(base))
                rounds = (P - 1) // 4
                with sp.Fori(0, rounds) as b:
                    for k in range(4):
                        load(u[b * 4 + (k + 1)], At(base + 2 * k + 1, b))
                        load(v[b * 4 + k], At(base + 2 * k + 2, b))
                for i in range(rounds * 4, P - 1):
                    load(u[i + 1], At(base + 2 * i + 1))
                    load(v[i], At(base + 2 * i + 2))
                load(v[P - 1], At(base + 2 * P - 1))

            for name, units in parts:
                if name.startswith("peer"):
                    l = int(name[-1])
                    stream_peer(t["u"][l], t["v"][l], first[name])
                else:
                    stream(t[name], first[name], units)
                if name == last_part:
                    break
            sp.wait_ge(s_result_ready, 1)
            if until is None:
                sp.dma_start(out, x[:, :, T0:TOK]).then_inc(s_out_done, 16)
            else:
                sp.dma_start(out, x[:, :, :]).then_inc(s_out_done, 16)
            sp.wait_ge(s_out_done, 16)

        @block.gpsimd
        def _(pool):
            c = Counts(pool)
            pool.memset(ones[:], 1.0).then_inc(s_memsets, 1)
            pool.memset(zeros_b[:], 0.0).then_inc(s_memsets, 1)
            pool.memset(small[:, 0:1], EPS).then_inc(s_memsets, 1)
            pool.memset(small[:, 1:2], float(np.pi / 2)).then_inc(s_memsets, 1)
            pool.memset(small[:, 2:4], 1.0).then_inc(s_memsets, 1)
            pool.memset(x[:, :, 0:T0], 0.0).then_inc(s_memsets, 1)
            pool.engine_nop().then_inc(s_bank_free, 4)
            pool.engine_nop().then_inc(s_dn_silu, 2)
            pool.wait_ge(s_ada_row, c.next(s_ada_row, 24))
            pool.dma_start(t["scratch"], ada_row).then_inc(s_row_out, 16)
            pool.wait_ge(s_row_out, 16)
            pool.dma_start(ada_sq, t["scratch"].rearrange("a (b c) -> (a b) c", c=P)).then_inc(s_row_in, 16)
            meet(c, s_met)
            if on["ret"]:
                pool.dma_start(ret_dec, t["ret_dec"]).then_inc(s_ret_in, 16)
                meet(c, s_met)
                meet(c, s_met)
            for layer in range(2):
                if on["peer%d" % layer]:
                    meet(c, s_met)
                    pool.dma_start(keysT, t["keysT"][layer]).then_inc(s_keys_in, 16)
                    meet(c, s_met)
                    meet(c, s_met)
                    meet(c, s_met)
                if layer == 0 and on["sgu"]:
                    pool.dma_start(sws, t["w_s"]).then_inc(s_sgu_in, 16)
                    pool.wait_ge(s_sgu_in, 16)
                    pool.memset(sws[64:128, :, 0:64], 0.0).then_inc(s_memsets, 1)
                    pool.dma_start(sbs[0:1, :, :], t["b_s"]).then_inc(s_sgu_in, 16)
                    meet(c, s_met)
                    meet(c, s_met)
            if on["att"]:
                pool.dma_start(x[:, :, 0:T0], t["metaT"]).then_inc(s_tabs_in, 16)
                pool.dma_start(tabs, t["const2"]).then_inc(s_tabs_in, 16)
                pool.dma_start(awf, t["att_wf"]).then_inc(s_tabs_in, 16)
                for _ in range(3):
                    meet(c, s_met)
            if on["ffn0"]:
                pool.memset(fact[:, 22:24, :], 0.0).then_inc(s_memsets, 1)
                meet(c, s_met)
                meet(c, s_met)
            if on["dn"]:
                pool.dma_start(dwf, t["dn_wf"]).then_inc(s_tabs_in, 16)
                for _ in range(3):
                    meet(c, s_met)
            if on["ffn1"]:
                pool.memset(fact[:, 22:24, :], 0.0).then_inc(s_memsets, 1)
                meet(c, s_met)
                meet(c, s_met)

        @block.tensor
        def _(pe):
            c = Counts(pe)
            mm, tr = nc.tensor.matmul, nc.tensor.transpose

            def unit(at, dst, moving, opened=False):
                for half in range(2):
                    pe.wait_ge(s_raw_free, at.halves(2 * ADA_UNITS + half + 1))
                    for q in range(4):
                        k, slot = 4 * half + q, at.slot(half)
                        hi, lo = moving(k)
                        begin, end = opened is False and k == 0, opened or k == KT - 1
                        mm(dst(k), w_lo[:, slot, q, :], hi, start=begin, stop=opened, skip_group_check=opened)
                        mm(dst(k), w_hi[:, slot, q, :], lo, start=False, stop=opened, skip_group_check=opened)
                        last = mm(dst(k), w_hi[:, slot, q, :], hi, start=False, stop=end, skip_group_check=opened)
                    last.then_inc(s_half_used, 1)

            def project(name, cols):
                base, count = first[name], dict(parts)[name]
                rounds = count // ROUND
                width = cols.stop - cols.start

                def one_unit(j, b=None):
                    pe.wait_ge(s_bank_free, c.next(s_bank_free))
                    unit(At(base + j, b), lambda k: ps[:, j % 4, 0:width], lambda k: (h_hi[:, k, 0:width], h_lo[:, k, 0:width]))

                with c.loop(rounds, bank_free=ROUND) as b:
                    for j in range(ROUND):
                        one_unit(j, b)
                for j in range(rounds * ROUND, count):
                    one_unit(j)

            def zero_banks(banks):
                for bank in banks:
                    for side in range(2):
                        mm(ps[:, bank, side * SEQ:side * SEQ + SEQ], zeros_b[:, :], ones[:].bitcast(bf16), start=True,
                           stop=True)

            def project_out(name, width, signal):
                base, count = first[name], dict(parts)[name]
                zero_banks(range(8))

                def round_of(r, b=None):
                    pe.wait_ge(s_h_ready, c.next(s_h_ready))
                    for m in range(8):
                        unit(At(base + r * ROUND + m, b), lambda k: ps[:, m, 0:width],
                             lambda k: (h_hi[:, k, 0:width], h_lo[:, k, 0:width]), opened=True)

                rounds = count // ROUND
                if rounds > 1:
                    with c.loop(rounds - 1, h_ready=1) as b:
                        round_of(0, b)
                round_of(rounds - 1)
                pe.drain().then_inc(signal, 1)

            def moved():
                pe.wait_ge(s_bank_free, c.n[s_bank_free.name] + 4)

            def sum_tiles(src, tiles, cols, signal=s_sums, bank=4):
                for k in range(tiles):
                    last = mm(ps[:, bank, 0:cols.stop - cols.start], ones[:], src[:, k, 0:cols.stop - cols.start], start=k == 0,
                              stop=k == tiles - 1)
                last.then_inc(signal, 1)

            def norm(cols):
                pe.wait_ge(s_squares, c.next(s_squares))
                sum_tiles(sq, KT, cols)
                pe.wait_ge(s_h_ready, c.next(s_h_ready))

            pe.wait_ge(s_memsets, c.next(s_memsets, 6))
            pe.wait_ge(s_c_act, c.next(s_c_act))
            def ada_unit(j, b=None):
                at = At(j, b)
                pe.wait_ge(full[at.raw], at.fill() * 16)
                for k in range(KT):
                    last = mm(ps[0:1, (j // 4) % 2, (j % 4) * P:(j % 4) * P + P], cact[:, k:k + 1], raw[:, at.raw, k, :],
                              start=k == 0, stop=k == KT - 1)
                last.then_inc(s_raw_free, 2)
            for j in range(8):
                ada_unit(j)
            with c.loop(11, ada_row=2) as b:
                for j in range(8):
                    if j % 4 == 0:
                        pe.wait_ge(s_ada_row, c.next(s_ada_row))
                    ada_unit(8 + j, b)
            pe.wait_ge(s_ada_row, c.next(s_ada_row, 2))
            pe.wait_ge(s_row_in, 16)
            pe.wait_ge(s_consts_in, c.next(s_consts_in, 64))
            tr(ps[:, 2, 0:96], ada_sq, ident[0:96, 0:96]).then_inc(s_ada_t, 1)
            meet(c, s_met)

            if on["ret"]:
                norm(one)
                project("ret_in", one)
                meet(c, s_met)
                for n in range(8):
                    for q in range(4):
                        m, jt = 2 * n + q // 2, q % 2
                        last = tr(ps[:, n, q * P:q * P + P], vT[:, m, jt * P:jt * P + P], ident)
                    last.then_inc(s_vt_ready, 1)
                for hd in range(RH):
                    pe.wait_ge(s_vt_copied, c.next(s_vt_copied, 2))
                for hd in range(RH):
                    for jt in range(2):
                        for k in range(2):
                            last = mm(ps[:, hd, jt * SEQ:jt * SEQ + SEQ], qk[:, 8 + 2 * hd + k, jt * P:jt * P + P],
                                      qk[:, 2 * hd + k, :], start=k == 0, stop=k == 1)
                    last.then_inc(s_scores_ready, 1)
                for hd in range(RH):
                    pe.wait_ge(s_decayed, c.next(s_decayed))
                for m in range(16):
                    hd = m // 4
                    if m >= 4:
                        pe.wait_ge(s_y_copied, c.next(s_y_copied))
                    for jt in range(2):
                        last = mm(ps[:, 4 + m % 4, 0:SEQ], vtok[:, jt, m * P:m * P + P], sT[:, hd, jt, :], start=jt == 0,
                                  stop=jt == 1)
                    last.then_inc(s_y_ready, 1)
                pe.wait_ge(s_y_copied, c.next(s_y_copied, 4))
                pe.wait_ge(s_squares, c.next(s_squares))
                for hd in range(RH):
                    for k in range(4):
                        last = mm(ps[:, hd // 2, (hd % 2) * SEQ:(hd % 2) * SEQ + SEQ], ones[:], ysq[:, 4 * hd + k, :],
                                  start=k == 0, stop=k == 3)
                last.then_inc(s_sums, 1)
                meet(c, s_met)
                project_out("ret_out", SEQ, s_acc_done)
                pe.wait_ge(s_x_ready, c.next(s_x_ready))

            def peer(layer):
                norm(one)
                meet(c, s_met)
                project(f"query{layer}", one)
                pe.wait_ge(s_keys_in, c.next(s_keys_in, 16))
                moved()
                for tt in range(2):
                    for m in range(16):
                        last = mm(ps[:, 4 * tt + m // 4, (m % 4) * P:(m % 4) * P + P], qT[:, m, tt * P:tt * P + P],
                                  keysT[:, m, :], start=True, stop=True)
                        if m % 4 == 3:
                            last.then_inc(s_key_scores, 1)
                pe.wait_ge(s_picks_ready, c.next(s_picks_ready))
                for n in range(3):
                    for tt in range(2):
                        last = tr(ps[:, n, tt * P:tt * P + P], picked[:, tt, n, :], ident)
                last.then_inc(s_tables_ready, 1)
                meet(c, s_met)
                def group(buf, first_time):
                    pe.wait_ge(s_picks_ready, c.next(s_picks_ready))
                    if not first_time:
                        pe.wait_ge(s_g_copied, c.next(s_g_copied))
                    for q in range(4):
                        last = mm(ps[:, buf, q * P:q * P + P], pick_j[:, buf, q, :], pick_i[:, buf, q, :], start=True,
                                  stop=True)
                    last.then_inc(s_g_banks, 1)
                group(0, True)
                group(1, True)
                with c.loop(SEQ // 8 - 1, picks_ready=2, g_copied=2) as b:
                    group(0, False)
                    group(1, False)
                pe.wait_ge(s_g_copied, c.next(s_g_copied, 2))
                meet(c, s_met)
                base = first[f"peer{layer}"]
                zero_banks(range(4, 8))

                def up(i, at, j):
                    if not (isinstance(i, int) and i < 4):
                        pe.wait_ge(s_gelu_done, i + (P * layer - 3))
                    unit(at, lambda k: ps[:, j % 4, 0:SEQ], lambda k: (h_hi[:, k, 0:SEQ], h_lo[:, k, 0:SEQ]))

                def down(i, at, j):
                    pe.wait_ge(s_mix_done, i + (P * layer + 1))
                    unit(at, lambda m: ps[:, 4 + m // 2, (m % 2) * SEQ:(m % 2) * SEQ + SEQ],
                         lambda m: (mixed_hi[:, j % 2, :], mixed_lo[:, j % 2, :]), opened=True)

                up(0, At(base), 0)
                for k in range(4):
                    up(k + 1, At(base + 2 * k + 1), k + 1)
                    down(k, At(base + 2 * k + 2), k)
                rounds = (P - 1) // 4 - 1
                with c.loop(rounds) as b:
                    for k in range(4):
                        up(b * 4 + (k + 5), At(base + 8 + 2 * k + 1, b), k + 5)
                        down(b * 4 + (k + 4), At(base + 8 + 2 * k + 2, b), k + 4)
                for i in range(4 + 4 * rounds, P - 1):
                    up(i + 1, At(base + 2 * i + 1), i + 1)
                    down(i, At(base + 2 * i + 2), i)
                down(P - 1, At(base + 2 * P - 1), P - 1)
                pe.drain().then_inc(s_acc_done, 1)
                pe.wait_ge(s_x_ready, c.next(s_x_ready))
                meet(c, s_met)

            if on["peer0"]:
                peer(0)

            if on["sgu"]:
                pe.wait_ge(s_memsets, c.next(s_memsets))
                norm(one)
                project("sgu_in", one)
                moved()
                sum_tiles(sv, ST_, slice(0, SEQ), s_mean_sum)
                pe.wait_ge(s_squares, c.next(s_squares))
                sum_tiles(ssq, ST_, slice(0, SEQ))
                pe.wait_ge(s_sgu_ready, c.next(s_sgu_ready))
                for n in range(12):
                    if n >= 4:
                        pe.wait_ge(s_vt_copied, c.next(s_vt_copied))
                    for q in range(4):
                        m, jt = 2 * n + q // 2, q % 2
                        last = tr(ps[:, n % 4, q * P:q * P + P], sv[:, m, jt * P:jt * P + P], ident)
                    last.then_inc(s_vt_ready, 1)
                pe.wait_ge(s_vt_copied, c.next(s_vt_copied, 4))
                pe.wait_ge(s_sgu_in, c.next(s_sgu_in, 32))
                for n in range(12):
                    if n >= 4:
                        pe.wait_ge(s_sgu_s, c.next(s_sgu_s))
                    for q in range(4):
                        m, jt = 2 * n + q // 2, q % 2
                        dst = ps[:, 4 + n % 4, q * P:q * P + P]
                        mm(dst, svtok[:, jt, m * P:m * P + P], sws[:, m // 3, :], start=True, stop=False)
                        last = mm(dst, ones[0:1, :], sbs[0:1, m // 3, :], start=False, stop=True)
                    last.then_inc(s_spatial_ready, 1)
                pe.wait_ge(s_sgu_s, c.next(s_sgu_s, 4))
                meet(c, s_met)
                project_out("sgu_out", SEQ, s_acc_done)
                pe.wait_ge(s_x_ready, c.next(s_x_ready))
                meet(c, s_met)

            if on["peer1"]:
                peer(1)
            if on["final1"]:
                pe.wait_ge(s_squares, c.next(s_squares))
                sum_tiles(sq, KT, one)
                pe.wait_ge(s_x_ready, c.next(s_x_ready))

            def norm_post():
                pe.wait_ge(s_fo_copied, c.next(s_fo_copied))
                sum_tiles(sq, KT, two)
                pe.wait_ge(s_x_ready, c.next(s_x_ready))

            if on["att"]:
                pe.wait_ge(s_tabs_in, c.next(s_tabs_in, 48))
                norm(two)
                project("att_in", two)
                for tt, (s, n) in enumerate(TILES):
                    for k in range(KT):
                        last = mm(ps[0:n, 5, tt * 16:tt * 16 + 16], h[:, k, s:s + n], awf[:, k, :], start=k == 0,
                                  stop=k == KT - 1)
                last.then_inc(s_scores_ready, 1)
                moved()
                pe.wait_ge(s_squares, c.next(s_squares))
                for b in range(16):
                    last = mm(ps[0:32, 6, 0:TOK], tab("colsel")[:, 32 - 2 * b:64 - 2 * b], asq[:, b, :], start=b == 0,
                              stop=b == 15)
                last.then_inc(s_sums, 1)
                pe.wait_ge(s_inv, c.next(s_inv))
                for b in range(16):
                    if b >= 4:
                        pe.wait_ge(s_scaled, c.next(s_scaled))
                    mm(ps[:, b % 4, 0:TOK], tab("rowsel", 32)[:, b * P:b * P + P], row_rstd, start=True,
                       stop=True).then_inc(s_norms, 1)
                pe.wait_ge(s_scaled, c.next(s_scaled, 4))
                for n in range(8):
                    if n >= 4:
                        pe.wait_ge(s_vt_copied, c.next(s_vt_copied))
                    for tt, (s, w) in enumerate(TILES):
                        last = tr(ps[0:w, n % 4, tt * P:tt * P + P], avT[:, n, s:s + w], ident)
                    last.then_inc(s_vt_ready, 1)
                pe.wait_ge(s_vt_copied, c.next(s_vt_copied, 4))
                pe.wait_ge(s_heads_prep, c.next(s_heads_prep))
                for tt, (s, n) in enumerate(TILES):
                    last = mm(ps[0:32, 5, 0:TOK], alf[0:n, tt, :], tab("tri")[0:n, tt * TOK:tt * TOK + TOK], start=tt == 0,
                              stop=tt == 2)
                last.then_inc(s_cum_ready, 1)
                meet(c, s_met)
                for pr in range(AH // 2):
                    for par_ in range(2):
                        lo = 64 * par_
                        pe.wait_ge(s_heads_prep, c.next(s_heads_prep))
                        for tt, (s, n) in enumerate(TILES):
                            kend = s + n
                            dst = ps[0:n, 3 * par_ + tt, 0:kend]
                            mm(dst, aqk[lo:lo + 64, pr, s:s + n], aqk[lo:lo + 64, 8 + pr, 0:kend], start=True, stop=False)
                            mm(dst, aL[0:32, par_, s:s + n], aR[0:32, par_, 0:kend], start=False,
                               stop=True).then_inc(s_att_s, 1)
                    for par_ in range(2):
                        for tt, (s, n) in enumerate(TILES):
                            pe.wait_ge(s_att_pn, c.next(s_att_pn))
                            for kt in range(tt + 1):
                                ks, kn = TILES[kt]
                                last = tr(ps[0:kn, 3 * par_ + tt, kt * P:kt * P + n], ap_[0:n, par_, tt, ks:ks + kn],
                                          ident[0:n, 0:n])
                            last.then_inc(s_att_t, 1)
                    for par_ in range(2):
                        lo = 64 * par_
                        for tt, (s, n) in enumerate(TILES):
                            pe.wait_ge(s_att_tc, c.next(s_att_tc))
                            for kt in range(tt + 1):
                                ks, kn = TILES[kt]
                                hd = 2 * pr + par_
                                last = mm(ps[lo:lo + 64, 6, s:s + n], avtok[0:kn, kt, hd * 64:hd * 64 + 64],
                                          apT[0:kn, par_, tt, kt, 0:n], start=kt == 0, stop=kt == tt)
                    last.then_inc(s_att_o, 1)
                    pe.wait_ge(s_att_od, c.next(s_att_od))
                meet(c, s_met)
                project_out("att_out", TOK, s_out_ready)
                norm_post()
                meet(c, s_met)

            def ffn(n):
                norm(two)
                project(f"up{n}", two)
                pe.wait_ge(s_memsets, c.next(s_memsets))
                meet(c, s_met)
                project_out(f"down{n}", TOK, s_out_ready)
                norm_post()
                meet(c, s_met)

            if on["ffn0"]:
                ffn(0)

            if on["dn"]:
                pe.wait_ge(s_tabs_in, c.next(s_tabs_in, 16))
                norm(two)
                project("dn_in", two)
                for tt, (s, n) in enumerate(TILES):
                    for k in range(KT):
                        last = mm(ps[0:n, 5, tt * 16:tt * 16 + 16], h[:, k, s:s + n], dwf[:, k, :], start=k == 0,
                                  stop=k == KT - 1)
                last.then_inc(s_scores_ready, 1)
                moved()
                pe.wait_ge(s_squares, c.next(s_squares))
                for b in range(16):
                    last = mm(ps[0:16, 6, 0:TOK], tab("colsel1")[:, 16 - b:32 - b], dsq[:, b, :], start=b == 0, stop=b == 15)
                last.then_inc(s_sums, 1)
                pe.wait_ge(s_inv, c.next(s_inv))
                for b in range(16):
                    if b >= 4:
                        pe.wait_ge(s_scaled, c.next(s_scaled))
                    mm(ps[:, b % 4, 0:TOK], tab("rowsel1", 16)[:, b * P:b * P + P], row_rstd[0:16, :], start=True,
                       stop=True).then_inc(s_norms, 1)
                pe.wait_ge(s_scaled, c.next(s_scaled, 4))
                meet(c, s_met)
                for ch, (s, n) in enumerate(TILES):
                    tri_n = trin(n)
                    mm(ps[0:n, 2, 0:8], tri_n, dsm[0:n, ch, 2, 0:8], start=True, stop=True)
                    for hd in range(8):
                        last = mm(ps[:, hd // 4, (hd % 4) * P:(hd % 4) * P + n], dsm[0:n, ch, 2, hd:hd + 1].to_broadcast([n, P]),
                                  tri_n, start=True, stop=True)
                    for hd in range(8):
                        mm(ps[0:n, 4 + hd // 4, (hd % 4) * P:(hd % 4) * P + n], dqkv[:, 8 + hd, s:s + n],
                           dqkv[:, 8 + hd, s:s + n], start=True, stop=True)
                        last = mm(ps[0:n, 6 + hd // 4, (hd % 4) * P:(hd % 4) * P + n], dqkv[:, 8 + hd, s:s + n],
                                  dqkv[:, hd, s:s + n], start=True, stop=True)
                    last.then_inc(s_dn_p, 1)
                    pe.wait_ge(s_dn_v, c.next(s_dn_v))
                    for hd in range(8):
                        tr(ps[0:n, 0 + hd // 4, (hd % 4) * P:(hd % 4) * P + P], dqkv[:, 8 + hd, s:s + n], ident)
                        last = tr(ps[0:n, 2 + hd // 4, (hd % 4) * P:(hd % 4) * P + P], dqkv[:, 16 + hd, s:s + n], ident)
                    last.then_inc(s_dn_p, 1)
                    pe.wait_ge(s_dn_v, c.next(s_dn_v))
                    levels = n.bit_length() - 1
                    for lv in range(levels):
                        pe.wait_ge(s_dn_v, c.next(s_dn_v))
                        for hd in range(8):
                            last = mm(ps[0:n, hd // 4, (hd % 4) * P:(hd % 4) * P + n], dMT[0:n, hd, 0:n], dX[0:n, hd, 0:n],
                                      start=True, stop=True)
                        last.then_inc(s_dn_p, 1)
                        pe.wait_ge(s_dn_v, c.next(s_dn_v))
                        for hd in range(8):
                            mm(ps[0:n, 2 + hd // 4, (hd % 4) * P:(hd % 4) * P + n], dXT[0:n, hd, 0:n], dT1[0:n, hd, 0:n],
                               start=True, stop=True)
                            last = mm(ps[0:n, 4 + hd // 4, (hd % 4) * P:(hd % 4) * P + n], dT1[0:n, hd, 0:n],
                                      dXT[0:n, hd, 0:n], start=True, stop=True)
                        last.then_inc(s_dn_p, 1)
                    pe.wait_ge(s_dn_v, c.next(s_dn_v))
                    for hd in range(8):
                        last = mm(ps[:, hd // 4, (hd % 4) * P:(hd % 4) * P + n], dkb[0:n, hd, :], dXT[0:n, hd, 0:n],
                                  start=True, stop=True)
                    last.then_inc(s_dn_p, 1)
                    pe.wait_ge(s_dn_v, c.next(s_dn_v))
                    for hd in range(8):
                        dst = ps[0:n, 2 + hd // 4, (hd % 4) * P:(hd % 4) * P + P]
                        mm(dst, dXT[0:n, hd, 0:n], dvb[0:n, hd, :], start=True, stop=False)
                        last = mm(dst, dW[:, hd, 0:n], dST[:, hd, :], start=False, stop=True)
                    last.then_inc(s_dn_p, 1)
                    pe.wait_ge(s_dn_v, c.next(s_dn_v))
                    for hd in range(8):
                        dst = ps[:, 4 + hd // 4, (hd % 4) * P:(hd % 4) * P + n]
                        mm(dst, dST[:, hd, :], dqd[:, hd, 0:n], start=True, stop=False)
                        mm(dst, dU[0:n, hd, :], dQK[0:n, hd, 0:n], start=False, stop=True)
                        last = mm(ps[:, 6 + hd // 4, (hd % 4) * P:(hd % 4) * P + P], dkd[0:n, hd, :], dU[0:n, hd, :], start=True,
                                  stop=True)
                    last.then_inc(s_dn_p, 1)
                    pe.wait_ge(s_dn_v, c.next(s_dn_v))
                pe.wait_ge(s_squares, c.next(s_squares))
                for b in range(8):
                    last = mm(ps[0:16, 6, 0:TOK], tab("colsel1")[:, 16 - b:32 - b], dsq[:, b, :], start=b == 0, stop=b == 7)
                last.then_inc(s_sums, 1)
                pe.wait_ge(s_inv, c.next(s_inv))
                for b in range(8):
                    if b >= 4:
                        pe.wait_ge(s_scaled, c.next(s_scaled))
                    mm(ps[:, b % 4, 0:TOK], tab("rowsel1", 16)[:, b * P:b * P + P], row_rstd[0:16, :], start=True,
                       stop=True).then_inc(s_norms, 1)
                pe.wait_ge(s_scaled, c.next(s_scaled, 4))
                meet(c, s_met)
                project_out("dn_out", TOK, s_out_ready)
                norm_post()
                meet(c, s_met)
            if on["ffn1"]:
                ffn(1)

        @block.scalar
        def _(act):
            c = Counts(act, s_act_own)
            A = nc.scalar.activation

            def split(at):
                if at.b is None and at.unit >= limit:
                    return
                act.wait_ge(full[at.raw], at.fill() * 16)
                for half in range(2):
                    if not (at.b is None and at.unit < ADA_UNITS + 2):
                        act.wait_ge(s_half_used, at.halves(half - 3))
                    A(w_hi[:, at.slot(half)], raw[:, at.raw, 4 * half:4 * half + 4, :], ACT.Copy).then_inc(s_hi_ready, 1)

            def take(name, skip, rounds, dst, func, bias=None):
                with c.loop(rounds) as b:
                    for j in range(ROUND):
                        at = At(first[name] + skip + j, b)
                        split(at.plus(2))
                        act.wait_ge(s_half_used, at.halves(2))
                        width = dst(0).shape[-1]
                        extra = {} if bias is None else {"bias": bias(b * ROUND + j)}
                        A(dst(b * ROUND + j), ps[:, j % 4, 0:width], func, **extra).then_inc(s_bank_free, 1)

            def feed(name, src, width):
                base, rounds = first[name], dict(parts)[name] // ROUND

                def round_of(r, b=None):
                    if not (b is None and r == 0):
                        act.wait_ge(s_half_used, At(base + r * ROUND, b).halves(0))
                    for k in range(KT):
                        A(h_hi[:, k, 0:width], src[:, (r * KT + k) if b is None else b * KT + (r * KT + k), 0:width],
                          ACT.Copy).then_inc(s_act_hi, 1)
                    for m in range(ROUND):
                        split(At(base + r * ROUND + m + 2, b))

                round_of(0)
                if rounds > 2:
                    with c.loop(rounds - 2) as b:
                        round_of(1, b)
                if rounds > 1:
                    round_of(rounds - 1)

            def norm_sums(scale=1.0 / D, src=None, dst=None):
                act.wait_ge(s_sums, c.next(s_sums))
                src = ps[:, 4, 0:SEQ] if src is None else src
                dst = rstd[:, 0:SEQ] if dst is None else dst
                A(dst, src, ACT.Sqrt, bias=eps[0:dst.shape[0], :], scale=scale).then_inc(s_root, 1)

            def norm_one(layer, which):
                A(sq[:, :, 0:SEQ], x[:, :, one], ACT.Square).then_inc(s_squares, 1)
                norm_sums()
                for k in range(KT):
                    act.wait_ge(s_h_scaled, c.next(s_h_scaled))
                    at = layer * 48 + (0 if which == 0 else 24) + k
                    A(h_hi[:, k, 0:SEQ], h[:, k, 0:SEQ], ACT.Identity, bias=mods[:, at:at + 1])
                    A(h[:, k, 0:SEQ], h[:, k, 0:SEQ], ACT.Identity, bias=mods[:, at:at + 1]).then_inc(s_act_hi, 1)

            def norm_two():
                A(sq[:, :, :], x[:, :, :], ACT.Square).then_inc(s_squares, 1)
                norm_sums(src=ps[:, 4, 0:TOK], dst=rstd[:, :])
                for k in range(KT):
                    act.wait_ge(s_h_whole, c.next(s_h_whole))
                    A(h_hi[:, k, :], h[:, k, :], ACT.Copy).then_inc(s_act_hi, 1)

            def norm_post():
                act.wait_ge(s_out_ready, c.next(s_out_ready))
                A(fo, ps[:, :, 0:TOK], ACT.Copy)
                A(sq, ps[:, :, 0:TOK], ACT.Square).then_inc(s_fo_copied, 1)
                norm_sums(src=ps[:, 4, 0:TOK], dst=rstd[:, :])
                act.wait_ge(s_x_ready, c.next(s_x_ready))
                meet(c, s_met)

            act.wait_ge(s_consts_in, c.next(s_consts_in, 64))
            act.wait_ge(s_memsets, c.next(s_memsets, 6))
            A(cact, par("c", 0, 8), ACT.Silu).then_inc(s_c_act, 1)
            act.wait_ge(s_rope_args, c.next(s_rope_args))
            A(sinT, rope[:, 4, :], ACT.Sin)
            A(cosT, rope[:, 5, :], ACT.Sin, bias=half_pi, scale=-1.0).then_inc(s_rope_ready, 1)
            with c.loop(12, raw_free=16) as b:
                for j in range(2):
                    act.wait_ge(s_raw_free, c.next(s_raw_free, 8))
                    A(ada_row.rearrange("p (s n) -> p s n", n=BANK)[:, b * 2 + j, :], ps[0:1, j, :],
                      ACT.Copy).then_inc(s_ada_row, 1)
            split(At(ADA_UNITS))
            split(At(ADA_UNITS + 1))
            meet(c, s_met)

            if on["ret"]:
                norm_one(0, 0)
                take("ret_in", 0, 2, lambda m: qk[:, m, :], ACT.Copy)
                take("ret_in", 16, 2, lambda m: vT[:, m, :], ACT.Copy)
                take("ret_in", 32, 2, lambda m: gT[:, m, :], ACT.Silu)
                meet(c, s_met)
                for n in range(8):
                    act.wait_ge(s_vt_ready, c.next(s_vt_ready))
                    A(vtok.rearrange("p j (m f) -> p m j f", f=P)[:, 2 * n:2 * n + 2],
                      ps[:, n, :].rearrange("p (m j f) -> p m j f", m=2, j=2), ACT.Copy).then_inc(s_vt_copied, 1)
                for m in range(16):
                    act.wait_ge(s_y_ready, c.next(s_y_ready))
                    A(yT[:, m, :], ps[:, 4 + m % 4, 0:SEQ], ACT.Copy).then_inc(s_y_copied, 1)
                act.wait_ge(s_y_copied, c.next(s_y_copied, 16))
                A(ysq, yT, ACT.Square).then_inc(s_squares, 1)
                norm_sums(1.0 / RDV, ps[:, 0:2, :], yrs.rearrange("p (a b) t -> p a (b t)", a=2))
                meet(c, s_met)
                feed("ret_out", yT, SEQ)
                act.wait_ge(s_x_ready, c.next(s_x_ready))

            def peer(layer):
                norm_one(layer, 1)
                meet(c, s_met)
                take(f"query{layer}", 0, 2, lambda m: qT[:, m, :], ACT.Copy)
                for n in range(8):
                    act.wait_ge(s_key_scores, c.next(s_key_scores))
                    A(sc[:, n // 4, (n % 4) * 4:(n % 4) * 4 + 4, :], ps[:, n, :].rearrange("p (m f) -> p m f", f=P),
                      ACT.Copy).then_inc(s_key_copied, 1)
                act.wait_ge(s_gate_in, c.next(s_gate_in))
                A(picked[:, :, 2, :], picked[:, :, 2, :], ACT.Exp).then_inc(s_gate_exp, 1)
                act.wait_ge(s_tables_ready, c.next(s_tables_ready))
                A(chosen[:], ps[:, 0:3, 0:SEQ], ACT.Copy)
                meet(c, s_met)
                with c.loop(SEQ // 8, g_banks=2) as b:
                    for buf in range(2):
                        act.wait_ge(s_g_banks, c.next(s_g_banks))
                        A(G.rearrange("p i (g t) -> p g t i", t=4)[:, b * 2 + buf],
                          ps[:, buf, :].rearrange("p (t i) -> p t i", t=4), ACT.Copy).then_inc(s_g_copied, 1)
                meet(c, s_met)
                base = first[f"peer{layer}"]

                def gelu(i, at, j):
                    split(at.plus(2))
                    act.wait_ge(s_half_used, at.halves(2))
                    if not (isinstance(i, int) and i < 2):
                        act.wait_ge(s_mix_done, i + (P * layer - 1))
                    A(mixin[:, j % 2, :], ps[:, j % 4, 0:SEQ], ACT.Gelu_apprx_tanh).then_inc(s_gelu_done, 1)

                gelu(0, At(base), 0)
                for k in range(4):
                    gelu(k + 1, At(base + 2 * k + 1), k + 1)
                    split(At(base + 2 * k + 4))
                rounds = (P - 1) // 4 - 1
                with c.loop(rounds) as b:
                    for k in range(4):
                        gelu(b * 4 + (k + 5), At(base + 8 + 2 * k + 1, b), k + 5)
                        split(At(base + 8 + 2 * k + 4, b))
                for i in range(4 + 4 * rounds, P - 1):
                    gelu(i + 1, At(base + 2 * i + 1), i + 1)
                    split(At(base + 2 * i + 4))
                split(At(base + 2 * P + 1))
                act.wait_ge(s_x_ready, c.next(s_x_ready))
                meet(c, s_met)

            if on["peer0"]:
                peer(0)

            if on["sgu"]:
                norm_one(1, 0)
                take("sgu_in", 0, 6, lambda m: view(0, 48, SEQ)[:, m, :], ACT.Gelu_apprx_tanh, bias=lambda m: par("sgu_b_in", 0, 48)[:, m:m + 1]
                     if isinstance(m, int) else par("sgu_b_in", 0, 48).unsqueeze(2)[:, m, :])
                act.wait_ge(s_sgu_centred, c.next(s_sgu_centred))
                A(ssq, sv, ACT.Square).then_inc(s_squares, 1)
                norm_sums(1.0 / SH, ps[:, 4, 0:SEQ], srstd)
                for n in range(12):
                    act.wait_ge(s_vt_ready, c.next(s_vt_ready))
                    A(svtok.rearrange("p j (m f) -> p m j f", f=P)[:, 2 * n:2 * n + 2],
                      ps[:, n % 4, :].rearrange("p (m j f) -> p m j f", m=2, j=2), ACT.Copy).then_inc(s_vt_copied, 1)
                meet(c, s_met)
                feed("sgu_out", uT, SEQ)
                act.wait_ge(s_x_ready, c.next(s_x_ready))
                meet(c, s_met)

            if on["peer1"]:
                peer(1)
            if on["final1"]:
                A(sq[:, :, 0:SEQ], x[:, :, one], ACT.Square).then_inc(s_squares, 1)
                norm_sums()
                act.wait_ge(s_x_ready, c.next(s_x_ready))

            if on["att"]:
                act.wait_ge(s_tabs_in, c.next(s_tabs_in, 48))
                norm_two()
                take("att_in", 0, 3, lambda m: aqkv[:, m, :], ACT.Copy)
                take("att_in", 24, 1, lambda m: aog[:, m, :], ACT.Sigmoid)
                act.wait_ge(s_bank_free, 4 + blocks_before["att_in"] + 32)
                A(asq, aqk, ACT.Square).then_inc(s_squares, 1)
                norm_sums(1.0 / ADH, ps[0:32, 6, 0:TOK], row_rstd)
                for n in range(8):
                    act.wait_ge(s_vt_ready, c.next(s_vt_ready))
                    A(avtok[0:META, 0, n * P:n * P + P], ps[0:META, n % 4, 0:P], ACT.Copy)
                    A(avtok[:, 1:3, n * P:n * P + P], ps[:, n % 4, P:3 * P].rearrange("p (a f) -> p a f", a=2),
                      ACT.Copy).then_inc(s_vt_copied, 1)
                act.wait_ge(s_logit_in, c.next(s_logit_in))
                c.link(A(awork[:, 1], awork[:, 1], ACT.Exp))
                A(awork[:, 1], awork[:, 1], ACT.Ln, bias=1.0).then_inc(s_logit_exp, 1)
                meet(c, s_met)
                for pr in range(AH // 2):
                    for par_ in range(2):
                        for tt, (s, n) in enumerate(TILES):
                            k = 3 * par_ + tt
                            act.wait_ge(s_att_m, c.next(s_att_m))
                            A(ap_[0:n, par_, tt, 0:s + n], ps[0:n, k, 0:s + n], ACT.Exp, bias=asm[0:n, 0, k:k + 1],
                              accum_out=asm[0:n, 1, k:k + 1]).then_inc(s_att_p, 1)
                    for par_ in range(2):
                        for tt, (s, n) in enumerate(TILES):
                            k = 3 * par_ + tt
                            act.wait_ge(s_att_t, c.next(s_att_t))
                            last = A(apT[0:META, par_, tt, 0, 0:n], ps[0:META, k, 0:n], ACT.Copy)
                            if tt:
                                last = A(apT[:, par_, tt, 1:tt + 1, 0:n],
                                         ps[:, k, P:P * (tt + 1)].rearrange("p (a f) -> p a f", f=P), ACT.Copy)
                            last.then_inc(s_att_tc, 1)
                meet(c, s_met)
                feed("att_out", ay, TOK)
                norm_post()

            def ffn(n):
                norm_two()
                c.n[s_bank_free.name] = 4 + blocks_before[f"up{n}"]
                w3 = par("ffn_conv", n * 132, 132).rearrange("p (b w) -> p b w", w=3)
                with c.loop(11, bank_free=4) as b:
                    for j in range(4):
                        at = At(first[f"up{n}"] + j, b, 4)
                        split(at.plus(2))
                        act.wait_ge(s_half_used, at.halves(2))
                        A(fconv[:, 0, j, :], ps[:, j, 0:TOK], ACT.Copy, scale=w3[:, b * 4 + j, 2:3]).then_inc(s_tap_done, 1)
                        if j % 2:
                            act.wait_ge(s_bank_free, c.next(s_bank_free))
                            A(fconv[:, 1, j - 1, :], fconv[:, 0, j - 1, :], ACT.Gelu_apprx_tanh).then_inc(s_ffn_gelu, 1)
                            act.wait_ge(s_bank_free, c.next(s_bank_free))
                meet(c, s_met)
                feed(f"down{n}", fact, TOK)
                norm_post()

            if on["ffn0"]:
                ffn(0)

            if on["dn"]:
                norm_two()
                c.n[s_bank_free.name] = 4 + blocks_before["dn_in"]
                with c.loop(3, bank_free=8) as b:
                    for j in range(8):
                        split(At(first["dn_in"] + j + 2, b))
                        act.wait_ge(s_bank_free, c.next(s_bank_free))
                        A(dqkv[:, b * 8 + j, :], dwork[:, j % 2, :], ACT.Silu).then_inc(s_dn_silu, 1)
                take("dn_in", 24, 1, lambda m: dog[:, m, :], ACT.Silu)
                act.wait_ge(s_dn_silu, 2 + 24)
                A(dsq, dqkv[:, 0:16, :], ACT.Square).then_inc(s_squares, 1)
                norm_sums(1.0, ps[0:16, 6, 0:TOK], row_rstd[0:16, :])
                act.wait_ge(s_logit_in, c.next(s_logit_in))
                A(dsm[:, :, 0, 0:8], dsm[:, :, 0, 0:8], ACT.Sigmoid)
                c.link(A(dsm[:, :, 5, 0:8], dsm[:, :, 5, 0:8], ACT.Exp))
                A(dsm[:, 0, 4, 8:16], par("a_log", 0, 8), ACT.Exp)
                A(dsm[:, :, 5, 0:8], dsm[:, :, 5, 0:8], ACT.Ln, bias=1.0).then_inc(s_logit_exp, 1)
                meet(c, s_met)
                for ch, (s, n) in enumerate(TILES):
                    act.wait_ge(s_logit_in, c.next(s_logit_in))
                    A(dER[:, :, 0:n], heads8(0, P, n), ACT.Exp)
                    A(ddec[0:n, :, 0:n], ddec[0:n, :, 0:n], ACT.Exp)
                    A(dsm[0:n, ch, 4, 0:8], dsm[0:n, ch, 3, 0:8], ACT.Exp).then_inc(s_logit_exp, 1)
                act.wait_ge(s_dn_v, 54)
                A(dsq[:, 0:8, :], dOT, ACT.Square).then_inc(s_squares, 1)
                norm_sums(1.0 / P, ps[0:16, 6, 0:TOK], row_rstd[0:16, :])
                meet(c, s_met)
                feed("dn_out", dOT, TOK)
                norm_post()
            if on["ffn1"]:
                ffn(1)

        @block.vector
        def _(v):
            c = Counts(v, s_dve_own)
            V = nc.vector
            TT, TS, STT = V.tensor_tensor, V.tensor_scalar, V.scalar_tensor_tensor

            def split(at):
                if at.b is None and at.unit >= limit:
                    return
                for half in range(2):
                    v.wait_ge(s_hi_ready, at.halves(half + 1))
                    TT(w_lo[:, at.slot(half)], raw[:, at.raw, 4 * half:4 * half + 4, :],
                       w_hi[:, at.slot(half)].bitcast(f32), SUB).then_inc(s_raw_free, 1)

            def split_all(name, skip=0, count=None):
                base = first[name] + skip
                rounds = (count or dict(parts)[name]) // ROUND
                last = base + rounds * ROUND == limit
                if rounds - last > 0:
                    with v.Fori(0, rounds - last) as b:
                        for j in range(ROUND):
                            split(At(base + j + 2, b))
                if last:
                    for j in range(ROUND):
                        split(At(base + (rounds - 1) * ROUND + j + 2))

            def low_h(width):
                for k in range(KT):
                    v.wait_ge(s_act_hi, c.next(s_act_hi))
                    last = TT(h_lo[:, k, 0:width], h[:, k, 0:width], h_hi[:, k, 0:width].bitcast(f32), SUB)
                last.then_inc(s_h_ready, 1)

            def feed(name, src, width):
                base, rounds = first[name], dict(parts)[name] // ROUND

                def round_of(r, b=None):
                    for k in range(KT):
                        v.wait_ge(s_act_hi, c.next(s_act_hi))
                        last = TT(h_lo[:, k, 0:width], src[:, (r * KT + k) if b is None else b * KT + (r * KT + k), 0:width],
                                  h_hi[:, k, 0:width].bitcast(f32), SUB)
                    last.then_inc(s_h_ready, 1)
                    for m in range(ROUND):
                        split(At(base + r * ROUND + m + 2, b))

                round_of(0)
                if rounds > 2:
                    with c.loop(rounds - 2, act_hi=KT) as b:
                        round_of(1, b)
                if rounds > 1:
                    round_of(rounds - 1)

            def inverse_root(dst):
                v.wait_ge(s_root, c.next(s_root))
                return V.reciprocal(dst, dst)

            def norm_one(n):
                c.link(inverse_root(rstd[:, 0:SEQ]))
                for k in range(KT):
                    STT(h[:, k, 0:SEQ], x[:, k, one], gains[:, n, k:k + 1], rstd[:, 0:SEQ], MUL, MUL).then_inc(s_h_scaled, 1)
                low_h(SEQ)

            def norm_two(gain):
                c.link(inverse_root(rstd[:, :]))
                for k in range(KT):
                    STT(h[:, k, :], x[:, k, :], gain[:, k:k + 1], rstd[:, :], MUL, MUL).then_inc(s_h_whole, 1)
                low_h(TOK)

            def add_gated(src, gate):
                v.wait_ge(s_acc_done, c.next(s_acc_done))
                for k in range(KT):
                    last = STT(x[:, k, one], src(k), mods[:, gate + k:gate + k + 1], x[:, k, one], MUL, ADD)
                last.then_inc(s_x_ready, 1)
                v.wait_ge(s_x_ready, c.next(s_x_ready))

            def norm_post(gain):
                c.link(inverse_root(rstd[:, :]))
                for k in range(KT):
                    last = STT(fo[:, k, :], fo[:, k, :], gain[:, k:k + 1], rstd[:, :], MUL, MUL)
                c.link(last)
                TT(x[:, :, :], x[:, :, :], fo, ADD).then_inc(s_x_ready, 1)
                v.wait_ge(s_x_ready, c.next(s_x_ready))
                meet(c, s_met)

            v.wait_ge(s_consts_in, c.next(s_consts_in, 64))
            v.wait_ge(s_memsets, c.next(s_memsets, 6))
            c.link(V.tensor_copy(rope[:, 0, :], posn))
            c.link(TS(rope[:, 1, :], rope[:, 0, :], inv_freq, None, MUL))
            c.link(TS(rope[:, 2, :], rope[:, 1, :], float(0.5 / np.pi), 12582912.0, MUL, ADD))
            c.link(TS(rope[:, 2, :], rope[:, 2, :], -12582912.0, None, ADD))
            for k, piece in enumerate(TWO_PI_PARTS):
                c.link(STT(rope[:, 1, :], rope[:, 2, :], -piece, rope[:, 1, :], MUL, ADD))
            c.link(TS(rope[:, 4, :], rope[:, 1, :], -3.1415925, 3.1415925, ALU.max, ALU.min))
            STT(rope[:, 5, :], rope[:, 4, :], -1.0, rope[:, 4, :], MUL, ALU.max).then_inc(s_rope_args, 1)
            v.wait_ge(s_ada_t, c.next(s_ada_t))
            c.link(TT(mods[:], ps[:, 2, 0:96], par("ada_b", 0, 96), ADD))
            for n in range(4):
                layer, which = n // 2, n % 2
                at = layer * 48 + 8 + 24 * which
                gain = par("norm_ffn" if which else "norm_mix", layer * 8, 8)
                STT(gains[:, n, :], mods[:, at:at + 8], 1.0, gain, ADD, MUL)
            split(At(ADA_UNITS))
            split(At(ADA_UNITS + 1))
            meet(c, s_met)

            if on["ret"]:
                norm_one(0)
                split_all("ret_in")
                v.wait_ge(s_rope_ready, c.next(s_rope_ready))
                v.wait_ge(s_bank_free, 4 + blocks_before["ret_in"] + 16)
                pair = qk.rearrange("p (m two) t -> p m two t", two=2)
                x1, x2 = pair[:, :, 0, :], pair[:, :, 1, :]
                cosb, sinb = bc(cosT, 1, [P, 8, SEQ]), bc(sinT, 1, [P, 8, SEQ])
                prod = [ropet[:, k, :].rearrange("p (m t) -> p m t", m=8) for k in range(4)]
                TT(prod[0], x1, cosb, MUL)
                TT(prod[1], x2, sinb, MUL)
                TT(prod[2], x1, sinb, MUL)
                c.link(TT(prod[3], x2, cosb, MUL))
                TT(x1, prod[0], prod[1], SUB)
                TT(x2, prod[2], prod[3], ADD)
                meet(c, s_met)
                v.wait_ge(s_ret_in, c.next(s_ret_in, 16))
                for hd in range(RH):
                    v.wait_ge(s_scores_ready, c.next(s_scores_ready))
                    TT(sT[:, hd], ps[:, hd, :].rearrange("p (j t) -> p j t", j=2), ret_dec[:, :, hd, :],
                       MUL).then_inc(s_decayed, 1)
                c.link(inverse_root(yrs))
                yv = yT.rearrange("p (g b) t -> p g b t", g=RH)
                c.link(TT(yv, yv, bc(yrs, 2, [P, RH, 4, SEQ]), MUL))
                TT(yT, yT, gT, MUL)
                meet(c, s_met)
                feed("ret_out", yT, SEQ)
                add_gated(lambda k: ps[:, k, 0:SEQ], 16)

            def top16(src, rest, vals, idx, rows):
                for r in rows:
                    last = V.max(vals(r)[:, 0:8], src(r))
                c.link(last)
                for r in rows:
                    V.max_index(idx(r)[:, 0:8], vals(r)[:, 0:8], src(r))
                    last = V.match_replace(rest(r), vals(r)[:, 0:8], src(r), -3e38)
                c.link(last)
                for r in rows:
                    last = V.max(vals(r)[:, 8:16], rest(r))
                c.link(last)
                for r in rows:
                    last = V.max_index(idx(r)[:, 8:16], vals(r)[:, 8:16], rest(r))
                c.link(last)

            def peer(layer):
                norm_one(2 * layer + 1)
                meet(c, s_met)
                split_all(f"query{layer}")
                for tt in range(2):
                    v.wait_ge(s_key_copied, c.next(s_key_copied, 4))
                    top16(lambda m: sc[:, tt, m, :], lambda m: sc2[:, tt, m, :], lambda m: tv[:, tt, m, :],
                          lambda m: ti[:, tt, m, :], range(16))
                    V.tensor_copy(tif[:, tt], ti[:, tt])
                    first_k = tv[:, tt].rearrange("p (g two) k -> p g two k", two=2)
                    c.link(TT(cand[:, tt].rearrange("p g (a b) -> p g a b", a=TOPK),
                              first_k[:, :, 0, :].unsqueeze(3).to_broadcast([P, HH, TOPK, TOPK]),
                              first_k[:, :, 1, :].unsqueeze(2).to_broadcast([P, HH, TOPK, TOPK]), ADD))
                    top16(lambda g: cand[:, tt, g, :], lambda g: cand2[:, tt, g, :], lambda g: bv[:, tt, g, :],
                          lambda g: bp[:, tt, g, :], range(HH))
                    flat = bp[:, tt].rearrange("p g k -> p (g k)")
                    TS(bq[:, tt, 0, :], flat, 4, None, ALU.logical_shift_right)
                    c.link(TS(bq[:, tt, 1, :], flat, 15, None, ALU.bitwise_and))
                    c.link(V.tensor_copy(bqf[:, tt], bq[:, tt]))
                    for n in range(2):
                        hot = cand2[:, tt].rearrange("p g (k a) -> p (g k) a", a=TOPK)
                        c.link(TT(hot, bqf[:, tt, n, :].unsqueeze(2).to_broadcast([P, P, TOPK]),
                                  bc(iota[:, 0:TOPK], 1, [P, P, TOPK]), ALU.is_equal))
                        hot4 = cand2[:, tt].rearrange("p g (k a) -> p g k a", a=TOPK)
                        index = tif[:, tt].rearrange("p (g two) a -> p g two a", two=2)[:, :, n, :]
                        c.link(TT(hot4, hot4, index.unsqueeze(2).to_broadcast([P, HH, TOPK, TOPK]), MUL))
                        c.link(V.tensor_reduce(picked[:, tt, n, :], hot, op=ADD, axis=AX))
                    last = TT(picked[:, tt, 2, :].rearrange("p (g k) -> p g k", k=TOPK), bv[:, tt],
                              bv[:, tt, :, 0:1].to_broadcast([P, HH, TOPK]), SUB)
                last.then_inc(s_gate_in, 1)
                v.wait_ge(s_gate_exp, c.next(s_gate_exp))
                gates = picked[:, :, 2, :].rearrange("p t (g k) -> p t g k", k=TOPK)
                c.link(V.tensor_reduce(gsum, gates, op=ADD, axis=AX))
                c.link(V.reciprocal(gsum, gsum))
                TT(gates, gates, gsum.unsqueeze(3).to_broadcast([P, 2, HH, TOPK]), MUL).then_inc(s_picks_ready, 1)
                meet(c, s_met)

                by4 = [chosen[:, n, :].rearrange("p (g t) -> p g t", t=4) for n in range(3)]

                def group(g, buf, first_time):
                    if not first_time:
                        v.wait_ge(s_g_banks, c.next(s_g_banks))
                    TT(pick_j[:, buf], bc(iota, 1, [P, 4, P]), by4[1][:, g, :].unsqueeze(2).to_broadcast([P, 4, P]),
                       ALU.is_equal)
                    for q in range(4):
                        last = TS(pick_i[:, buf, q, :], iota, by4[0][:, g, q:q + 1], by4[2][:, g, q:q + 1], ALU.is_equal, MUL)
                    last.then_inc(s_picks_ready, 1)

                group(0, 0, True)
                group(1, 1, True)
                with c.loop(SEQ // 8 - 1, g_banks=2) as b:
                    group(b * 2 + 2, 0, False)
                    group(b * 2 + 3, 1, False)
                v.wait_ge(s_g_banks, c.next(s_g_banks, 2))
                meet(c, s_met)
                base = first[f"peer{layer}"]

                def mix(i, at, j):
                    split(at.plus(2))
                    v.wait_ge(s_gelu_done, i + (P * layer + 1))
                    if not (isinstance(i, int) and i < 2):
                        v.wait_ge(s_half_used, at.halves(-2))
                    c.link(TT(mixin[:, j % 2, :], mixin[:, j % 2, :], G[:, i, :], MUL))
                    c.link(V.tensor_copy(mixed_hi[:, j % 2, :], mixin[:, j % 2, :]))
                    TT(mixed_lo[:, j % 2, :], mixin[:, j % 2, :], mixed_hi[:, j % 2, :].bitcast(f32),
                       SUB).then_inc(s_mix_done, 1)

                mix(0, At(base), 0)
                for k in range(4):
                    mix(k + 1, At(base + 2 * k + 1), k + 1)
                    split(At(base + 2 * k + 4))
                rounds = (P - 1) // 4 - 1
                with c.loop(rounds, dve_own=8) as b:
                    for k in range(4):
                        mix(b * 4 + (k + 5), At(base + 8 + 2 * k + 1, b), k + 5)
                        split(At(base + 8 + 2 * k + 4, b))
                for i in range(4 + 4 * rounds, P - 1):
                    mix(i + 1, At(base + 2 * i + 1), i + 1)
                    split(At(base + 2 * i + 4))
                split(At(base + 2 * P + 1))
                add_gated(lambda k: ps[:, 4 + k // 2, (k % 2) * SEQ:(k % 2) * SEQ + SEQ], 48 * layer + 40)
                meet(c, s_met)

            if on["peer0"]:
                peer(0)

            if on["sgu"]:
                norm_one(2)
                split_all("sgu_in")
                v.wait_ge(s_mean_sum, c.next(s_mean_sum))
                c.link(TS(smean, ps[:, 4, 0:SEQ], 1.0 / SH, None, MUL))
                TT(sv, sv, bc(smean, 1, [P, ST_, SEQ]), SUB).then_inc(s_sgu_centred, 1)
                c.link(inverse_root(srstd))
                c.link(TT(sv, sv, bc(srstd, 1, [P, ST_, SEQ]), MUL))
                for m in range(ST_):
                    last = TS(sv[:, m, :], sv[:, m, :], par("sgu_ln_g", m), par("sgu_ln_b", m), MUL, ADD)
                last.then_inc(s_sgu_ready, 1)
                for n in range(12):
                    v.wait_ge(s_spatial_ready, c.next(s_spatial_ready))
                    TT(uT[:, 2 * n:2 * n + 2, :], ps[:, 4 + n % 4, :].rearrange("p (m t) -> p m t", m=2),
                       uT[:, 2 * n:2 * n + 2, :], MUL).then_inc(s_sgu_s, 1)
                meet(c, s_met)
                feed("sgu_out", uT, SEQ)
                add_gated(lambda k: ps[:, k, 0:SEQ], 48 + 16)
                meet(c, s_met)

            if on["peer1"]:
                peer(1)
            if on["final1"]:
                c.link(inverse_root(rstd[:, 0:SEQ]))
                for k in range(KT):
                    last = STT(x[:, k, one], x[:, k, one], par("norm_final", k), rstd[:, 0:SEQ], MUL, MUL)
                last.then_inc(s_x_ready, 1)
                v.wait_ge(s_x_ready, c.next(s_x_ready))

            if on["att"]:
                v.wait_ge(s_tabs_in, c.next(s_tabs_in, 48))
                norm_two(par("mix_pre", 0, 8))
                split_all("att_in")
                TS(qgain, par("q_gain"), ADH ** -0.5, None, MUL)
                c.link(V.memset(awork[:, 0:2], 0.0))
                v.wait_ge(s_scores_ready, c.next(s_scores_ready))
                for tt, (s, n) in enumerate(TILES):
                    last = TT(awork[0:n, 0, tt, :], ps[0:n, 5, tt * 16:tt * 16 + 16], par("b_forget", 0, 16)[0:n, :], ADD)
                c.link(last)
                STT(awork[:, 1], awork[:, 0], -1.0, awork[:, 0], MUL, ALU.min).then_inc(s_logit_in, 1)
                v.wait_ge(s_root, c.next(s_root))
                V.reciprocal(row_rstd, row_rstd).then_inc(s_inv, 1)
                for b in range(16):
                    v.wait_ge(s_norms, c.next(s_norms))
                    STT(aqk[:, b, :], aqk[:, b, :], qgain if b < 8 else par("k_gain"), ps[:, b % 4, 0:TOK], MUL,
                        MUL).then_inc(s_scaled, 1)
                v.wait_ge(s_logit_exp, c.next(s_logit_exp))
                c.link(STT(alf[:, :, 0:16], awork[:, 0], 0.0, awork[:, 1], ALU.min, SUB))
                TS(alf[:, :, 16:32], alf[:, :, 0:16], -1.0, None, MUL).then_inc(s_heads_prep, 1)
                v.wait_ge(s_cum_ready, c.next(s_cum_ready))
                V.tensor_copy(acum, ps[0:32, 5, 0:TOK])
                meet(c, s_met)
                half = tab("half", 32)
                for pr in range(AH // 2):
                    for par_ in range(2):
                        hd = 2 * pr + par_
                        TS(aL[0:32, par_, :], acum, half[:, 0:1], tab("selbot", 32)[:, hd:hd + 1], MUL, ADD)
                        TS(aR[0:32, par_, :], acum, half[:, 1:2], tab("seltop", 32)[:, hd:hd + 1], MUL,
                           ADD).then_inc(s_heads_prep, 1)
                    for par_ in range(2):
                        for tt, (s, n) in enumerate(TILES):
                            k = 3 * par_ + tt
                            v.wait_ge(s_att_s, c.next(s_att_s))
                            c.link(TT(ps[0:n, k, s:s + n], ps[0:n, k, s:s + n], tab("causal")[0:n, 0:n], ADD))
                            V.tensor_reduce(asm[0:n, 0, k:k + 1], ps[0:n, k, 0:s + n], op=ALU.max, axis=AX,
                                            negate=True).then_inc(s_att_m, 1)
                    for par_ in range(2):
                        for tt, (s, n) in enumerate(TILES):
                            k = 3 * par_ + tt
                            v.wait_ge(s_att_p, c.next(s_att_p))
                            c.link(V.reciprocal(asm[0:n, 1, k:k + 1], asm[0:n, 1, k:k + 1]))
                            TS(ap_[0:n, par_, tt, 0:s + n], ap_[0:n, par_, tt, 0:s + n], asm[0:n, 1, k:k + 1], None,
                               MUL).then_inc(s_att_pn, 1)
                    v.wait_ge(s_att_o, c.next(s_att_o))
                    TT(ay[:, pr, :], ps[:, 6, 0:TOK], aog[:, pr, :], MUL).then_inc(s_att_od, 1)
                meet(c, s_met)
                feed("att_out", ay, TOK)
                norm_post(par("mix_post", 0, 8))

            def conv(dst, src, w, taps):
                for back in range(1, taps):
                    last = STT(dst[:, back:TOK], src[:, 0:TOK - back], w(taps - 1 - back), dst[:, back:TOK], MUL, ADD)
                    if back < taps - 1:
                        c.link(last)
                return last

            def ffn(n):
                norm_two(par("ffn_pre", 8 * n, 8))
                c.n[s_bank_free.name] = 4 + blocks_before[f"up{n}"]
                w3 = par("ffn_conv", n * 132, 132).rearrange("p (b w) -> p b w", w=3)
                with c.loop(11, tap_done=4, bank_free=4, ffn_gelu=2, dve_own=4) as b:
                    for q in range(2):
                        for j in (2 * q, 2 * q + 1):
                            split(At(first[f"up{n}"] + j + 2, b, 4))
                            v.wait_ge(s_tap_done, c.next(s_tap_done))
                            conv(fconv[:, 0, j, :], ps[:, j, 0:TOK], lambda k: w3[:, b * 4 + j, k:k + 1],
                                 3).then_inc(s_bank_free, 1)
                        v.wait_ge(s_bank_free, c.next(s_bank_free, 2))
                        v.wait_ge(s_ffn_gelu, c.next(s_ffn_gelu))
                        TT(fact[:, b * 2 + q, :], fconv[:, 1, 2 * q, :], fconv[:, 0, 2 * q + 1, :], MUL)
                meet(c, s_met)
                feed(f"down{n}", fact, TOK)
                norm_post(par("ffn_post", 8 * n, 8))

            if on["ffn0"]:
                ffn(0)

            if on["dn"]:
                v.wait_ge(s_tabs_in, c.next(s_tabs_in, 16))
                norm_two(par("mix_pre", 8, 8))
                w4 = par("dn_conv", 0, 96).rearrange("p (b w) -> p b w", w=4)
                with c.loop(3, dn_silu=8, dve_own=24) as b:
                    for j in range(8):
                        split(At(first["dn_in"] + j + 2, b))
                        v.wait_ge(s_half_used, At(first["dn_in"] + j, b).halves(2))
                        v.wait_ge(s_dn_silu, c.next(s_dn_silu))
                        c.link(TS(dwork[:, j % 2, :], ps[:, j % 4, 0:TOK], w4[:, b * 8 + j, 3:4], None, MUL))
                        conv(dwork[:, j % 2, :], ps[:, j % 4, 0:TOK], lambda k: w4[:, b * 8 + j, k:k + 1],
                             4).then_inc(s_bank_free, 1)
                split_all("dn_in", 24, 8)
                c.link(V.memset(dsm, 0.0))
                v.wait_ge(s_scores_ready, c.next(s_scores_ready))
                for tt, (s, n) in enumerate(TILES):
                    V.tensor_copy(dsm[0:n, tt, 0, 0:8], ps[0:n, 5, tt * 16:tt * 16 + 8])
                    last = TT(dsm[0:n, tt, 1, 0:8], ps[0:n, 5, tt * 16 + 8:tt * 16 + 16], par("dt_bias", 0, 8)[0:n, :], ADD)
                c.link(last)
                STT(dsm[:, :, 5, 0:8], dsm[:, :, 1, 0:8], -1.0, dsm[:, :, 1, 0:8], MUL, ALU.min).then_inc(s_logit_in, 1)
                v.wait_ge(s_root, c.next(s_root))
                V.reciprocal(row_rstd[0:16, :], row_rstd[0:16, :]).then_inc(s_inv, 1)
                for b in range(16):
                    v.wait_ge(s_norms, c.next(s_norms))
                    STT(dqkv[:, b, :], dqkv[:, b, :], P ** -0.5 if b < 8 else 1.0, ps[:, b % 4, 0:TOK], MUL,
                        MUL).then_inc(s_scaled, 1)
                v.wait_ge(s_logit_exp, c.next(s_logit_exp))
                c.link(STT(dsm[:, :, 1, 0:8], dsm[:, :, 1, 0:8], 0.0, dsm[:, :, 5, 0:8], ALU.max, ADD))
                STT(dsm[:, :, 2, 0:8], dsm[:, :, 1, 0:8], -1.0, bc(dsm[:, 0, 4, 8:16], 1, [P, 3, 8]), MUL, MUL)
                V.memset(dST, 0.0)
                meet(c, s_met)
                idb = ident
                for ch, (s, n) in enumerate(TILES):
                    beta = dsm[0:n, ch, 0, 0:8]
                    beta_n = beta.unsqueeze(2).to_broadcast([n, 8, n])
                    v.wait_ge(s_dn_p, c.next(s_dn_p))
                    c.link(V.tensor_copy(dsm[0:n, ch, 3, 0:8], ps[0:n, 2, 0:8]))
                    c.link(TT(ddec[0:n, :, 0:n], heads8(0, n, n), dsm[0:n, ch, 3, 0:8].unsqueeze(2).to_broadcast([n, 8, n]), SUB))
                    TT(ddec[0:n, :, 0:n], ddec[0:n, :, 0:n], bc(tab("mneg")[0:n, 0:n], 1, [n, 8, n]),
                       ADD).then_inc(s_logit_in, 1)
                    V.tensor_copy(dX[0:n, :, 0:n], bc(idb[0:n, 0:n], 1, [n, 8, n]))
                    V.tensor_copy(dXT[0:n, :, 0:n], bc(idb[0:n, 0:n], 1, [n, 8, n]))
                    v.wait_ge(s_logit_exp, c.next(s_logit_exp))
                    TT(dLT[0:n, :, 0:n], heads8(4, n, n), ddec[0:n, :, 0:n], MUL)
                    TT(dqd[:, :, 0:n], dqkv[:, 0:8, s:s + n], dER[:, :, 0:n], MUL)
                    TT(dsm[0:n, ch, 4, 0:8], dsm[0:n, ch, 4, 0:8], beta, MUL)
                    TT(dQK[0:n, :, 0:n], heads8(6, n, n), ddec[0:n, :, 0:n], MUL).then_inc(s_dn_v, 1)
                    v.wait_ge(s_dn_p, c.next(s_dn_p))
                    TT(dkb[0:n], heads8(0, n, P), dsm[0:n, ch, 4, 0:8].unsqueeze(2).to_broadcast([n, 8, P]), MUL)
                    TT(dkd[0:n], heads8(0, n, P), ddec[0:n, :, n - 1:n].to_broadcast([n, 8, P]), MUL)
                    TT(dvb[0:n], heads8(2, n, P), beta.unsqueeze(2).to_broadcast([n, 8, P]), MUL).then_inc(s_dn_v, 1)
                    levels = n.bit_length() - 1
                    mask = tab("levels").rearrange("p (l c) -> p l c", l=LEVELS)

                    def masked(lv):
                        return TT(dMT[0:n, :, 0:n], dLT[0:n, :, 0:n], bc(mask[0:n, lv, 0:n], 1, [n, 8, n]), MUL)

                    masked(0).then_inc(s_dn_v, 1)
                    for lv in range(levels):
                        v.wait_ge(s_dn_p, c.next(s_dn_p))
                        TT(dT1[0:n, :, 0:n], heads8(0, n, n), beta_n, MUL).then_inc(s_dn_v, 1)
                        if lv < levels - 1:
                            masked(lv + 1)
                        v.wait_ge(s_dn_p, c.next(s_dn_p))
                        TT(dX[0:n, :, 0:n], dX[0:n, :, 0:n], heads8(2, n, n), SUB)
                        TT(dXT[0:n, :, 0:n], dXT[0:n, :, 0:n], heads8(4, n, n), SUB).then_inc(s_dn_v, 1)
                    v.wait_ge(s_dn_p, c.next(s_dn_p))
                    TS(dW[:, :, 0:n], heads8(0, P, n), -1.0, None, MUL).then_inc(s_dn_v, 1)
                    v.wait_ge(s_dn_p, c.next(s_dn_p))
                    V.tensor_copy(dU[0:n], heads8(2, n, P)).then_inc(s_dn_v, 1)
                    v.wait_ge(s_dn_p, c.next(s_dn_p))
                    V.tensor_copy(dOT[:, :, s:s + n], heads8(4, P, n))
                    c.link(TT(dST, dST, dER[:, :, n - 1:n].to_broadcast([P, 8, P]), MUL))
                    TT(dST, dST, heads8(6, P, P), ADD).then_inc(s_dn_v, 1)
                v.wait_ge(s_root, c.next(s_root))
                V.reciprocal(row_rstd[0:16, :], row_rstd[0:16, :]).then_inc(s_inv, 1)
                for b in range(8):
                    v.wait_ge(s_norms, c.next(s_norms))
                    last = STT(dOT[:, b, :], dOT[:, b, :], par("o_gain"), ps[:, b % 4, 0:TOK], MUL, MUL)
                    last.then_inc(s_scaled, 1)
                v.wait_ge(s_scaled, 16 + 16 + 8)
                TT(dOT, dOT, dog, MUL)
                meet(c, s_met)
                feed("dn_out", dOT, TOK)
                norm_post(par("mix_post", 8, 8))
            if on["ffn1"]:
                ffn(1)
            v.drain().then_inc(s_result_ready, 1)


def columns(a):
    a = np.asarray(a)
    return np.ascontiguousarray(a.reshape(-1, P).T)


def units_k(w):
    K, N = w.shape
    return np.ascontiguousarray(w.reshape(KT, P, N // P, P).transpose(2, 1, 0, 3))


def units_out(w):
    K = w.shape[0]
    rounds = -(-K // D)
    full = np.zeros((rounds * D, D), w.dtype)
    full[:K] = w
    return np.ascontiguousarray(full.reshape(rounds, KT, P, KT, P).transpose(0, 3, 2, 1, 4)).reshape(-1, P, KT, P)


def kernel(_until=None, **inputs):
    import concourse.bacc as bacc
    from concourse import mybir
    from concourse.bass_utils import run_bass_kernel_spmd

    a = {k: np.asarray(v) for k, v in inputs.items()}
    f32 = np.float32
    c1, c2, ret_dec = shape_constants()
    rows = lambda v: np.broadcast_to(v.reshape(1, -1), (P, v.size))
    conv = lambda w: w.T.reshape(-1, P, w.shape[0]).transpose(1, 0, 2).reshape(P, -1)
    pairs = lambda w: w.reshape(w.shape[0], 2, FFT, P).transpose(0, 2, 1, 3).reshape(w.shape[0], -1)
    twice = lambda g: np.concatenate([g, g]).reshape(P, 1)
    pieces = {
        "c": columns(a["c"]), "ada_b": columns(a["ada_b"]), "norm_mix": columns(a["norm_mix"]),
        "norm_ffn": columns(a["norm_ffn"]), "norm_final": columns(a["norm_final"]), "sgu_b_in": columns(a["sgu_b_in"]),
        "sgu_ln_g": columns(a["sgu_ln_g"]), "sgu_ln_b": columns(a["sgu_ln_b"]), "mix_pre": columns(a["norm_mix_pre_2"]),
        "mix_post": columns(a["norm_mix_post_2"]), "ffn_pre": columns(a["norm_ffn_pre_2"]),
        "ffn_post": columns(a["norm_ffn_post_2"]), "q_gain": twice(a["attn_q_norm_2"][0]),
        "k_gain": twice(a["attn_k_norm_2"][0]), "o_gain": a["dn_o_norm_2"].reshape(P, 1),
        "ffn_conv": np.concatenate([conv(pairs(w)) for w in a["ffn_conv_2"]], 1), "dn_conv": conv(a["dn_conv_2"][0]),
        "b_forget": rows(a["attn_b_forget_2"]), "a_log": rows(a["dn_a_log_2"]), "dt_bias": rows(a["dn_dt_bias_2"]),
    }
    params = np.concatenate([pieces[n] for n, _ in PCOLS], 1)
    assert params.shape == (P, PW), params.shape
    ada = a["ada_w"]
    aw, dw = a["attn_w_in_2"][0], a["dn_w_in_2"][0]
    tail = lambda w: np.ascontiguousarray(w[:, -16:].reshape(KT, P, 16).transpose(1, 0, 2))
    feed = {
        "params": params, "const1": c1, "const2": c2, "ret_dec": ret_dec,
        "xT": np.ascontiguousarray(a["x"][0].T.reshape(KT, P, SEQ).transpose(1, 0, 2)),
        "metaT": np.ascontiguousarray(a["meta_tokens_2"].T.reshape(KT, P, META).transpose(1, 0, 2)),
        "positions": np.ascontiguousarray(np.broadcast_to(a["positions"][0][None, :], (P, SEQ))),
        "ada": np.concatenate([units_k(ada[0]), units_k(ada[1])]),
        "ret_in": units_k(a["ret_w_in"][0]), "ret_out": units_out(a["ret_w_out"][0]),
        "query0": units_k(a["peer_w_query"][0]), "query1": units_k(a["peer_w_query"][1]),
        "keysT": np.ascontiguousarray(a["peer_sub_keys"].reshape(2, 16, NKEYS, P).transpose(0, 3, 1, 2)),
        "u": np.ascontiguousarray(a["peer_u"].reshape(2, P, P, KT, P).transpose(0, 1, 4, 3, 2)),
        "v": a["peer_v"].reshape(2, P, P, KT, P),
        "sgu_in": units_k(a["sgu_w_in"][0]), "sgu_out": units_out(a["sgu_w_out"][0]),
        "w_s": np.ascontiguousarray(a["sgu_w_s"][0].transpose(2, 0, 1)), "b_s": a["sgu_b_s"],
        "att_in": units_k(np.ascontiguousarray(aw[:, :4096])), "att_wf": tail(aw), "att_out": units_out(a["attn_w_out_2"][0]),
        "dn_in": units_k(np.ascontiguousarray(dw[:, :4096])), "dn_wf": tail(dw), "dn_out": units_out(a["dn_w_out_2"][0]),
    }
    for n in range(2):
        feed[f"up{n}"] = units_k(pairs(a["ffn_w_up_2"][n]))
        feed[f"down{n}"] = units_out(a["ffn_w_down_2"][n])

    nc = bacc.Bacc("TRN2", target_bir_lowering=False, num_devices=1)
    t = {k: nc.dram_tensor(f"in_{k}", v.shape, mybir.dt.from_np(v.dtype), kind="ExternalInput").ap()
         for k, v in feed.items()}
    t["scratch"] = nc.dram_tensor("ada_scratch", (1, 12288), mybir.dt.float32, kind="Internal").ap()
    width = SEQ if _until is None else TOK
    out = nc.dram_tensor("out_xT", (P, KT, width), mybir.dt.float32, kind="ExternalOutput").ap()
    build_program(nc, t, out, _until)
    r = run_bass_kernel_spmd(nc, [{f"in_{k}": v for k, v in feed.items()}], core_ids=[0])
    got = r.results[0]["out_xT"]
    if _until is not None:
        return got
    return np.ascontiguousarray(got.transpose(2, 1, 0)).reshape(1, SEQ, D)
```

```python
from contextlib import ExitStack, contextmanager

import numpy as np

P = 128
D = 1024
KT = D // P
SEQ = 256
META = 16
TOK = SEQ + META
T0 = META
RAW = 4
ADA_UNITS = 96
ROUND = 8
BANK = 512
EPS = 1e-6
NEG = -1e30
TWO_PI_PARTS = (6.28125, 1.9350051879882812e-03, 3.0199159819567e-07)
RH, RDK, RDV = 4, 256, 512
CHUNK = 64
HH, TOPK, NKEYS = 8, 16, 128
SG, SH = 8, 3072
ST_ = SH // P
AH, ADH = 16, 64
DH = 8
FFT = 2816 // P
TILES = [(0, META), (META, P), (META + P, P)]
LEVELS = 7

PCOLS = [("c", 8), ("ada_b", 96), ("norm_mix", 16), ("norm_ffn", 16), ("norm_final", 8), ("sgu_b_in", 48),
         ("sgu_ln_g", 24), ("sgu_ln_b", 24), ("mix_pre", 16), ("mix_post", 16), ("ffn_pre", 16), ("ffn_post", 16),
         ("q_gain", 1), ("k_gain", 1), ("o_gain", 1), ("ffn_conv", 2 * 44 * 3), ("dn_conv", 24 * 4),
         ("b_forget", 16), ("a_log", 8), ("dt_bias", 8)]
PO, _o = {}, 0
for _n, _w in PCOLS:
    PO[_n] = _o
    _o += _w
PW = _o
C1COLS = [("ident", 128), ("iota", 128), ("inv_freq", 1)]
C2COLS = [("tri", 3 * TOK), ("causal", 128), ("mneg", 128), ("levels", LEVELS * 128), ("colsel", 64), ("colsel1", 32),
          ("rowsel", 16 * 128), ("rowsel1", 16 * 128), ("half", 2), ("selbot", 16), ("seltop", 16)]


def offsets(cols):
    out, at = {}, 0
    for name, width in cols:
        out[name] = (at, width)
        at += width
    return out, at


C1O, C1W = offsets(C1COLS)
C2O, C2W = offsets(C2COLS)


def shape_constants():
    c1 = np.zeros((P, C1W), np.float32)
    c2 = np.zeros((P, C2W), np.float32)

    def put(c, o, name, v):
        a, w = o[name]
        v = np.asarray(v, np.float32).reshape(v.shape[0], w)
        c[:v.shape[0], a:a + w] = v

    put(c1, C1O, "ident", np.eye(P))
    put(c1, C1O, "iota", np.tile(np.arange(P, dtype=np.float32), (P, 1)))
    half = RDK // 2
    put(c1, C1O, "inv_freq", (np.float32(1.0) / (np.float32(10000.0) ** (
        np.arange(half, dtype=np.float32) / np.float32(half)))).reshape(P, 1))
    tri = np.zeros((P, 3, TOK))
    for t, (s, n) in enumerate(TILES):
        for j in range(n):
            tri[j, t, s + j:] = 1.0
    put(c2, C2O, "tri", tri)
    i = np.arange(P)
    put(c2, C2O, "causal", np.where(i[None, :] > i[:, None], NEG, 0.0))
    put(c2, C2O, "mneg", np.where(i[None, :] < i[:, None], NEG, 0.0))
    lv = np.zeros((P, LEVELS, P))
    for n in range(LEVELS):
        b = 1 << n
        lv[:, n, :] = ((i[None, :] // b) % 2 == 1) & (i[:, None] // b == i[None, :] // b - 1)
    put(c2, C2O, "levels", lv)
    cs = np.zeros((P, 64))
    cs[:64, 32] = 1
    cs[64:, 33] = 1
    put(c2, C2O, "colsel", cs)
    cs = np.zeros((P, 32))
    cs[:, 16] = 1
    put(c2, C2O, "colsel1", cs)
    rs = np.zeros((32, 16, P))
    rs1 = np.zeros((16, 16, P))
    for b in range(16):
        rs[2 * b, b, :64] = 1
        rs[2 * b + 1, b, 64:] = 1
        rs1[b, b, :] = 1
    put(c2, C2O, "rowsel", rs)
    put(c2, C2O, "rowsel1", rs1)
    hf = np.zeros((32, 2))
    hf[:16, 0] = 1
    hf[16:, 1] = 1
    put(c2, C2O, "half", hf)
    sb = np.zeros((32, 16))
    stp = np.zeros((32, 16))
    for h in range(16):
        stp[h, h] = 1
        sb[16 + h, h] = 1
    put(c2, C2O, "selbot", sb)
    put(c2, C2O, "seltop", stp)
    ret = np.zeros((P, 2, RH, SEQ))
    pos = np.arange(SEQ)
    for h in range(RH):
        lg = np.log(1.0 - 2.0 ** (-5.0 - h))
        dist = np.abs(pos[None, :] - pos[:, None]).astype(np.float64)
        d = np.exp(lg * dist) * (pos[None, :] // CHUNK >= pos[:, None] // CHUNK)
        ret[:, :, h, :] = (d * RDK ** -0.5).reshape(2, P, SEQ).transpose(1, 0, 2)
    return c1, c2, ret.astype(np.float32).reshape(P, -1)


class At:

    def __init__(self, unit, b=None, step=ROUND):
        self.unit, self.b, self.step = unit, b, step
        self.raw = unit % RAW

    def plus(self, n):
        return At(self.unit + n, self.b, self.step)

    def number(self, k=0):
        return self.unit + k if self.b is None else self.b * self.step + (self.unit + k)

    def fill(self):
        n = self.unit // RAW + 1
        return n if self.b is None else self.b * (self.step // RAW) + n

    def halves(self, k):
        n = 2 * (self.unit - ADA_UNITS) + k
        return n if self.b is None else self.b * (2 * self.step) + n

    def slot(self, half):
        return (2 * self.unit + half) % 4


class Counts:

    def __init__(self, engine, own=None):
        self.engine, self.own, self.n, self.reg, self.per = engine, own, {}, None, {}

    def value(self, sem):
        v = self.n.get(sem.name, 0)
        return self.reg * self.per.get(sem.name, 0) + v if self.reg is not None else v

    def next(self, sem, k=1):
        self.n[sem.name] = self.n.get(sem.name, 0) + k
        return self.value(sem)

    def link(self, instruction):
        instruction.then_inc(self.own, 1)
        self.engine.wait_ge(self.own, self.next(self.own))

    @contextmanager
    def loop(self, count, **per):
        with self.engine.Fori(0, count) as i:
            before = dict(self.n)
            self.reg, self.per = i, per
            yield i
            self.reg = None
        for name in self.n:
            grew = self.n[name] - before.get(name, 0)
            assert grew == per.get(name, 0), (name, grew, per.get(name, 0))
            self.n[name] += grew * (count - 1)


def build_program(nc, t, out, until=None, taps=None):
    from concourse import mybir
    f32, bf16, u32, i32 = mybir.dt.float32, mybir.dt.bfloat16, mybir.dt.uint32, mybir.dt.int32
    ALU, ACT = mybir.AluOpType, mybir.ActivationFunctionType
    AX = mybir.AxisListType.X
    MUL, ADD, SUB = ALU.mult, ALU.add, ALU.subtract

    ctx = ExitStack()
    with ctx:
        def sb(name, shape, dt=f32):
            return ctx.enter_context(nc.sbuf_tensor(name, shape, dt))

        f32r = mybir.dt.float32r
        raw = sb("raw", [P, RAW, KT, P])
        w_hi = sb("w_hi", [P, 4, KT // 2, P], f32r)
        w_lo = sb("w_lo", [P, 4, KT // 2, P], f32r)
        x = sb("x", [P, KT, TOK])
        h_hi = sb("h_hi", [P, KT, TOK], f32r)
        h_lo = sb("h_lo", [P, KT, TOK], f32r)
        params = sb("params", [P, PW])
        const1 = sb("const1", [P, C1W])
        ones = sb("ones", [P, P])
        zeros_b = sb("zeros_b", [P, P], bf16)
        small = sb("small", [P, 4])
        mods = sb("mods", [P, 96])
        gains = sb("gains", [P, 4, KT])
        rstd = sb("rstd", [P, TOK])
        mixed_hi = sb("mixed_hi", [P, 2, SEQ], f32r)
        mixed_lo = sb("mixed_lo", [P, 2, SEQ], f32r)
        pick_i = sb("pick_i", [P, 2, 4, P])
        pick_j = sb("pick_j", [P, 2, 4, P])
        chosen = sb("chosen", [P, 3, SEQ])
        silu_c = sb("silu_c", [P, KT])
        arena = sb("arena", [P, 32768])
        ps = ctx.enter_context(nc.psum_tensor("ps", [P, 8, BANK], f32))

        def view(at, *shape):
            n = int(np.prod(shape))
            a = arena[:, at:at + n]
            if len(shape) == 1:
                return a
            names = " ".join(f"d{k}" for k in range(len(shape)))
            return a.rearrange(f"p ({names}) -> p {names}", **{f"d{k}": s for k, s in enumerate(shape[:-1])})

        ident = const1[:, 0:128]
        iota = const1[:, 128:256]
        inv_freq = const1[:, 256:257]
        eps, half_pi = small[:, 0:1], small[:, 1:2]

        def par(name, k=0, n=1):
            return params[:, PO[name] + k:PO[name] + k + n]

        def bc(ap, axis, shape):
            return ap.unsqueeze(axis).to_broadcast(list(shape))

        def sem(name):
            return ctx.enter_context(nc.semaphore(name))

        s_consts_in = sem("consts_in")
        s_ret_in = sem("ret_in")
        s_keys_in = sem("keys_in")
        s_sgu_in = sem("sgu_in")
        s_tabs_in = sem("tabs_in")
        s_row_out = sem("row_out")
        s_row_in = sem("row_in")
        s_out_done = sem("out_done")
        s_result_ready = sem("result_ready")
        s_memsets = sem("memsets")
        s_met = sem("met")
        s_half_used = sem("half_used")
        s_hi_ready = sem("hi_ready")
        s_raw_free = sem("raw_free")
        s_bank_free = sem("bank_free")
        s_act_own = sem("act_own")
        s_dve_own = sem("dve_own")
        s_c_act = sem("c_act")
        s_rope_args = sem("rope_args")
        s_rope_ready = sem("rope_ready")
        s_ada_row = sem("ada_row")
        s_ada_t = sem("ada_t")
        s_squares = sem("squares")
        s_sums = sem("sums")
        s_mean_sum = sem("mean_sum")
        s_root = sem("root")
        s_inv = sem("inv")
        s_tap_done = sem("tap_done")
        s_h_scaled = sem("h_scaled")
        s_h_whole = sem("h_whole")
        s_act_hi = sem("act_hi")
        s_h_ready = sem("h_ready")
        s_acc_done = sem("acc_done")
        s_out_ready = sem("out_ready")
        s_x_ready = sem("x_ready")
        s_vt_ready = sem("vt_ready")
        s_vt_copied = sem("vt_copied")
        s_scores_ready = sem("scores_ready")
        s_decayed = sem("decayed")
        s_y_ready = sem("y_ready")
        s_y_copied = sem("y_copied")
        s_key_scores = sem("key_scores")
        s_key_copied = sem("key_copied")
        s_gate_in = sem("gate_in")
        s_gate_exp = sem("gate_exp")
        s_picks_ready = sem("picks_ready")
        s_tables_ready = sem("tables_ready")
        s_g_banks = sem("g_banks")
        s_g_applied = sem("g_applied")
        s_chosen_ready = sem("chosen_ready")
        s_mix_done = sem("mix_done")
        s_sgu_centred = sem("sgu_centred")
        s_sgu_ready = sem("sgu_ready")
        s_spatial_ready = sem("spatial_ready")
        s_sgu_s = sem("sgu_s")
        s_norms = sem("norms")
        s_scaled = sem("scaled")
        s_heads_prep = sem("heads_prep")
        s_cum_ready = sem("cum_ready")
        s_att_s = sem("att_s")
        s_att_m = sem("att_m")
        s_att_p = sem("att_p")
        s_att_pn = sem("att_pn")
        s_att_t = sem("att_t")
        s_att_tc = sem("att_tc")
        s_att_o = sem("att_o")
        s_att_od = sem("att_od")
        s_logit_in = sem("logit_in")
        s_logit_exp = sem("logit_exp")
        s_ffn_gelu = sem("ffn_gelu")
        s_dn_silu = sem("dn_silu")
        s_dn_p = sem("dn_p")
        s_dn_v = sem("dn_v")
        s_fo_copied = sem("fo_copied")
        full = [ctx.enter_context(nc.semaphore(f"raw_full{k}")) for k in range(RAW)]

        ada_row = arena[0:1, 0:12288]
        ada_sq = arena[0:96, 12288:12416]
        rope = view(16384, 8, SEQ)
        posn = view(18432, SEQ).bitcast(i32)
        qk = view(0, 16, SEQ)
        vT = view(4096, 16, SEQ)
        gT = view(8192, 16, SEQ)
        vtok = view(12288, 2, 2048)
        cosT, sinT = rope[:, 6, :], rope[:, 7, :]
        ropet = view(18688, 4, 2048)
        yT = view(0, 16, SEQ)
        sT = view(4096, RH, 2, SEQ)
        ysq = view(18688, 16, SEQ)
        yrs = view(22784, RH, SEQ)
        ret_dec = view(26880, 2, RH, SEQ)
        sq = view(22400, KT, TOK)
        h = sq
        B2 = 16384
        sc = view(B2, 2, 16, P)
        qT = view(B2 + 4096, 16, SEQ)
        sc2 = view(B2 + 4096, 16, P)
        cand = view(B2 + 6144, HH, TOPK * TOPK)
        keysT = view(B2 + 8192, 16, P)
        cand2 = view(B2 + 8192, HH, TOPK * TOPK)
        tv = view(B2 + 10240, 2, 16, TOPK)
        ti = view(B2 + 10752, 2, 16, TOPK).bitcast(u32)
        tif = view(B2 + 11264, 2, 16, TOPK)
        bv = view(B2 + 11776, 2, HH, TOPK)
        bp = view(B2 + 12032, 2, HH, TOPK).bitcast(u32)
        bq = view(B2 + 12288, 2, 2, HH * TOPK).bitcast(u32)
        bqf = view(B2 + 12800, 2, 2, HH * TOPK)
        picked = view(B2 + 13312, 2, 3, P)
        gsum = view(B2 + 14080, 2, HH)
        G = view(0, P, SEQ)
        uT = view(0, ST_, SEQ)
        sv = view(6144, ST_, SEQ)
        ssq = view(12288, ST_, SEQ)
        svtok = view(12288, 2, SH)
        smean = view(18432, SEQ)
        srstd = view(18688, SEQ)
        sws = view(20000, SG, P)
        sbs = view(21024, SG, P)
        tabs = view(24576, C2W)
        T2 = 24576 + C2W
        dwf = view(T2, KT, 16)
        awf = view(T2 + 128, KT, 16)
        row_rstd = arena[0:32, T2 + 256:T2 + 256 + TOK]
        dsm = view(T2 + 528, 3, 6, 16)
        assert T2 + 528 + 288 <= 32768
        fo = view(20224, KT, TOK)

        def tab(name, rows=P):
            a, w = C2O[name]
            return tabs[0:rows, a:a + w]

        aqk = view(0, 16, TOK)
        aqkv = view(0, 24, TOK)
        avT = view(4352, 8, TOK)
        aog = view(6528, 8, TOK)
        asq = view(8704, 16, TOK)
        avtok = view(13056, 3, D)
        alf = view(16528, 3, 32)
        awork = view(16640, 4, 3, 16)
        acum = arena[0:32, 16832:16832 + TOK]
        aL = view(17104, 2, TOK)
        aR = view(17648, 2, TOK)
        asm = view(18192, 2, 6)
        ap_ = view(18208, 2, 3, TOK)
        qgain = view(19840, 1)
        apT = view(8704, 2, 3, 3, P)
        ay = view(4352, 8, TOK)
        dqkv = view(0, 24, TOK)
        dog = view(6528, 8, TOK)
        dsq = view(8704, 16, TOK)
        dwork = view(8704, 2, TOK)
        (dER, ddec, dLT, dQK, dkb, dkd, dvb, dX, dXT, dMT, dT1, dqd, dW, dU, dST) = (
            view(8704 + 1024 * k, 8, P) for k in range(15))
        dOT = dqkv[:, 16:24, :]
        fact = view(0, 24, TOK)
        fconv = view(6528, 2, 4, TOK)
        cact = silu_c[:, :]
        one, two = slice(T0, TOK), slice(0, TOK)

        def heads4(bank, rows, cols):
            return ps[0:rows, bank, :].rearrange("p (g c) -> p g c", c=P)[:, :, 0:cols]

        def trin(n):
            return tab("tri")[0:n, TOK + META:TOK + META + n]

        block = ctx.enter_context(nc.Block())

        parts = [("ada", 96), ("ret_in", 48), ("ret_out", 16), ("query0", 16), ("u0", 128), ("v0", 128), ("sgu_in", 48),
                 ("sgu_out", 24), ("query1", 16), ("u1", 128), ("v1", 128), ("att_in", 32), ("att_out", 8), ("up0", 44),
                 ("down0", 24), ("dn_in", 32), ("dn_out", 8), ("up1", 44), ("down1", 24)]
        first, n = {}, 0
        for name, units in parts:
            first[name] = n
            n += units
        n_units = n
        stages = ["ada", "ret", "peer0", "sgu", "peer1", "final1", "att", "ffn0", "dn", "ffn1"]
        on = {s: until is None or stages.index(s) <= stages.index(until) for s in stages}
        last_part = {None: "down1", "ada": "ada", "ret": "ret_out", "peer0": "v0", "sgu": "sgu_out", "peer1": "v1",
                     "final1": "v1", "att": "att_out", "ffn0": "down0", "dn": "dn_out", "ffn1": "down1"}[until]

        limit = first[last_part] + dict(parts)[last_part]
        blocks_before, nb = {}, 0
        for name, units in parts:
            blocks_before[name] = nb
            if name in ("ret_in", "query0", "query1", "u0", "u1", "sgu_in", "att_in", "up0", "up1", "dn_in"):
                nb += units

        def meet(c, sem):
            c.engine.drain().then_inc(sem, 1)
            c.engine.wait_ge(sem, c.next(sem, 4))

        @block.sync
        def _(sp):
            sp.dma_start(params[:], t["params"]).then_inc(s_consts_in, 16)
            sp.dma_start(const1[:], t["const1"]).then_inc(s_consts_in, 16)
            sp.dma_start(x[:, :, T0:TOK], t["xT"]).then_inc(s_consts_in, 16)
            sp.dma_start(posn, t["positions"]).then_inc(s_consts_in, 16)

            def load(src, at):
                if not (at.b is None and at.unit < RAW):
                    sp.wait_ge(s_raw_free, at.number(1 - RAW) * 2)
                sp.dma_start(raw[:, at.raw, :, :], src).then_inc(full[at.raw], 16)

            def stream(src, base, count):
                done = 0
                if base == 0:
                    for k in range(ROUND):
                        load(src[k], At(k))
                    done = ROUND
                rounds = (count - done) // ROUND
                with sp.Fori(0, rounds) as b:
                    for k in range(ROUND):
                        load(src[b * ROUND + (done + k)], At(base + done + k, b))
                for k in range(done + rounds * ROUND, count):
                    load(src[k], At(base + k))

            for name, units in parts:
                stream(t[name], first[name], units)
                if name == last_part:
                    break
            sp.wait_ge(s_result_ready, 1)
            if until is None:
                sp.dma_start(out, x[:, :, T0:TOK]).then_inc(s_out_done, 16)
            else:
                sp.dma_start(out, x[:, :, :]).then_inc(s_out_done, 16)
            sp.wait_ge(s_out_done, 16)

        @block.gpsimd
        def _(pool):
            c = Counts(pool)
            pool.memset(ones[:], 1.0).then_inc(s_memsets, 1)
            pool.memset(zeros_b[:], 0.0).then_inc(s_memsets, 1)
            pool.memset(small[:, 0:1], EPS).then_inc(s_memsets, 1)
            pool.memset(small[:, 1:2], float(np.pi / 2)).then_inc(s_memsets, 1)
            pool.memset(small[:, 2:4], 1.0).then_inc(s_memsets, 1)
            pool.memset(x[:, :, 0:T0], 0.0).then_inc(s_memsets, 1)
            pool.engine_nop().then_inc(s_bank_free, 4)
            pool.engine_nop().then_inc(s_dn_silu, 2)
            pool.wait_ge(s_ada_row, c.next(s_ada_row, 24))
            pool.dma_start(t["scratch"], ada_row).then_inc(s_row_out, 16)
            pool.wait_ge(s_row_out, 16)
            pool.dma_start(ada_sq, t["scratch"].rearrange("a (b c) -> (a b) c", c=P)).then_inc(s_row_in, 16)
            meet(c, s_met)
            if on["ret"]:
                pool.dma_start(ret_dec, t["ret_dec"]).then_inc(s_ret_in, 16)
                meet(c, s_met)
                meet(c, s_met)
            for layer in range(2):
                if on["peer%d" % layer]:
                    meet(c, s_met)
                    pool.dma_start(keysT, t["keysT"][layer]).then_inc(s_keys_in, 16)
                    meet(c, s_met)
                if layer == 0 and on["sgu"]:
                    pool.dma_start(sws, t["w_s"]).then_inc(s_sgu_in, 16)
                    pool.wait_ge(s_sgu_in, 16)
                    pool.memset(sws[64:128, :, 0:64], 0.0).then_inc(s_memsets, 1)
                    pool.dma_start(sbs[0:1, :, :], t["b_s"]).then_inc(s_sgu_in, 16)
                    meet(c, s_met)
                    meet(c, s_met)
            if on["att"]:
                pool.dma_start(x[:, :, 0:T0], t["metaT"]).then_inc(s_tabs_in, 16)
                pool.dma_start(tabs, t["const2"]).then_inc(s_tabs_in, 16)
                pool.dma_start(awf, t["att_wf"]).then_inc(s_tabs_in, 16)
                for _ in range(3):
                    meet(c, s_met)
            if on["ffn0"]:
                pool.memset(fact[:, 22:24, :], 0.0).then_inc(s_memsets, 1)
                meet(c, s_met)
                meet(c, s_met)
            if on["dn"]:
                pool.dma_start(dwf, t["dn_wf"]).then_inc(s_tabs_in, 16)
                for _ in range(3):
                    meet(c, s_met)
            if on["ffn1"]:
                pool.memset(fact[:, 22:24, :], 0.0).then_inc(s_memsets, 1)
                meet(c, s_met)
                meet(c, s_met)

        @block.tensor
        def _(pe):
            c = Counts(pe)
            mm, tr = nc.tensor.matmul, nc.tensor.transpose

            def unit(at, dst, moving, opened=False):
                for half in range(2):
                    pe.wait_ge(s_raw_free, at.halves(2 * ADA_UNITS + half + 1))
                    for q in range(4):
                        k, slot = 4 * half + q, at.slot(half)
                        hi, lo = moving(k)
                        begin, end = opened is False and k == 0, opened or k == KT - 1
                        mm(dst(k), w_lo[:, slot, q, :], hi, start=begin, stop=opened, skip_group_check=opened)
                        mm(dst(k), w_hi[:, slot, q, :], lo, start=False, stop=opened, skip_group_check=opened)
                        last = mm(dst(k), w_hi[:, slot, q, :], hi, start=False, stop=end, skip_group_check=opened)
                    last.then_inc(s_half_used, 1)

            def project(name, cols, count=None):
                base, count = first[name], count or dict(parts)[name]
                rounds = count // ROUND
                width = cols.stop - cols.start

                def one_unit(j, b=None):
                    pe.wait_ge(s_bank_free, c.next(s_bank_free))
                    unit(At(base + j, b), lambda k: ps[:, j % 4, 0:width], lambda k: (h_hi[:, k, 0:width], h_lo[:, k, 0:width]))

                with c.loop(rounds, bank_free=ROUND) as b:
                    for j in range(ROUND):
                        one_unit(j, b)
                for j in range(rounds * ROUND, count):
                    one_unit(j)

            def zero_banks(banks):
                for bank in banks:
                    for side in range(2):
                        mm(ps[:, bank, side * SEQ:side * SEQ + SEQ], zeros_b[:, :], ones[:].bitcast(bf16), start=True,
                           stop=True)

            def project_out(name, width, signal):
                base, count = first[name], dict(parts)[name]
                zero_banks(range(8))

                def round_of(r, b=None):
                    pe.wait_ge(s_h_ready, c.next(s_h_ready))
                    for m in range(8):
                        unit(At(base + r * ROUND + m, b), lambda k: ps[:, m, 0:width],
                             lambda k: (h_hi[:, k, 0:width], h_lo[:, k, 0:width]), opened=True)

                rounds = count // ROUND
                if rounds > 1:
                    with c.loop(rounds - 1, h_ready=1) as b:
                        round_of(0, b)
                round_of(rounds - 1)
                pe.drain().then_inc(signal, 1)

            def moved():
                pe.wait_ge(s_bank_free, c.n[s_bank_free.name] + 4)

            def sum_tiles(src, tiles, cols, signal=s_sums, bank=4):
                for k in range(tiles):
                    last = mm(ps[:, bank, 0:cols.stop - cols.start], ones[:], src[:, k, 0:cols.stop - cols.start], start=k == 0,
                              stop=k == tiles - 1)
                last.then_inc(signal, 1)

            def norm(cols):
                pe.wait_ge(s_squares, c.next(s_squares))
                sum_tiles(sq, KT, cols)
                pe.wait_ge(s_h_ready, c.next(s_h_ready))

            pe.wait_ge(s_memsets, c.next(s_memsets, 6))
            pe.wait_ge(s_c_act, c.next(s_c_act))
            def ada_unit(j, b=None):
                at = At(j, b)
                pe.wait_ge(full[at.raw], at.fill() * 16)
                for k in range(KT):
                    last = mm(ps[0:1, (j // 4) % 2, (j % 4) * P:(j % 4) * P + P], cact[:, k:k + 1], raw[:, at.raw, k, :],
                              start=k == 0, stop=k == KT - 1)
                last.then_inc(s_raw_free, 2)
            for j in range(8):
                ada_unit(j)
            with c.loop(11, ada_row=2) as b:
                for j in range(8):
                    if j % 4 == 0:
                        pe.wait_ge(s_ada_row, c.next(s_ada_row))
                    ada_unit(8 + j, b)
            pe.wait_ge(s_ada_row, c.next(s_ada_row, 2))
            pe.wait_ge(s_row_in, 16)
            pe.wait_ge(s_consts_in, c.next(s_consts_in, 64))
            tr(ps[:, 2, 0:96], ada_sq, ident[0:96, 0:96]).then_inc(s_ada_t, 1)
            meet(c, s_met)

            if on["ret"]:
                norm(one)
                project("ret_in", one)
                meet(c, s_met)
                for n in range(8):
                    for q in range(4):
                        m, jt = 2 * n + q // 2, q % 2
                        last = tr(ps[:, n, q * P:q * P + P], vT[:, m, jt * P:jt * P + P], ident)
                    last.then_inc(s_vt_ready, 1)
                for hd in range(RH):
                    pe.wait_ge(s_vt_copied, c.next(s_vt_copied, 2))
                for hd in range(RH):
                    for jt in range(2):
                        for k in range(2):
                            last = mm(ps[:, hd, jt * SEQ:jt * SEQ + SEQ], qk[:, 8 + 2 * hd + k, jt * P:jt * P + P],
                                      qk[:, 2 * hd + k, :], start=k == 0, stop=k == 1)
                    last.then_inc(s_scores_ready, 1)
                for hd in range(RH):
                    pe.wait_ge(s_decayed, c.next(s_decayed))
                for m in range(16):
                    hd = m // 4
                    if m >= 4:
                        pe.wait_ge(s_y_copied, c.next(s_y_copied))
                    for jt in range(2):
                        last = mm(ps[:, 4 + m % 4, 0:SEQ], vtok[:, jt, m * P:m * P + P], sT[:, hd, jt, :], start=jt == 0,
                                  stop=jt == 1)
                    last.then_inc(s_y_ready, 1)
                pe.wait_ge(s_y_copied, c.next(s_y_copied, 4))
                pe.wait_ge(s_squares, c.next(s_squares))
                for hd in range(RH):
                    for k in range(4):
                        last = mm(ps[:, hd // 2, (hd % 2) * SEQ:(hd % 2) * SEQ + SEQ], ones[:], ysq[:, 4 * hd + k, :],
                                  start=k == 0, stop=k == 3)
                last.then_inc(s_sums, 1)
                meet(c, s_met)
                project_out("ret_out", SEQ, s_acc_done)
                pe.wait_ge(s_x_ready, c.next(s_x_ready))

            def peer(layer):
                norm(one)
                meet(c, s_met)
                project(f"query{layer}", one)
                pe.wait_ge(s_keys_in, c.next(s_keys_in, 16))
                moved()
                for tt in range(2):
                    for m in range(16):
                        last = mm(ps[:, 4 * tt + m // 4, (m % 4) * P:(m % 4) * P + P], qT[:, m, tt * P:tt * P + P],
                                  keysT[:, m, :], start=True, stop=True)
                        if m % 4 == 3:
                            last.then_inc(s_key_scores, 1)
                pe.wait_ge(s_key_copied, c.next(s_key_copied, 8))
                project(f"u{layer}", one, 64)
                pe.wait_ge(s_picks_ready, c.next(s_picks_ready))
                moved()
                for n in range(3):
                    for tt in range(2):
                        last = tr(ps[:, n, tt * P:tt * P + P], picked[:, tt, n, :], ident)
                last.then_inc(s_tables_ready, 1)

                def group(bank, buf):
                    pe.wait_ge(s_picks_ready, c.next(s_picks_ready))
                    for q in range(4):
                        last = mm(ps[:, bank + buf, q * 64:q * 64 + 64], pick_j[:, buf, q, :], pick_i[:, buf, q, 0:64],
                                  start=True, stop=True)
                    last.then_inc(s_g_banks, 1)

                base = first[f"u{layer}"] + 64
                pe.wait_ge(s_chosen_ready, c.next(s_chosen_ready))
                with c.loop(8, bank_free=ROUND, picks_ready=ROUND) as b:
                    for j in range(ROUND):
                        pe.wait_ge(s_bank_free, c.next(s_bank_free))
                        unit(At(base + j, b), lambda k: ps[:, j % 4, 0:SEQ], lambda k: (h_hi[:, k, 0:SEQ], h_lo[:, k, 0:SEQ]))
                        group(4, j % 2)
                pe.wait_ge(s_g_applied, c.next(s_g_applied))
                moved()
                zero_banks(range(4, 8))
                base = first[f"v{layer}"]

                def down(at, j):
                    pe.wait_ge(s_mix_done, c.next(s_mix_done))
                    unit(at, lambda m: ps[:, 4 + m // 2, (m % 2) * SEQ:(m % 2) * SEQ + SEQ],
                         lambda m: (mixed_hi[:, j % 2, :], mixed_lo[:, j % 2, :]), opened=True)

                with c.loop(7, mix_done=ROUND, picks_ready=ROUND) as b:
                    for j in range(ROUND):
                        down(At(base + j, b), j)
                        group(0, j % 2)
                for j in range(ROUND):
                    down(At(base + 56 + j), j)
                    if j < 4:
                        group(0, 0)
                        group(0, 1)
                pe.wait_ge(s_g_applied, c.next(s_g_applied))
                with c.loop(8, mix_done=ROUND) as b:
                    for j in range(ROUND):
                        down(At(base + 64 + j, b), j)
                pe.drain().then_inc(s_acc_done, 1)
                pe.wait_ge(s_x_ready, c.next(s_x_ready))
                meet(c, s_met)

            if on["peer0"]:
                peer(0)

            if on["sgu"]:
                pe.wait_ge(s_memsets, c.next(s_memsets))
                norm(one)
                project("sgu_in", one)
                moved()
                sum_tiles(sv, ST_, slice(0, SEQ), s_mean_sum)
                pe.wait_ge(s_squares, c.next(s_squares))
                sum_tiles(ssq, ST_, slice(0, SEQ))
                pe.wait_ge(s_sgu_ready, c.next(s_sgu_ready))
                for n in range(12):
                    if n >= 4:
                        pe.wait_ge(s_vt_copied, c.next(s_vt_copied))
                    for q in range(4):
                        m, jt = 2 * n + q // 2, q % 2
                        last = tr(ps[:, n % 4, q * P:q * P + P], sv[:, m, jt * P:jt * P + P], ident)
                    last.then_inc(s_vt_ready, 1)
                pe.wait_ge(s_vt_copied, c.next(s_vt_copied, 4))
                pe.wait_ge(s_sgu_in, c.next(s_sgu_in, 32))
                for n in range(12):
                    if n >= 4:
                        pe.wait_ge(s_sgu_s, c.next(s_sgu_s))
                    for q in range(4):
                        m, jt = 2 * n + q // 2, q % 2
                        dst = ps[:, 4 + n % 4, q * P:q * P + P]
                        mm(dst, svtok[:, jt, m * P:m * P + P], sws[:, m // 3, :], start=True, stop=False)
                        last = mm(dst, ones[0:1, :], sbs[0:1, m // 3, :], start=False, stop=True)
                    last.then_inc(s_spatial_ready, 1)
                pe.wait_ge(s_sgu_s, c.next(s_sgu_s, 4))
                meet(c, s_met)
                project_out("sgu_out", SEQ, s_acc_done)
                pe.wait_ge(s_x_ready, c.next(s_x_ready))
                meet(c, s_met)

            if on["peer1"]:
                peer(1)
            if on["final1"]:
                pe.wait_ge(s_squares, c.next(s_squares))
                sum_tiles(sq, KT, one)
                pe.wait_ge(s_x_ready, c.next(s_x_ready))

            def norm_post():
                pe.wait_ge(s_fo_copied, c.next(s_fo_copied))
                sum_tiles(sq, KT, two)
                pe.wait_ge(s_x_ready, c.next(s_x_ready))

            if on["att"]:
                pe.wait_ge(s_tabs_in, c.next(s_tabs_in, 48))
                norm(two)
                project("att_in", two)
                for tt, (s, n) in enumerate(TILES):
                    for k in range(KT):
                        last = mm(ps[0:n, 5, tt * 16:tt * 16 + 16], h[:, k, s:s + n], awf[:, k, :], start=k == 0,
                                  stop=k == KT - 1)
                last.then_inc(s_scores_ready, 1)
                moved()
                pe.wait_ge(s_squares, c.next(s_squares))
                for b in range(16):
                    last = mm(ps[0:32, 6, 0:TOK], tab("colsel")[:, 32 - 2 * b:64 - 2 * b], asq[:, b, :], start=b == 0,
                              stop=b == 15)
                last.then_inc(s_sums, 1)
                pe.wait_ge(s_inv, c.next(s_inv))
                for b in range(16):
                    if b >= 4:
                        pe.wait_ge(s_scaled, c.next(s_scaled))
                    mm(ps[:, b % 4, 0:TOK], tab("rowsel", 32)[:, b * P:b * P + P], row_rstd, start=True,
                       stop=True).then_inc(s_norms, 1)
                pe.wait_ge(s_scaled, c.next(s_scaled, 4))
                for n in range(8):
                    if n >= 4:
                        pe.wait_ge(s_vt_copied, c.next(s_vt_copied))
                    for tt, (s, w) in enumerate(TILES):
                        last = tr(ps[0:w, n % 4, tt * P:tt * P + P], avT[:, n, s:s + w], ident)
                    last.then_inc(s_vt_ready, 1)
                pe.wait_ge(s_vt_copied, c.next(s_vt_copied, 4))
                pe.wait_ge(s_heads_prep, c.next(s_heads_prep))
                for tt, (s, n) in enumerate(TILES):
                    last = mm(ps[0:32, 5, 0:TOK], alf[0:n, tt, :], tab("tri")[0:n, tt * TOK:tt * TOK + TOK], start=tt == 0,
                              stop=tt == 2)
                last.then_inc(s_cum_ready, 1)
                meet(c, s_met)
                for pr in range(AH // 2):
                    for par_ in range(2):
                        lo = 64 * par_
                        pe.wait_ge(s_heads_prep, c.next(s_heads_prep))
                        for tt, (s, n) in enumerate(TILES):
                            kend = s + n
                            dst = ps[0:n, 3 * par_ + tt, 0:kend]
                            mm(dst, aqk[lo:lo + 64, pr, s:s + n], aqk[lo:lo + 64, 8 + pr, 0:kend], start=True, stop=False)
                            mm(dst, aL[0:32, par_, s:s + n], aR[0:32, par_, 0:kend], start=False,
                               stop=True).then_inc(s_att_s, 1)
                    for par_ in range(2):
                        for tt, (s, n) in enumerate(TILES):
                            pe.wait_ge(s_att_pn, c.next(s_att_pn))
                            for kt in range(tt + 1):
                                ks, kn = TILES[kt]
                                last = tr(ps[0:kn, 3 * par_ + tt, kt * P:kt * P + n], ap_[0:n, par_, tt, ks:ks + kn],
                                          ident[0:n, 0:n])
                            last.then_inc(s_att_t, 1)
                    for par_ in range(2):
                        lo = 64 * par_
                        for tt, (s, n) in enumerate(TILES):
                            pe.wait_ge(s_att_tc, c.next(s_att_tc))
                            for kt in range(tt + 1):
                                ks, kn = TILES[kt]
                                hd = 2 * pr + par_
                                last = mm(ps[lo:lo + 64, 6, s:s + n], avtok[0:kn, kt, hd * 64:hd * 64 + 64],
                                          apT[0:kn, par_, tt, kt, 0:n], start=kt == 0, stop=kt == tt)
                    last.then_inc(s_att_o, 1)
                    pe.wait_ge(s_att_od, c.next(s_att_od))
                meet(c, s_met)
                project_out("att_out", TOK, s_out_ready)
                norm_post()
                meet(c, s_met)

            def ffn(n):
                norm(two)
                project(f"up{n}", two)
                pe.wait_ge(s_memsets, c.next(s_memsets))
                meet(c, s_met)
                project_out(f"down{n}", TOK, s_out_ready)
                norm_post()
                meet(c, s_met)

            if on["ffn0"]:
                ffn(0)

            if on["dn"]:
                pe.wait_ge(s_tabs_in, c.next(s_tabs_in, 16))
                norm(two)
                project("dn_in", two)
                for tt, (s, n) in enumerate(TILES):
                    for k in range(KT):
                        last = mm(ps[0:n, 5, tt * 16:tt * 16 + 16], h[:, k, s:s + n], dwf[:, k, :], start=k == 0,
                                  stop=k == KT - 1)
                last.then_inc(s_scores_ready, 1)
                moved()
                pe.wait_ge(s_squares, c.next(s_squares))
                for b in range(16):
                    last = mm(ps[0:16, 6, 0:TOK], tab("colsel1")[:, 16 - b:32 - b], dsq[:, b, :], start=b == 0, stop=b == 15)
                last.then_inc(s_sums, 1)
                pe.wait_ge(s_inv, c.next(s_inv))
                for b in range(16):
                    if b >= 4:
                        pe.wait_ge(s_scaled, c.next(s_scaled))
                    mm(ps[:, b % 4, 0:TOK], tab("rowsel1", 16)[:, b * P:b * P + P], row_rstd[0:16, :], start=True,
                       stop=True).then_inc(s_norms, 1)
                pe.wait_ge(s_scaled, c.next(s_scaled, 4))
                meet(c, s_met)
                for ch, (s, n) in enumerate(TILES):
                    tri_n = trin(n)
                    levels = n.bit_length() - 1
                    col = lambda hd, w: slice((hd % 4) * P, (hd % 4) * P + w)
                    mm(ps[0:n, 2, 0:8], tri_n, dsm[0:n, ch, 2, 0:8], start=True, stop=True)
                    for g in range(2):
                        for hd in range(4 * g, 4 * g + 4):
                            mm(ps[:, g, col(hd, n)], dsm[0:n, ch, 2, hd:hd + 1].to_broadcast([n, P]), tri_n, start=True,
                               stop=True)
                            mm(ps[0:n, 4 + g, col(hd, n)], dqkv[:, 8 + hd, s:s + n], dqkv[:, 8 + hd, s:s + n],
                               start=True, stop=True)
                            last = mm(ps[0:n, 6 + g, col(hd, n)], dqkv[:, 8 + hd, s:s + n], dqkv[:, hd, s:s + n],
                                      start=True, stop=True)
                        last.then_inc(s_dn_p, 1)
                    for g in range(2):
                        pe.wait_ge(s_dn_v, c.next(s_dn_v))
                        for hd in range(4 * g, 4 * g + 4):
                            tr(ps[0:n, g, col(hd, P)], dqkv[:, 8 + hd, s:s + n], ident)
                            last = tr(ps[0:n, 2 + g, col(hd, P)], dqkv[:, 16 + hd, s:s + n], ident)
                        last.then_inc(s_dn_p, 1)
                    for lv in range(levels):
                        for g in range(2):
                            pe.wait_ge(s_dn_v, c.next(s_dn_v))
                            for hd in range(4 * g, 4 * g + 4):
                                last = mm(ps[0:n, g, col(hd, n)], dMT[0:n, hd, 0:n], dX[0:n, hd, 0:n], start=True, stop=True)
                            last.then_inc(s_dn_p, 1)
                        for g in range(2):
                            pe.wait_ge(s_dn_v, c.next(s_dn_v))
                            for hd in range(4 * g, 4 * g + 4):
                                mm(ps[0:n, 2 + g, col(hd, n)], dXT[0:n, hd, 0:n], dT1[0:n, hd, 0:n], start=True, stop=True)
                                last = mm(ps[0:n, 4 + g, col(hd, n)], dT1[0:n, hd, 0:n], dXT[0:n, hd, 0:n], start=True,
                                          stop=True)
                            last.then_inc(s_dn_p, 1)
                    for g in range(2):
                        pe.wait_ge(s_dn_v, c.next(s_dn_v))
                        for hd in range(4 * g, 4 * g + 4):
                            last = mm(ps[:, g, col(hd, n)], dkb[0:n, hd, :], dXT[0:n, hd, 0:n], start=True, stop=True)
                        last.then_inc(s_dn_p, 1)
                    for g in range(2):
                        pe.wait_ge(s_dn_v, c.next(s_dn_v))
                        for hd in range(4 * g, 4 * g + 4):
                            dst = ps[0:n, 2 + g, col(hd, P)]
                            mm(dst, dXT[0:n, hd, 0:n], dvb[0:n, hd, :], start=True, stop=False)
                            last = mm(dst, dW[:, hd, 0:n], dST[:, hd, :], start=False, stop=True)
                        last.then_inc(s_dn_p, 1)
                    for g in range(2):
                        pe.wait_ge(s_dn_v, c.next(s_dn_v))
                        for hd in range(4 * g, 4 * g + 4):
                            dst = ps[:, 4 + g, col(hd, n)]
                            mm(dst, dST[:, hd, :], dqd[:, hd, 0:n], start=True, stop=False)
                            mm(dst, dU[0:n, hd, :], dQK[0:n, hd, 0:n], start=False, stop=True)
                            last = mm(ps[:, 6 + g, col(hd, P)], dkd[0:n, hd, :], dU[0:n, hd, :], start=True, stop=True)
                        last.then_inc(s_dn_p, 1)
                    pe.wait_ge(s_dn_v, c.next(s_dn_v, 2))
                pe.wait_ge(s_squares, c.next(s_squares))
                for b in range(8):
                    last = mm(ps[0:16, 6, 0:TOK], tab("colsel1")[:, 16 - b:32 - b], dsq[:, b, :], start=b == 0, stop=b == 7)
                last.then_inc(s_sums, 1)
                pe.wait_ge(s_inv, c.next(s_inv))
                for b in range(8):
                    if b >= 4:
                        pe.wait_ge(s_scaled, c.next(s_scaled))
                    mm(ps[:, b % 4, 0:TOK], tab("rowsel1", 16)[:, b * P:b * P + P], row_rstd[0:16, :], start=True,
                       stop=True).then_inc(s_norms, 1)
                pe.wait_ge(s_scaled, c.next(s_scaled, 4))
                meet(c, s_met)
                project_out("dn_out", TOK, s_out_ready)
                norm_post()
                meet(c, s_met)
            if on["ffn1"]:
                ffn(1)

        @block.scalar
        def _(act):
            c = Counts(act, s_act_own)
            A = nc.scalar.activation

            def split(at):
                if at.b is None and at.unit >= limit:
                    return
                act.wait_ge(full[at.raw], at.fill() * 16)
                for half in range(2):
                    if not (at.b is None and at.unit < ADA_UNITS + 2):
                        act.wait_ge(s_half_used, at.halves(half - 3))
                    A(w_hi[:, at.slot(half)], raw[:, at.raw, 4 * half:4 * half + 4, :], ACT.Copy).then_inc(s_hi_ready, 1)

            def take(name, skip, rounds, dst, func, bias=None):
                with c.loop(rounds) as b:
                    for j in range(ROUND):
                        at = At(first[name] + skip + j, b)
                        split(at.plus(2))
                        act.wait_ge(s_half_used, at.halves(2))
                        width = dst(0).shape[-1]
                        extra = {} if bias is None else {"bias": bias(b * ROUND + j)}
                        A(dst(b * ROUND + j), ps[:, j % 4, 0:width], func, **extra).then_inc(s_bank_free, 1)

            def feed(name, src, width):
                base, rounds = first[name], dict(parts)[name] // ROUND

                def round_of(r, b=None):
                    if not (b is None and r == 0):
                        act.wait_ge(s_half_used, At(base + r * ROUND, b).halves(0))
                    for k in range(KT):
                        A(h_hi[:, k, 0:width], src[:, (r * KT + k) if b is None else b * KT + (r * KT + k), 0:width],
                          ACT.Copy).then_inc(s_act_hi, 1)
                    for m in range(ROUND):
                        split(At(base + r * ROUND + m + 2, b))

                round_of(0)
                if rounds > 2:
                    with c.loop(rounds - 2) as b:
                        round_of(1, b)
                if rounds > 1:
                    round_of(rounds - 1)

            def norm_sums(scale=1.0 / D, src=None, dst=None):
                act.wait_ge(s_sums, c.next(s_sums))
                src = ps[:, 4, 0:SEQ] if src is None else src
                dst = rstd[:, 0:SEQ] if dst is None else dst
                A(dst, src, ACT.Sqrt, bias=eps[0:dst.shape[0], :], scale=scale).then_inc(s_root, 1)

            def norm_one(layer, which):
                A(sq[:, :, 0:SEQ], x[:, :, one], ACT.Square).then_inc(s_squares, 1)
                norm_sums()
                for k in range(KT):
                    act.wait_ge(s_h_scaled, c.next(s_h_scaled))
                    at = layer * 48 + (0 if which == 0 else 24) + k
                    A(h_hi[:, k, 0:SEQ], h[:, k, 0:SEQ], ACT.Identity, bias=mods[:, at:at + 1])
                    A(h[:, k, 0:SEQ], h[:, k, 0:SEQ], ACT.Identity, bias=mods[:, at:at + 1]).then_inc(s_act_hi, 1)

            def norm_two():
                A(sq[:, :, :], x[:, :, :], ACT.Square).then_inc(s_squares, 1)
                norm_sums(src=ps[:, 4, 0:TOK], dst=rstd[:, :])
                for k in range(KT):
                    act.wait_ge(s_h_whole, c.next(s_h_whole))
                    A(h_hi[:, k, :], h[:, k, :], ACT.Copy).then_inc(s_act_hi, 1)

            def norm_post():
                act.wait_ge(s_out_ready, c.next(s_out_ready))
                A(fo, ps[:, :, 0:TOK], ACT.Copy)
                A(sq, ps[:, :, 0:TOK], ACT.Square).then_inc(s_fo_copied, 1)
                norm_sums(src=ps[:, 4, 0:TOK], dst=rstd[:, :])
                act.wait_ge(s_x_ready, c.next(s_x_ready))
                meet(c, s_met)

            act.wait_ge(s_consts_in, c.next(s_consts_in, 64))
            act.wait_ge(s_memsets, c.next(s_memsets, 6))
            A(cact, par("c", 0, 8), ACT.Silu).then_inc(s_c_act, 1)
            act.wait_ge(s_rope_args, c.next(s_rope_args))
            A(sinT, rope[:, 4, :], ACT.Sin)
            A(cosT, rope[:, 5, :], ACT.Sin, bias=half_pi, scale=-1.0).then_inc(s_rope_ready, 1)
            with c.loop(12, raw_free=16) as b:
                for j in range(2):
                    act.wait_ge(s_raw_free, c.next(s_raw_free, 8))
                    A(ada_row.rearrange("p (s n) -> p s n", n=BANK)[:, b * 2 + j, :], ps[0:1, j, :],
                      ACT.Copy).then_inc(s_ada_row, 1)
            split(At(ADA_UNITS))
            split(At(ADA_UNITS + 1))
            meet(c, s_met)

            if on["ret"]:
                norm_one(0, 0)
                take("ret_in", 0, 2, lambda m: qk[:, m, :], ACT.Copy)
                take("ret_in", 16, 2, lambda m: vT[:, m, :], ACT.Copy)
                take("ret_in", 32, 2, lambda m: gT[:, m, :], ACT.Silu)
                meet(c, s_met)
                for n in range(8):
                    act.wait_ge(s_vt_ready, c.next(s_vt_ready))
                    A(vtok.rearrange("p j (m f) -> p m j f", f=P)[:, 2 * n:2 * n + 2],
                      ps[:, n, :].rearrange("p (m j f) -> p m j f", m=2, j=2), ACT.Copy).then_inc(s_vt_copied, 1)
                for m in range(16):
                    act.wait_ge(s_y_ready, c.next(s_y_ready))
                    A(yT[:, m, :], ps[:, 4 + m % 4, 0:SEQ], ACT.Copy).then_inc(s_y_copied, 1)
                act.wait_ge(s_y_copied, c.next(s_y_copied, 16))
                A(ysq, yT, ACT.Square).then_inc(s_squares, 1)
                norm_sums(1.0 / RDV, ps[:, 0:2, :], yrs.rearrange("p (a b) t -> p a (b t)", a=2))
                meet(c, s_met)
                feed("ret_out", yT, SEQ)
                act.wait_ge(s_x_ready, c.next(s_x_ready))

            def peer(layer):
                norm_one(layer, 1)
                meet(c, s_met)
                take(f"query{layer}", 0, 2, lambda m: qT[:, m, :], ACT.Copy)
                for n in range(8):
                    act.wait_ge(s_key_scores, c.next(s_key_scores))
                    A(sc[:, n // 4, (n % 4) * 4:(n % 4) * 4 + 4, :], ps[:, n, :].rearrange("p (m f) -> p m f", f=P),
                      ACT.Copy).then_inc(s_key_copied, 1)
                take(f"u{layer}", 0, 8, lambda m: G[:, m, :], ACT.Gelu_apprx_tanh)
                act.wait_ge(s_gate_in, c.next(s_gate_in))
                A(picked[:, :, 2, :], picked[:, :, 2, :], ACT.Exp).then_inc(s_gate_exp, 1)
                act.wait_ge(s_tables_ready, c.next(s_tables_ready))
                A(chosen[:], ps[:, 0:3, 0:SEQ], ACT.Copy).then_inc(s_chosen_ready, 1)
                take(f"u{layer}", 64, 8, lambda m: G[:, 64 + m, :] if isinstance(m, int) else G[:, m + 64, :],
                     ACT.Gelu_apprx_tanh)
                base = first[f"v{layer}"]

                def mix(at, i, j):
                    if at is not None:
                        act.wait_ge(s_half_used, at.halves(2))
                    A(mixed_hi[:, j % 2, :], G[:, i, :], ACT.Copy).then_inc(s_act_hi, 1)

                act.wait_ge(s_g_applied, c.next(s_g_applied))
                mix(None, 0, 0)
                mix(None, 1, 1)
                with c.loop(7) as b:
                    for j in range(ROUND):
                        at = At(base + j, b)
                        split(at.plus(2))
                        mix(at, b * ROUND + (j + 2), j)
                for i in range(56, 64):
                    split(At(base + i + 2))
                    if i == 62:
                        act.wait_ge(s_g_applied, c.next(s_g_applied))
                    mix(At(base + i), i + 2, i)
                with c.loop(7) as b:
                    for j in range(ROUND):
                        at = At(base + 64 + j, b)
                        split(at.plus(2))
                        mix(at, b * ROUND + (j + 66), j)
                for i in range(120, 128):
                    split(At(base + i + 2))
                    if i < 126:
                        mix(At(base + i), i + 2, i)
                act.wait_ge(s_x_ready, c.next(s_x_ready))
                meet(c, s_met)

            if on["peer0"]:
                peer(0)

            if on["sgu"]:
                norm_one(1, 0)
                take("sgu_in", 0, 6, lambda m: view(0, 48, SEQ)[:, m, :], ACT.Gelu_apprx_tanh, bias=lambda m: par("sgu_b_in", 0, 48)[:, m:m + 1]
                     if isinstance(m, int) else par("sgu_b_in", 0, 48).unsqueeze(2)[:, m, :])
                act.wait_ge(s_sgu_centred, c.next(s_sgu_centred))
                A(ssq, sv, ACT.Square).then_inc(s_squares, 1)
                norm_sums(1.0 / SH, ps[:, 4, 0:SEQ], srstd)
                for n in range(12):
                    act.wait_ge(s_vt_ready, c.next(s_vt_ready))
                    A(svtok.rearrange("p j (m f) -> p m j f", f=P)[:, 2 * n:2 * n + 2],
                      ps[:, n % 4, :].rearrange("p (m j f) -> p m j f", m=2, j=2), ACT.Copy).then_inc(s_vt_copied, 1)
                meet(c, s_met)
                feed("sgu_out", uT, SEQ)
                act.wait_ge(s_x_ready, c.next(s_x_ready))
                meet(c, s_met)

            if on["peer1"]:
                peer(1)
            if on["final1"]:
                A(sq[:, :, 0:SEQ], x[:, :, one], ACT.Square).then_inc(s_squares, 1)
                norm_sums()
                act.wait_ge(s_x_ready, c.next(s_x_ready))

            if on["att"]:
                act.wait_ge(s_tabs_in, c.next(s_tabs_in, 48))
                norm_two()
                take("att_in", 0, 3, lambda m: aqkv[:, m, :], ACT.Copy)
                take("att_in", 24, 1, lambda m: aog[:, m, :], ACT.Sigmoid)
                act.wait_ge(s_bank_free, 4 + blocks_before["att_in"] + 32)
                A(asq, aqk, ACT.Square).then_inc(s_squares, 1)
                norm_sums(1.0 / ADH, ps[0:32, 6, 0:TOK], row_rstd)
                for n in range(8):
                    act.wait_ge(s_vt_ready, c.next(s_vt_ready))
                    A(avtok[0:META, 0, n * P:n * P + P], ps[0:META, n % 4, 0:P], ACT.Copy)
                    A(avtok[:, 1:3, n * P:n * P + P], ps[:, n % 4, P:3 * P].rearrange("p (a f) -> p a f", a=2),
                      ACT.Copy).then_inc(s_vt_copied, 1)
                act.wait_ge(s_logit_in, c.next(s_logit_in))
                c.link(A(awork[:, 1], awork[:, 1], ACT.Exp))
                A(awork[:, 1], awork[:, 1], ACT.Ln, bias=1.0).then_inc(s_logit_exp, 1)
                meet(c, s_met)
                for pr in range(AH // 2):
                    for par_ in range(2):
                        for tt, (s, n) in enumerate(TILES):
                            k = 3 * par_ + tt
                            act.wait_ge(s_att_m, c.next(s_att_m))
                            A(ap_[0:n, par_, tt, 0:s + n], ps[0:n, k, 0:s + n], ACT.Exp, bias=asm[0:n, 0, k:k + 1],
                              accum_out=asm[0:n, 1, k:k + 1]).then_inc(s_att_p, 1)
                    for par_ in range(2):
                        for tt, (s, n) in enumerate(TILES):
                            k = 3 * par_ + tt
                            act.wait_ge(s_att_t, c.next(s_att_t))
                            last = A(apT[0:META, par_, tt, 0, 0:n], ps[0:META, k, 0:n], ACT.Copy)
                            if tt:
                                last = A(apT[:, par_, tt, 1:tt + 1, 0:n],
                                         ps[:, k, P:P * (tt + 1)].rearrange("p (a f) -> p a f", f=P), ACT.Copy)
                            last.then_inc(s_att_tc, 1)
                meet(c, s_met)
                feed("att_out", ay, TOK)
                norm_post()

            def ffn(n):
                norm_two()
                c.n[s_bank_free.name] = 4 + blocks_before[f"up{n}"]
                w3 = par("ffn_conv", n * 132, 132).rearrange("p (b w) -> p b w", w=3)
                with c.loop(11, bank_free=4) as b:
                    for j in range(4):
                        at = At(first[f"up{n}"] + j, b, 4)
                        split(at.plus(2))
                        act.wait_ge(s_half_used, at.halves(2))
                        A(fconv[:, 0, j, :], ps[:, j, 0:TOK], ACT.Copy, scale=w3[:, b * 4 + j, 2:3]).then_inc(s_tap_done, 1)
                        if j % 2:
                            act.wait_ge(s_bank_free, c.next(s_bank_free))
                            A(fconv[:, 1, j - 1, :], fconv[:, 0, j - 1, :], ACT.Gelu_apprx_tanh).then_inc(s_ffn_gelu, 1)
                            act.wait_ge(s_bank_free, c.next(s_bank_free))
                meet(c, s_met)
                feed(f"down{n}", fact, TOK)
                norm_post()

            if on["ffn0"]:
                ffn(0)

            if on["dn"]:
                norm_two()
                c.n[s_bank_free.name] = 4 + blocks_before["dn_in"]
                with c.loop(3, bank_free=8) as b:
                    for j in range(8):
                        split(At(first["dn_in"] + j + 2, b))
                        act.wait_ge(s_bank_free, c.next(s_bank_free))
                        A(dqkv[:, b * 8 + j, :], dwork[:, j % 2, :], ACT.Silu).then_inc(s_dn_silu, 1)
                take("dn_in", 24, 1, lambda m: dog[:, m, :], ACT.Silu)
                act.wait_ge(s_dn_silu, 2 + 24)
                A(dsq, dqkv[:, 0:16, :], ACT.Square).then_inc(s_squares, 1)
                norm_sums(1.0, ps[0:16, 6, 0:TOK], row_rstd[0:16, :])
                act.wait_ge(s_logit_in, c.next(s_logit_in))
                A(dsm[:, :, 0, 0:8], dsm[:, :, 0, 0:8], ACT.Sigmoid)
                c.link(A(dsm[:, :, 5, 0:8], dsm[:, :, 5, 0:8], ACT.Exp))
                A(dsm[:, 0, 4, 8:16], par("a_log", 0, 8), ACT.Exp)
                A(dsm[:, :, 5, 0:8], dsm[:, :, 5, 0:8], ACT.Ln, bias=1.0).then_inc(s_logit_exp, 1)
                meet(c, s_met)
                for ch, (s, n) in enumerate(TILES):
                    act.wait_ge(s_logit_in, c.next(s_logit_in))
                    A(dsm[0:n, ch, 4, 0:8], dsm[0:n, ch, 3, 0:8], ACT.Exp)
                    for g in range(2):
                        if g:
                            act.wait_ge(s_logit_in, c.next(s_logit_in))
                        here = slice(4 * g, 4 * g + 4)
                        A(ddec[0:n, here, 0:n], ddec[0:n, here, 0:n], ACT.Exp)
                        A(dER[:, here, 0:n], heads4(g, P, n), ACT.Exp).then_inc(s_logit_exp, 1)
                act.wait_ge(s_dn_v, sum(2 * (5 + 2 * (n.bit_length() - 1)) for _, n in TILES))
                A(dsq[:, 0:8, :], dOT, ACT.Square).then_inc(s_squares, 1)
                norm_sums(1.0 / P, ps[0:16, 6, 0:TOK], row_rstd[0:16, :])
                meet(c, s_met)
                feed("dn_out", dOT, TOK)
                norm_post()
            if on["ffn1"]:
                ffn(1)

        @block.vector
        def _(v):
            c = Counts(v, s_dve_own)
            V = nc.vector
            TT, TS, STT = V.tensor_tensor, V.tensor_scalar, V.scalar_tensor_tensor

            def split(at):
                if at.b is None and at.unit >= limit:
                    return
                for half in range(2):
                    v.wait_ge(s_hi_ready, at.halves(half + 1))
                    TT(w_lo[:, at.slot(half)], raw[:, at.raw, 4 * half:4 * half + 4, :],
                       w_hi[:, at.slot(half)].bitcast(f32), SUB).then_inc(s_raw_free, 1)

            def split_all(name, skip=0, count=None):
                base = first[name] + skip
                rounds = (count or dict(parts)[name]) // ROUND
                last = base + rounds * ROUND == limit
                if rounds - last > 0:
                    with v.Fori(0, rounds - last) as b:
                        for j in range(ROUND):
                            split(At(base + j + 2, b))
                if last:
                    for j in range(ROUND):
                        split(At(base + (rounds - 1) * ROUND + j + 2))

            def low_h(width):
                for k in range(KT):
                    v.wait_ge(s_act_hi, c.next(s_act_hi))
                    last = TT(h_lo[:, k, 0:width], h[:, k, 0:width], h_hi[:, k, 0:width].bitcast(f32), SUB)
                last.then_inc(s_h_ready, 1)

            def feed(name, src, width):
                base, rounds = first[name], dict(parts)[name] // ROUND

                def round_of(r, b=None):
                    for k in range(KT):
                        v.wait_ge(s_act_hi, c.next(s_act_hi))
                        last = TT(h_lo[:, k, 0:width], src[:, (r * KT + k) if b is None else b * KT + (r * KT + k), 0:width],
                                  h_hi[:, k, 0:width].bitcast(f32), SUB)
                    last.then_inc(s_h_ready, 1)
                    for m in range(ROUND):
                        split(At(base + r * ROUND + m + 2, b))

                round_of(0)
                if rounds > 2:
                    with c.loop(rounds - 2, act_hi=KT) as b:
                        round_of(1, b)
                if rounds > 1:
                    round_of(rounds - 1)

            def inverse_root(dst):
                v.wait_ge(s_root, c.next(s_root))
                return V.reciprocal(dst, dst)

            def norm_one(n):
                c.link(inverse_root(rstd[:, 0:SEQ]))
                for k in range(KT):
                    STT(h[:, k, 0:SEQ], x[:, k, one], gains[:, n, k:k + 1], rstd[:, 0:SEQ], MUL, MUL).then_inc(s_h_scaled, 1)
                low_h(SEQ)

            def norm_two(gain):
                c.link(inverse_root(rstd[:, :]))
                for k in range(KT):
                    STT(h[:, k, :], x[:, k, :], gain[:, k:k + 1], rstd[:, :], MUL, MUL).then_inc(s_h_whole, 1)
                low_h(TOK)

            def add_gated(src, gate):
                v.wait_ge(s_acc_done, c.next(s_acc_done))
                for k in range(KT):
                    last = STT(x[:, k, one], src(k), mods[:, gate + k:gate + k + 1], x[:, k, one], MUL, ADD)
                last.then_inc(s_x_ready, 1)
                v.wait_ge(s_x_ready, c.next(s_x_ready))

            def norm_post(gain):
                c.link(inverse_root(rstd[:, :]))
                for k in range(KT):
                    last = STT(fo[:, k, :], fo[:, k, :], gain[:, k:k + 1], rstd[:, :], MUL, MUL)
                c.link(last)
                TT(x[:, :, :], x[:, :, :], fo, ADD).then_inc(s_x_ready, 1)
                v.wait_ge(s_x_ready, c.next(s_x_ready))
                meet(c, s_met)

            v.wait_ge(s_consts_in, c.next(s_consts_in, 64))
            v.wait_ge(s_memsets, c.next(s_memsets, 6))
            c.link(V.tensor_copy(rope[:, 0, :], posn))
            c.link(TS(rope[:, 1, :], rope[:, 0, :], inv_freq, None, MUL))
            c.link(TS(rope[:, 2, :], rope[:, 1, :], float(0.5 / np.pi), 12582912.0, MUL, ADD))
            c.link(TS(rope[:, 2, :], rope[:, 2, :], -12582912.0, None, ADD))
            for k, piece in enumerate(TWO_PI_PARTS):
                c.link(STT(rope[:, 1, :], rope[:, 2, :], -piece, rope[:, 1, :], MUL, ADD))
            c.link(TS(rope[:, 4, :], rope[:, 1, :], -3.1415925, 3.1415925, ALU.max, ALU.min))
            STT(rope[:, 5, :], rope[:, 4, :], -1.0, rope[:, 4, :], MUL, ALU.max).then_inc(s_rope_args, 1)
            v.wait_ge(s_ada_t, c.next(s_ada_t))
            c.link(TT(mods[:], ps[:, 2, 0:96], par("ada_b", 0, 96), ADD))
            for n in range(4):
                layer, which = n // 2, n % 2
                at = layer * 48 + 8 + 24 * which
                gain = par("norm_ffn" if which else "norm_mix", layer * 8, 8)
                STT(gains[:, n, :], mods[:, at:at + 8], 1.0, gain, ADD, MUL)
            split(At(ADA_UNITS))
            split(At(ADA_UNITS + 1))
            meet(c, s_met)

            if on["ret"]:
                norm_one(0)
                split_all("ret_in")
                v.wait_ge(s_rope_ready, c.next(s_rope_ready))
                v.wait_ge(s_bank_free, 4 + blocks_before["ret_in"] + 16)
                pair = qk.rearrange("p (m two) t -> p m two t", two=2)
                x1, x2 = pair[:, :, 0, :], pair[:, :, 1, :]
                cosb, sinb = bc(cosT, 1, [P, 8, SEQ]), bc(sinT, 1, [P, 8, SEQ])
                prod = [ropet[:, k, :].rearrange("p (m t) -> p m t", m=8) for k in range(4)]
                TT(prod[0], x1, cosb, MUL)
                TT(prod[1], x2, sinb, MUL)
                TT(prod[2], x1, sinb, MUL)
                c.link(TT(prod[3], x2, cosb, MUL))
                TT(x1, prod[0], prod[1], SUB)
                TT(x2, prod[2], prod[3], ADD)
                meet(c, s_met)
                v.wait_ge(s_ret_in, c.next(s_ret_in, 16))
                for hd in range(RH):
                    v.wait_ge(s_scores_ready, c.next(s_scores_ready))
                    TT(sT[:, hd], ps[:, hd, :].rearrange("p (j t) -> p j t", j=2), ret_dec[:, :, hd, :],
                       MUL).then_inc(s_decayed, 1)
                c.link(inverse_root(yrs))
                yv = yT.rearrange("p (g b) t -> p g b t", g=RH)
                c.link(TT(yv, yv, bc(yrs, 2, [P, RH, 4, SEQ]), MUL))
                TT(yT, yT, gT, MUL)
                meet(c, s_met)
                feed("ret_out", yT, SEQ)
                add_gated(lambda k: ps[:, k, 0:SEQ], 16)

            def top16(src, rest, vals, idx, rows, ahead):
                for r in rows:
                    last = V.max(vals(r)[:, 0:8], src(r))
                    if r != rows[-1]:
                        ahead(r)
                c.link(last)
                for r in rows:
                    V.max_index(idx(r)[:, 0:8], vals(r)[:, 0:8], src(r))
                    last = V.match_replace(rest(r), vals(r)[:, 0:8], src(r), -3e38)
                    if r != rows[-1]:
                        ahead(r)
                c.link(last)
                for r in rows:
                    last = V.max(vals(r)[:, 8:16], rest(r))
                    if r != rows[-1]:
                        ahead(r)
                c.link(last)
                for r in rows:
                    last = V.max_index(idx(r)[:, 8:16], vals(r)[:, 8:16], rest(r))
                    if r != rows[-1]:
                        ahead(r)
                c.link(last)

            def peer(layer):
                norm_one(2 * layer + 1)
                meet(c, s_met)
                split_all(f"query{layer}")
                base = first[f"u{layer}"]
                split_next = [0]

                def ahead(every, r):
                    if r % every == 0 and split_next[0] < 64:
                        split(At(base + split_next[0] + 2))
                        split_next[0] += 1

                v.wait_ge(s_key_copied, c.next(s_key_copied, 8))
                for tt in range(2):
                    top16(lambda m: sc[:, tt, m, :], lambda m: sc2[:, m, :], lambda m: tv[:, tt, m, :],
                          lambda m: ti[:, tt, m, :], range(16), lambda r: ahead(4, r))
                    V.tensor_copy(tif[:, tt], ti[:, tt])
                    first_k = tv[:, tt].rearrange("p (g two) k -> p g two k", two=2)
                    c.link(TT(cand.rearrange("p g (a b) -> p g a b", a=TOPK),
                              first_k[:, :, 0, :].unsqueeze(3).to_broadcast([P, HH, TOPK, TOPK]),
                              first_k[:, :, 1, :].unsqueeze(2).to_broadcast([P, HH, TOPK, TOPK]), ADD))
                    ahead(1, 0)
                    top16(lambda g: cand[:, g, :], lambda g: cand2[:, g, :], lambda g: bv[:, tt, g, :],
                          lambda g: bp[:, tt, g, :], range(HH), lambda r: ahead(4, r))
                    flat = bp[:, tt].rearrange("p g k -> p (g k)")
                    TS(bq[:, tt, 0, :], flat, 4, None, ALU.logical_shift_right)
                    c.link(TS(bq[:, tt, 1, :], flat, 15, None, ALU.bitwise_and))
                    c.link(V.tensor_copy(bqf[:, tt], bq[:, tt]))
                    for n in range(2):
                        ahead(1, 0)
                        hot = cand2.rearrange("p g (k a) -> p (g k) a", a=TOPK)
                        c.link(TT(hot, bqf[:, tt, n, :].unsqueeze(2).to_broadcast([P, P, TOPK]),
                                  bc(iota[:, 0:TOPK], 1, [P, P, TOPK]), ALU.is_equal))
                        ahead(1, 0)
                        hot4 = cand2.rearrange("p g (k a) -> p g k a", a=TOPK)
                        index = tif[:, tt].rearrange("p (g two) a -> p g two a", two=2)[:, :, n, :]
                        c.link(TT(hot4, hot4, index.unsqueeze(2).to_broadcast([P, HH, TOPK, TOPK]), MUL))
                        ahead(1, 0)
                        c.link(V.tensor_reduce(picked[:, tt, n, :], hot, op=ADD, axis=AX))
                    last = TT(picked[:, tt, 2, :].rearrange("p (g k) -> p g k", k=TOPK), bv[:, tt],
                              bv[:, tt, :, 0:1].to_broadcast([P, HH, TOPK]), SUB)
                last.then_inc(s_gate_in, 1)
                while split_next[0] < 64:
                    ahead(1, 0)
                v.wait_ge(s_gate_exp, c.next(s_gate_exp))
                gates = picked[:, :, 2, :].rearrange("p t (g k) -> p t g k", k=TOPK)
                c.link(V.tensor_reduce(gsum, gates, op=ADD, axis=AX))
                c.link(V.reciprocal(gsum, gsum))
                TT(gates, gates, gsum.unsqueeze(3).to_broadcast([P, 2, HH, TOPK]), MUL).then_inc(s_picks_ready, 1)
                v.wait_ge(s_chosen_ready, c.next(s_chosen_ready))

                by4 = [chosen[:, n, :].rearrange("p (g t) -> p g t", t=4) for n in range(3)]
                by_token = G.rearrange("p i (g t) -> p g t i", t=4)

                def picks(g, buf, half):
                    TT(pick_j[:, buf], bc(iota, 1, [P, 4, P]), by4[1][:, g, :].unsqueeze(2).to_broadcast([P, 4, P]),
                       ALU.is_equal)
                    for q in range(4):
                        last = TS(pick_i[:, buf, q, 0:64], iota[:, 64 * half:64 * half + 64], by4[0][:, g, q:q + 1],
                                  by4[2][:, g, q:q + 1], ALU.is_equal, MUL)
                    last.then_inc(s_picks_ready, 1)

                def apply(g, bank, buf, half):
                    v.wait_ge(s_g_banks, c.next(s_g_banks))
                    here = by_token[:, g, :, 64 * half:64 * half + 64]
                    return TT(here, ps[:, bank + buf, 0:256].rearrange("p (t i) -> p t i", t=4), here, MUL)

                picks(0, 0, 0)
                with c.loop(7, g_banks=ROUND) as b:
                    for j in range(ROUND):
                        split(At(base + 64 + j + 2, b))
                        picks(b * ROUND + (j + 1), (j + 1) % 2, 0)
                        apply(b * ROUND + j, 4, j % 2, 0)
                for g in range(56, 64):
                    split(At(base + 64 + g + 2))
                    if g < 63:
                        picks(g + 1, (g + 1) % 2, 0)
                    last = apply(g, 4, g % 2, 0)
                last.then_inc(s_g_applied, 1)
                v.wait_ge(s_bank_free, 4 + blocks_before[f"u{layer}"] + 128)
                base = first[f"v{layer}"]

                def mix(i, j):
                    v.wait_ge(s_act_hi, c.next(s_act_hi))
                    TT(mixed_lo[:, j % 2, :], G[:, i, :], mixed_hi[:, j % 2, :].bitcast(f32), SUB).then_inc(s_mix_done, 1)

                picks(0, 0, 1)
                mix(0, 0)
                mix(1, 1)
                with c.loop(7, g_banks=ROUND, act_hi=ROUND) as b:
                    for j in range(ROUND):
                        split(At(base + j + 2, b))
                        mix(b * ROUND + (j + 2), j)
                        picks(b * ROUND + (j + 1), (j + 1) % 2, 1)
                        apply(b * ROUND + j, 0, j % 2, 1)
                for i in range(56, 64):
                    split(At(base + i + 2))
                    mix(i + 2, i)
                    if i < 60:
                        for g in (2 * i - 56, 2 * i - 55):
                            if g < 63:
                                picks(g + 1, (g + 1) % 2, 1)
                            last = apply(g, 0, g % 2, 1)
                    if i == 59:
                        last.then_inc(s_g_applied, 1)
                with c.loop(7, act_hi=ROUND) as b:
                    for j in range(ROUND):
                        split(At(base + 64 + j + 2, b))
                        mix(b * ROUND + (j + 66), j)
                for i in range(120, 128):
                    split(At(base + i + 2))
                    if i < 126:
                        mix(i + 2, i)
                add_gated(lambda k: ps[:, 4 + k // 2, (k % 2) * SEQ:(k % 2) * SEQ + SEQ], 48 * layer + 40)
                meet(c, s_met)

            if on["peer0"]:
                peer(0)

            if on["sgu"]:
                norm_one(2)
                split_all("sgu_in")
                v.wait_ge(s_mean_sum, c.next(s_mean_sum))
                c.link(TS(smean, ps[:, 4, 0:SEQ], 1.0 / SH, None, MUL))
                TT(sv, sv, bc(smean, 1, [P, ST_, SEQ]), SUB).then_inc(s_sgu_centred, 1)
                c.link(inverse_root(srstd))
                c.link(TT(sv, sv, bc(srstd, 1, [P, ST_, SEQ]), MUL))
                for m in range(ST_):
                    last = TS(sv[:, m, :], sv[:, m, :], par("sgu_ln_g", m), par("sgu_ln_b", m), MUL, ADD)
                last.then_inc(s_sgu_ready, 1)
                for n in range(12):
                    v.wait_ge(s_spatial_ready, c.next(s_spatial_ready))
                    TT(uT[:, 2 * n:2 * n + 2, :], ps[:, 4 + n % 4, :].rearrange("p (m t) -> p m t", m=2),
                       uT[:, 2 * n:2 * n + 2, :], MUL).then_inc(s_sgu_s, 1)
                meet(c, s_met)
                feed("sgu_out", uT, SEQ)
                add_gated(lambda k: ps[:, k, 0:SEQ], 48 + 16)
                meet(c, s_met)

            if on["peer1"]:
                peer(1)
            if on["final1"]:
                c.link(inverse_root(rstd[:, 0:SEQ]))
                for k in range(KT):
                    last = STT(x[:, k, one], x[:, k, one], par("norm_final", k), rstd[:, 0:SEQ], MUL, MUL)
                last.then_inc(s_x_ready, 1)
                v.wait_ge(s_x_ready, c.next(s_x_ready))

            if on["att"]:
                v.wait_ge(s_tabs_in, c.next(s_tabs_in, 48))
                norm_two(par("mix_pre", 0, 8))
                split_all("att_in")
                TS(qgain, par("q_gain"), ADH ** -0.5, None, MUL)
                c.link(V.memset(awork[:, 0:2], 0.0))
                v.wait_ge(s_scores_ready, c.next(s_scores_ready))
                for tt, (s, n) in enumerate(TILES):
                    last = TT(awork[0:n, 0, tt, :], ps[0:n, 5, tt * 16:tt * 16 + 16], par("b_forget", 0, 16)[0:n, :], ADD)
                c.link(last)
                STT(awork[:, 1], awork[:, 0], -1.0, awork[:, 0], MUL, ALU.min).then_inc(s_logit_in, 1)
                v.wait_ge(s_root, c.next(s_root))
                V.reciprocal(row_rstd, row_rstd).then_inc(s_inv, 1)
                for b in range(16):
                    v.wait_ge(s_norms, c.next(s_norms))
                    STT(aqk[:, b, :], aqk[:, b, :], qgain if b < 8 else par("k_gain"), ps[:, b % 4, 0:TOK], MUL,
                        MUL).then_inc(s_scaled, 1)
                v.wait_ge(s_logit_exp, c.next(s_logit_exp))
                c.link(STT(alf[:, :, 0:16], awork[:, 0], 0.0, awork[:, 1], ALU.min, SUB))
                TS(alf[:, :, 16:32], alf[:, :, 0:16], -1.0, None, MUL).then_inc(s_heads_prep, 1)
                v.wait_ge(s_cum_ready, c.next(s_cum_ready))
                V.tensor_copy(acum, ps[0:32, 5, 0:TOK])
                meet(c, s_met)
                half = tab("half", 32)
                for pr in range(AH // 2):
                    for par_ in range(2):
                        hd = 2 * pr + par_
                        TS(aL[0:32, par_, :], acum, half[:, 0:1], tab("selbot", 32)[:, hd:hd + 1], MUL, ADD)
                        TS(aR[0:32, par_, :], acum, half[:, 1:2], tab("seltop", 32)[:, hd:hd + 1], MUL,
                           ADD).then_inc(s_heads_prep, 1)
                    for par_ in range(2):
                        for tt, (s, n) in enumerate(TILES):
                            k = 3 * par_ + tt
                            v.wait_ge(s_att_s, c.next(s_att_s))
                            c.link(TT(ps[0:n, k, s:s + n], ps[0:n, k, s:s + n], tab("causal")[0:n, 0:n], ADD))
                            V.tensor_reduce(asm[0:n, 0, k:k + 1], ps[0:n, k, 0:s + n], op=ALU.max, axis=AX,
                                            negate=True).then_inc(s_att_m, 1)
                    for par_ in range(2):
                        for tt, (s, n) in enumerate(TILES):
                            k = 3 * par_ + tt
                            v.wait_ge(s_att_p, c.next(s_att_p))
                            c.link(V.reciprocal(asm[0:n, 1, k:k + 1], asm[0:n, 1, k:k + 1]))
                            TS(ap_[0:n, par_, tt, 0:s + n], ap_[0:n, par_, tt, 0:s + n], asm[0:n, 1, k:k + 1], None,
                               MUL).then_inc(s_att_pn, 1)
                    v.wait_ge(s_att_o, c.next(s_att_o))
                    TT(ay[:, pr, :], ps[:, 6, 0:TOK], aog[:, pr, :], MUL).then_inc(s_att_od, 1)
                meet(c, s_met)
                feed("att_out", ay, TOK)
                norm_post(par("mix_post", 0, 8))

            def conv(dst, src, w, taps):
                for back in range(1, taps):
                    last = STT(dst[:, back:TOK], src[:, 0:TOK - back], w(taps - 1 - back), dst[:, back:TOK], MUL, ADD)
                    if back < taps - 1:
                        c.link(last)
                return last

            def ffn(n):
                norm_two(par("ffn_pre", 8 * n, 8))
                c.n[s_bank_free.name] = 4 + blocks_before[f"up{n}"]
                w3 = par("ffn_conv", n * 132, 132).rearrange("p (b w) -> p b w", w=3)
                with c.loop(11, tap_done=4, bank_free=4, ffn_gelu=2, dve_own=4) as b:
                    for q in range(2):
                        for j in (2 * q, 2 * q + 1):
                            split(At(first[f"up{n}"] + j + 2, b, 4))
                            v.wait_ge(s_tap_done, c.next(s_tap_done))
                            conv(fconv[:, 0, j, :], ps[:, j, 0:TOK], lambda k: w3[:, b * 4 + j, k:k + 1],
                                 3).then_inc(s_bank_free, 1)
                        v.wait_ge(s_bank_free, c.next(s_bank_free, 2))
                        v.wait_ge(s_ffn_gelu, c.next(s_ffn_gelu))
                        TT(fact[:, b * 2 + q, :], fconv[:, 1, 2 * q, :], fconv[:, 0, 2 * q + 1, :], MUL)
                meet(c, s_met)
                feed(f"down{n}", fact, TOK)
                norm_post(par("ffn_post", 8 * n, 8))

            if on["ffn0"]:
                ffn(0)

            if on["dn"]:
                v.wait_ge(s_tabs_in, c.next(s_tabs_in, 16))
                norm_two(par("mix_pre", 8, 8))
                w4 = par("dn_conv", 0, 96).rearrange("p (b w) -> p b w", w=4)
                with c.loop(3, dn_silu=8, dve_own=24) as b:
                    for j in range(8):
                        split(At(first["dn_in"] + j + 2, b))
                        v.wait_ge(s_half_used, At(first["dn_in"] + j, b).halves(2))
                        v.wait_ge(s_dn_silu, c.next(s_dn_silu))
                        c.link(TS(dwork[:, j % 2, :], ps[:, j % 4, 0:TOK], w4[:, b * 8 + j, 3:4], None, MUL))
                        conv(dwork[:, j % 2, :], ps[:, j % 4, 0:TOK], lambda k: w4[:, b * 8 + j, k:k + 1],
                             4).then_inc(s_bank_free, 1)
                split_all("dn_in", 24, 8)
                c.link(V.memset(dsm, 0.0))
                v.wait_ge(s_scores_ready, c.next(s_scores_ready))
                for tt, (s, n) in enumerate(TILES):
                    V.tensor_copy(dsm[0:n, tt, 0, 0:8], ps[0:n, 5, tt * 16:tt * 16 + 8])
                    last = TT(dsm[0:n, tt, 1, 0:8], ps[0:n, 5, tt * 16 + 8:tt * 16 + 16], par("dt_bias", 0, 8)[0:n, :], ADD)
                c.link(last)
                STT(dsm[:, :, 5, 0:8], dsm[:, :, 1, 0:8], -1.0, dsm[:, :, 1, 0:8], MUL, ALU.min).then_inc(s_logit_in, 1)
                v.wait_ge(s_root, c.next(s_root))
                V.reciprocal(row_rstd[0:16, :], row_rstd[0:16, :]).then_inc(s_inv, 1)
                for b in range(16):
                    v.wait_ge(s_norms, c.next(s_norms))
                    STT(dqkv[:, b, :], dqkv[:, b, :], P ** -0.5 if b < 8 else 1.0, ps[:, b % 4, 0:TOK], MUL,
                        MUL).then_inc(s_scaled, 1)
                v.wait_ge(s_logit_exp, c.next(s_logit_exp))
                c.link(STT(dsm[:, :, 1, 0:8], dsm[:, :, 1, 0:8], 0.0, dsm[:, :, 5, 0:8], ALU.max, ADD))
                STT(dsm[:, :, 2, 0:8], dsm[:, :, 1, 0:8], -1.0, bc(dsm[:, 0, 4, 8:16], 1, [P, 3, 8]), MUL, MUL)
                V.memset(dST, 0.0)
                meet(c, s_met)
                for ch, (s, n) in enumerate(TILES):
                    beta = dsm[0:n, ch, 0, 0:8]
                    beta_n = lambda here: beta[:, here].unsqueeze(2).to_broadcast([n, 4, n])
                    levels = n.bit_length() - 1
                    groups = (slice(0, 4), slice(4, 8))
                    mask = tab("levels").rearrange("p (l c) -> p l c", l=LEVELS)

                    def masked(lv, here):
                        return TT(dMT[0:n, here, 0:n], dLT[0:n, here, 0:n], bc(mask[0:n, lv, 0:n], 1, [n, 4, n]), MUL)

                    for g, here in enumerate(groups):
                        v.wait_ge(s_dn_p, c.next(s_dn_p))
                        if g == 0:
                            c.link(V.tensor_copy(dsm[0:n, ch, 3, 0:8], ps[0:n, 2, 0:8]))
                        c.link(TT(ddec[0:n, here, 0:n], heads4(g, n, n),
                                  dsm[0:n, ch, 3, 0:8][:, here].unsqueeze(2).to_broadcast([n, 4, n]), SUB))
                        TT(ddec[0:n, here, 0:n], ddec[0:n, here, 0:n], bc(tab("mneg")[0:n, 0:n], 1, [n, 4, n]),
                           ADD).then_inc(s_logit_in, 1)
                    V.tensor_copy(dX[0:n, :, 0:n], bc(ident[0:n, 0:n], 1, [n, 8, n]))
                    V.tensor_copy(dXT[0:n, :, 0:n], bc(ident[0:n, 0:n], 1, [n, 8, n]))
                    for g, here in enumerate(groups):
                        v.wait_ge(s_logit_exp, c.next(s_logit_exp))
                        TT(dLT[0:n, here, 0:n], heads4(4 + g, n, n), ddec[0:n, here, 0:n], MUL)
                        TT(dqd[:, here, 0:n], dqkv[:, here, s:s + n], dER[:, here, 0:n], MUL)
                        if g == 0:
                            TT(dsm[0:n, ch, 4, 0:8], dsm[0:n, ch, 4, 0:8], beta, MUL)
                        TT(dQK[0:n, here, 0:n], heads4(6 + g, n, n), ddec[0:n, here, 0:n], MUL).then_inc(s_dn_v, 1)
                    for g, here in enumerate(groups):
                        v.wait_ge(s_dn_p, c.next(s_dn_p))
                        masked(0, here)
                        TT(dkb[0:n, here], heads4(g, n, P), dsm[0:n, ch, 4, 0:8][:, here].unsqueeze(2).to_broadcast([n, 4, P]), MUL)
                        TT(dkd[0:n, here], heads4(g, n, P), ddec[0:n, here, n - 1:n].to_broadcast([n, 4, P]), MUL)
                        TT(dvb[0:n, here], heads4(2 + g, n, P), beta[:, here].unsqueeze(2).to_broadcast([n, 4, P]),
                           MUL).then_inc(s_dn_v, 1)
                    for lv in range(levels):
                        for g, here in enumerate(groups):
                            v.wait_ge(s_dn_p, c.next(s_dn_p))
                            TT(dT1[0:n, here, 0:n], heads4(g, n, n), beta_n(here), MUL).then_inc(s_dn_v, 1)
                            if lv < levels - 1:
                                masked(lv + 1, here)
                        for g, here in enumerate(groups):
                            v.wait_ge(s_dn_p, c.next(s_dn_p))
                            TT(dX[0:n, here, 0:n], dX[0:n, here, 0:n], heads4(2 + g, n, n), SUB)
                            TT(dXT[0:n, here, 0:n], dXT[0:n, here, 0:n], heads4(4 + g, n, n), SUB).then_inc(s_dn_v, 1)
                    for g, here in enumerate(groups):
                        v.wait_ge(s_dn_p, c.next(s_dn_p))
                        TS(dW[:, here, 0:n], heads4(g, P, n), -1.0, None, MUL).then_inc(s_dn_v, 1)
                    for g, here in enumerate(groups):
                        v.wait_ge(s_dn_p, c.next(s_dn_p))
                        V.tensor_copy(dU[0:n, here], heads4(2 + g, n, P)).then_inc(s_dn_v, 1)
                    for g, here in enumerate(groups):
                        v.wait_ge(s_dn_p, c.next(s_dn_p))
                        c.link(TT(dST[:, here], dST[:, here], dER[:, here, n - 1:n].to_broadcast([P, 4, P]), MUL))
                        V.tensor_copy(dOT[:, here, s:s + n], heads4(4 + g, P, n))
                        TT(dST[:, here], dST[:, here], heads4(6 + g, P, P), ADD).then_inc(s_dn_v, 1)
                v.wait_ge(s_root, c.next(s_root))
                V.reciprocal(row_rstd[0:16, :], row_rstd[0:16, :]).then_inc(s_inv, 1)
                for b in range(8):
                    v.wait_ge(s_norms, c.next(s_norms))
                    last = STT(dOT[:, b, :], dOT[:, b, :], par("o_gain"), ps[:, b % 4, 0:TOK], MUL, MUL)
                    last.then_inc(s_scaled, 1)
                v.wait_ge(s_scaled, 16 + 16 + 8)
                TT(dOT, dOT, dog, MUL)
                meet(c, s_met)
                feed("dn_out", dOT, TOK)
                norm_post(par("mix_post", 8, 8))
            if on["ffn1"]:
                ffn(1)
            v.drain().then_inc(s_result_ready, 1)


def columns(a):
    a = np.asarray(a)
    return np.ascontiguousarray(a.reshape(-1, P).T)


def units_k(w):
    K, N = w.shape
    return np.ascontiguousarray(w.reshape(KT, P, N // P, P).transpose(2, 1, 0, 3))


def units_out(w):
    K = w.shape[0]
    rounds = -(-K // D)
    full = np.zeros((rounds * D, D), w.dtype)
    full[:K] = w
    return np.ascontiguousarray(full.reshape(rounds, KT, P, KT, P).transpose(0, 3, 2, 1, 4)).reshape(-1, P, KT, P)


def kernel(_until=None, **inputs):
    import concourse.bacc as bacc
    from concourse import mybir
    from concourse.bass_utils import run_bass_kernel_spmd

    a = {k: np.asarray(v) for k, v in inputs.items()}
    f32 = np.float32
    c1, c2, ret_dec = shape_constants()
    rows = lambda v: np.broadcast_to(v.reshape(1, -1), (P, v.size))
    conv = lambda w: w.T.reshape(-1, P, w.shape[0]).transpose(1, 0, 2).reshape(P, -1)
    pairs = lambda w: w.reshape(w.shape[0], 2, FFT, P).transpose(0, 2, 1, 3).reshape(w.shape[0], -1)
    twice = lambda g: np.concatenate([g, g]).reshape(P, 1)
    pieces = {
        "c": columns(a["c"]), "ada_b": columns(a["ada_b"]), "norm_mix": columns(a["norm_mix"]),
        "norm_ffn": columns(a["norm_ffn"]), "norm_final": columns(a["norm_final"]), "sgu_b_in": columns(a["sgu_b_in"]),
        "sgu_ln_g": columns(a["sgu_ln_g"]), "sgu_ln_b": columns(a["sgu_ln_b"]), "mix_pre": columns(a["norm_mix_pre_2"]),
        "mix_post": columns(a["norm_mix_post_2"]), "ffn_pre": columns(a["norm_ffn_pre_2"]),
        "ffn_post": columns(a["norm_ffn_post_2"]), "q_gain": twice(a["attn_q_norm_2"][0]),
        "k_gain": twice(a["attn_k_norm_2"][0]), "o_gain": a["dn_o_norm_2"].reshape(P, 1),
        "ffn_conv": np.concatenate([conv(pairs(w)) for w in a["ffn_conv_2"]], 1), "dn_conv": conv(a["dn_conv_2"][0]),
        "b_forget": rows(a["attn_b_forget_2"]), "a_log": rows(a["dn_a_log_2"]), "dt_bias": rows(a["dn_dt_bias_2"]),
    }
    params = np.concatenate([pieces[n] for n, _ in PCOLS], 1)
    assert params.shape == (P, PW), params.shape
    ada = a["ada_w"]
    aw, dw = a["attn_w_in_2"][0], a["dn_w_in_2"][0]
    tail = lambda w: np.ascontiguousarray(w[:, -16:].reshape(KT, P, 16).transpose(1, 0, 2))
    feed = {
        "params": params, "const1": c1, "const2": c2, "ret_dec": ret_dec,
        "xT": np.ascontiguousarray(a["x"][0].T.reshape(KT, P, SEQ).transpose(1, 0, 2)),
        "metaT": np.ascontiguousarray(a["meta_tokens_2"].T.reshape(KT, P, META).transpose(1, 0, 2)),
        "positions": np.ascontiguousarray(np.broadcast_to(a["positions"][0][None, :], (P, SEQ))),
        "ada": np.concatenate([units_k(ada[0]), units_k(ada[1])]),
        "ret_in": units_k(a["ret_w_in"][0]), "ret_out": units_out(a["ret_w_out"][0]),
        "query0": units_k(a["peer_w_query"][0]), "query1": units_k(a["peer_w_query"][1]),
        "keysT": np.ascontiguousarray(a["peer_sub_keys"].reshape(2, 16, NKEYS, P).transpose(0, 3, 1, 2)),
        "sgu_in": units_k(a["sgu_w_in"][0]), "sgu_out": units_out(a["sgu_w_out"][0]),
        "w_s": np.ascontiguousarray(a["sgu_w_s"][0].transpose(2, 0, 1)), "b_s": a["sgu_b_s"],
        "att_in": units_k(np.ascontiguousarray(aw[:, :4096])), "att_wf": tail(aw), "att_out": units_out(a["attn_w_out_2"][0]),
        "dn_in": units_k(np.ascontiguousarray(dw[:, :4096])), "dn_wf": tail(dw), "dn_out": units_out(a["dn_w_out_2"][0]),
    }
    for n in range(2):
        feed[f"u{n}"] = np.ascontiguousarray(a["peer_u"][n].reshape(P, P, KT, P).transpose(0, 3, 2, 1))
        feed[f"v{n}"] = a["peer_v"][n].reshape(P, P, KT, P)
        feed[f"up{n}"] = units_k(pairs(a["ffn_w_up_2"][n]))
        feed[f"down{n}"] = units_out(a["ffn_w_down_2"][n])

    nc = bacc.Bacc("TRN2", target_bir_lowering=False, num_devices=1)
    t = {k: nc.dram_tensor(f"in_{k}", v.shape, mybir.dt.from_np(v.dtype), kind="ExternalInput").ap()
         for k, v in feed.items()}
    t["scratch"] = nc.dram_tensor("ada_scratch", (1, 12288), mybir.dt.float32, kind="Internal").ap()
    width = SEQ if _until is None else TOK
    out = nc.dram_tensor("out_xT", (P, KT, width), mybir.dt.float32, kind="ExternalOutput").ap()
    build_program(nc, t, out, _until)
    r = run_bass_kernel_spmd(nc, [{f"in_{k}": v for k, v in feed.items()}], core_ids=[0])
    got = r.results[0]["out_xT"]
    if _until is not None:
        return got
    return np.ascontiguousarray(got.transpose(2, 1, 0)).reshape(1, SEQ, D)
```

```python
from contextlib import ExitStack, contextmanager

import numpy as np

P = 128
D = 1024
KT = D // P
SEQ = 256
META = 16
TOK = SEQ + META
T0 = META
RAW = 4
ADA_UNITS = 96
ROUND = 8
BANK = 512
EPS = 1e-6
NEG = -1e30
TWO_PI_PARTS = (6.28125, 1.9350051879882812e-03, 3.0199159819567e-07)
RH, RDK, RDV = 4, 256, 512
CHUNK = 64
HH, TOPK, NKEYS = 8, 16, 128
EARLY = 72
GATE_ROUNDS = [(4, 72, 0, 10), (3, 104, 40, 8)]
SG, SH = 8, 3072
ST_ = SH // P
THIRD = ST_ // 3
AH, ADH = 16, 64
DH = 8
FFT = 2816 // P
TILES = [(0, META), (META, P), (META + P, P)]
LEVELS = 7
X_ORDER = (4, 0, 1, 5, 6, 7, 2, 3)

PCOLS = [("c", 8), ("ada_b", 96), ("norm_mix", 16), ("norm_ffn", 16), ("norm_final", 8), ("sgu_b_in", 48),
         ("sgu_ln_g", 24), ("sgu_ln_b", 24), ("mix_pre", 16), ("mix_post", 16), ("ffn_pre", 16), ("ffn_post", 16),
         ("q_gain", 1), ("k_gain", 1), ("o_gain", 1), ("ffn_conv", 2 * 44 * 3), ("dn_conv", 24 * 4),
         ("b_forget", 16), ("a_log", 8), ("dt_bias", 8)]
PO, _o = {}, 0
for _n, _w in PCOLS:
    PO[_n] = _o
    _o += _w
PW = _o
C1COLS = [("ident", 128), ("iota", 128), ("inv_freq", 1)]
C2COLS = [("tri", 3 * TOK), ("causal", 128), ("mneg", 128), ("levels", LEVELS * 128), ("colsel", 64), ("colsel1", 32),
          ("rowsel", 16 * 128), ("rowsel1", 16 * 128), ("half", 2), ("selbot", 16), ("seltop", 16)]


def offsets(cols):
    out, at = {}, 0
    for name, width in cols:
        out[name] = (at, width)
        at += width
    return out, at


C1O, C1W = offsets(C1COLS)
C2O, C2W = offsets(C2COLS)


def shape_constants():
    c1 = np.zeros((P, C1W), np.float32)
    c2 = np.zeros((P, C2W), np.float32)

    def put(c, o, name, v):
        a, w = o[name]
        v = np.asarray(v, np.float32).reshape(v.shape[0], w)
        c[:v.shape[0], a:a + w] = v

    put(c1, C1O, "ident", np.eye(P))
    put(c1, C1O, "iota", np.tile(np.arange(P, dtype=np.float32), (P, 1)))
    half = RDK // 2
    put(c1, C1O, "inv_freq", (np.float32(1.0) / (np.float32(10000.0) ** (
        np.arange(half, dtype=np.float32) / np.float32(half)))).reshape(P, 1))
    tri = np.zeros((P, 3, TOK))
    for t, (s, n) in enumerate(TILES):
        for j in range(n):
            tri[j, t, s + j:] = 1.0
    put(c2, C2O, "tri", tri)
    i = np.arange(P)
    put(c2, C2O, "causal", np.where(i[None, :] > i[:, None], NEG, 0.0))
    put(c2, C2O, "mneg", np.where(i[None, :] < i[:, None], NEG, 0.0))
    lv = np.zeros((P, LEVELS, P))
    for n in range(LEVELS):
        b = 1 << n
        lv[:, n, :] = ((i[None, :] // b) % 2 == 1) & (i[:, None] // b == i[None, :] // b - 1)
    put(c2, C2O, "levels", lv)
    cs = np.zeros((P, 64))
    cs[:64, 32] = 1
    cs[64:, 33] = 1
    put(c2, C2O, "colsel", cs)
    cs = np.zeros((P, 32))
    cs[:, 16] = 1
    put(c2, C2O, "colsel1", cs)
    rs = np.zeros((32, 16, P))
    rs1 = np.zeros((16, 16, P))
    for b in range(16):
        rs[2 * b, b, :64] = 1
        rs[2 * b + 1, b, 64:] = 1
        rs1[b, b, :] = 1
    put(c2, C2O, "rowsel", rs)
    put(c2, C2O, "rowsel1", rs1)
    hf = np.zeros((32, 2))
    hf[:16, 0] = 1
    hf[16:, 1] = 1
    put(c2, C2O, "half", hf)
    sb = np.zeros((32, 16))
    stp = np.zeros((32, 16))
    for h in range(16):
        stp[h, h] = 1
        sb[16 + h, h] = 1
    put(c2, C2O, "selbot", sb)
    put(c2, C2O, "seltop", stp)
    ret = np.zeros((P, 2, RH, SEQ))
    pos = np.arange(SEQ)
    for h in range(RH):
        lg = np.log(1.0 - 2.0 ** (-5.0 - h))
        dist = np.abs(pos[None, :] - pos[:, None]).astype(np.float64)
        d = np.exp(lg * dist) * (pos[None, :] // CHUNK >= pos[:, None] // CHUNK)
        ret[:, :, h, :] = (d * RDK ** -0.5).reshape(2, P, SEQ).transpose(1, 0, 2)
    return c1, c2, ret.astype(np.float32).reshape(P, -1)


class At:

    def __init__(self, unit, b=None, step=ROUND):
        self.unit, self.b, self.step = unit, b, step
        self.raw = unit % RAW

    def plus(self, n):
        return At(self.unit + n, self.b, self.step)

    def number(self, k=0):
        return self.unit + k if self.b is None else self.b * self.step + (self.unit + k)

    def fill(self):
        n = self.unit // RAW + 1
        return n if self.b is None else self.b * (self.step // RAW) + n

    def halves(self, k):
        n = 2 * (self.unit - ADA_UNITS) + k
        return n if self.b is None else self.b * (2 * self.step) + n

    def slot(self, half):
        return (2 * self.unit + half) % 4


class Counts:

    def __init__(self, engine, own=None):
        self.engine, self.own, self.n, self.reg, self.per = engine, own, {}, None, {}

    def value(self, sem):
        v = self.n.get(sem.name, 0)
        return self.reg * self.per.get(sem.name, 0) + v if self.reg is not None else v

    def next(self, sem, k=1):
        self.n[sem.name] = self.n.get(sem.name, 0) + k
        return self.value(sem)

    def link(self, instruction):
        instruction.then_inc(self.own, 1)
        self.engine.wait_ge(self.own, self.next(self.own))

    @contextmanager
    def loop(self, count, **per):
        with self.engine.Fori(0, count) as i:
            before = dict(self.n)
            self.reg, self.per = i, per
            yield i
            self.reg = None
        for name in self.n:
            grew = self.n[name] - before.get(name, 0)
            assert grew == per.get(name, 0), (name, grew, per.get(name, 0))
            self.n[name] += grew * (count - 1)


def build_program(nc, t, out, until=None, taps=None):
    from concourse import mybir
    f32, bf16, u32, i32 = mybir.dt.float32, mybir.dt.bfloat16, mybir.dt.uint32, mybir.dt.int32
    ALU, ACT = mybir.AluOpType, mybir.ActivationFunctionType
    AX = mybir.AxisListType.X
    MUL, ADD, SUB = ALU.mult, ALU.add, ALU.subtract

    ctx = ExitStack()
    with ctx:
        def sb(name, shape, dt=f32):
            return ctx.enter_context(nc.sbuf_tensor(name, shape, dt))

        f32r = mybir.dt.float32r
        raw = sb("raw", [P, RAW, KT, P])
        w_hi = sb("w_hi", [P, 4, KT // 2, P], f32r)
        w_lo = sb("w_lo", [P, 4, KT // 2, P], f32r)
        x = sb("x", [P, KT, TOK])
        h_hi = sb("h_hi", [P, KT, TOK], f32r)
        h_lo = sb("h_lo", [P, KT, TOK], f32r)
        params = sb("params", [P, PW])
        const1 = sb("const1", [P, C1W])
        ones = sb("ones", [P, P])
        zeros_b = sb("zeros_b", [P, P], bf16)
        small = sb("small", [P, 4])
        mods = sb("mods", [P, 96])
        gains = sb("gains", [P, 4, KT])
        rstd = sb("rstd", [P, TOK])
        mixed_hi = sb("mixed_hi", [P, 2, SEQ], f32r)
        mixed_lo = sb("mixed_lo", [P, 2, SEQ], f32r)
        pick_space = sb("pick_space", [P, 2 * 2 * 4 * P])
        chosen = sb("chosen", [P, 3, SEQ])
        silu_c = sb("silu_c", [P, KT])
        arena = sb("arena", [P, 32768])
        ps = ctx.enter_context(nc.psum_tensor("ps", [P, 8, BANK], f32))

        def view(at, *shape):
            n = int(np.prod(shape))
            a = arena[:, at:at + n]
            if len(shape) == 1:
                return a
            names = " ".join(f"d{k}" for k in range(len(shape)))
            return a.rearrange(f"p ({names}) -> p {names}", **{f"d{k}": s for k, s in enumerate(shape[:-1])})

        pick = pick_space[:].rearrange("p (b n q k) -> p b n q k", b=2, n=2, q=4)
        picked = pick_space[:, 0:2 * 3 * P].rearrange("p (t n k) -> p t n k", t=2, n=3)
        gsum = pick_space[:, 1024:1024 + 2 * HH].rearrange("p (t g) -> p t g", t=2)

        ident = const1[:, 0:128]
        iota = const1[:, 128:256]
        inv_freq = const1[:, 256:257]
        eps, half_pi = small[:, 0:1], small[:, 1:2]

        def par(name, k=0, n=1):
            return params[:, PO[name] + k:PO[name] + k + n]

        def bc(ap, axis, shape):
            return ap.unsqueeze(axis).to_broadcast(list(shape))

        def sem(name):
            return ctx.enter_context(nc.semaphore(name))

        s_consts_in = sem("consts_in")
        s_ret_in = sem("ret_in")
        s_keys_in = sem("keys_in")
        s_sgu_in = sem("sgu_in")
        s_tabs_in = sem("tabs_in")
        s_row_out = sem("row_out")
        s_row_in = sem("row_in")
        s_out_done = sem("out_done")
        s_result_ready = sem("result_ready")
        s_memsets = sem("memsets")
        s_met = sem("met")
        s_half_used = sem("half_used")
        s_hi_ready = sem("hi_ready")
        s_raw_free = sem("raw_free")
        s_bank_free = sem("bank_free")
        s_act_own = sem("act_own")
        s_dve_own = sem("dve_own")
        s_c_act = sem("c_act")
        s_rope_args = sem("rope_args")
        s_rope_ready = sem("rope_ready")
        s_ada_row = sem("ada_row")
        s_ada_t = sem("ada_t")
        s_squares = sem("squares")
        s_sums = sem("sums")
        s_mean_sum = sem("mean_sum")
        s_root = sem("root")
        s_inv = sem("inv")
        s_tap_done = sem("tap_done")
        s_h_scaled = sem("h_scaled")
        s_h_whole = sem("h_whole")
        s_act_hi = sem("act_hi")
        s_h_ready = sem("h_ready")
        s_acc_done = sem("acc_done")
        s_out_ready = sem("out_ready")
        s_x_tile = sem("x_tile")
        s_vt_ready = sem("vt_ready")
        s_vt_copied = sem("vt_copied")
        s_scores_ready = sem("scores_ready")
        s_decayed = sem("decayed")
        s_y_ready = sem("y_ready")
        s_y_copied = sem("y_copied")
        s_key_scores = sem("key_scores")
        s_key_copied = sem("key_copied")
        s_gate_in = sem("gate_in")
        s_gate_exp = sem("gate_exp")
        s_picked_ready = sem("picked_ready")
        s_onehots = sem("onehots")
        s_g_ones = sem("g_ones")
        s_gelu_done = sem("gelu_done")
        s_picks_ready = sem("picks_ready")
        s_tables_ready = sem("tables_ready")
        s_g_banks = sem("g_banks")
        s_g_applied = sem("g_applied")
        s_chosen_ready = sem("chosen_ready")
        s_mix_done = sem("mix_done")
        s_sgu_centred = sem("sgu_centred")
        s_sgu_ready = sem("sgu_ready")
        s_spatial_ready = sem("spatial_ready")
        s_sgu_s = sem("sgu_s")
        s_norms = sem("norms")
        s_scaled = sem("scaled")
        s_heads_prep = sem("heads_prep")
        s_cum_ready = sem("cum_ready")
        s_att_s = sem("att_s")
        s_att_m = sem("att_m")
        s_att_p = sem("att_p")
        s_att_pn = sem("att_pn")
        s_att_t = sem("att_t")
        s_att_tc = sem("att_tc")
        s_att_o = sem("att_o")
        s_att_od = sem("att_od")
        s_logit_in = sem("logit_in")
        s_logit_exp = sem("logit_exp")
        s_ffn_gelu = sem("ffn_gelu")
        s_dn_silu = sem("dn_silu")
        s_dn_p = sem("dn_p")
        s_dn_v = sem("dn_v")
        s_fo_copied = sem("fo_copied")
        full = [ctx.enter_context(nc.semaphore(f"raw_full{k}")) for k in range(RAW)]

        ada_row = arena[0:1, 0:12288]
        ada_sq = arena[0:96, 12288:12416]
        rope = view(16384, 8, SEQ)
        posn = view(18432, SEQ).bitcast(i32)
        qk = view(0, 16, SEQ)
        vT = view(4096, 16, SEQ)
        gT = view(8192, 16, SEQ)
        vtok = view(12288, 2, 2048)
        cosT, sinT = rope[:, 6, :], rope[:, 7, :]
        ropet = view(18688, 4, 2048)
        yT = view(0, 16, SEQ)
        sT = view(4096, RH, 2, SEQ)
        ysq = view(18688, 16, SEQ)
        yrs = view(22784, RH, SEQ)
        ret_dec = view(26880, 2, RH, SEQ)
        sq = view(22400, KT, TOK)
        h = sq
        B2 = EARLY * SEQ
        sc = view(B2, 2, 16, P)
        qT = view(B2 + 4096, 16, SEQ)
        sc2 = view(B2 + 4096, 16, P)
        cand = view(B2 + 6144, HH, TOPK * TOPK)
        keysT = view(B2 + 8192, 16, P)
        cand2 = view(B2 + 8192, HH, TOPK * TOPK)
        tv = view(B2 + 10240, 2, 16, TOPK)
        ti = view(B2 + 10752, 2, 16, TOPK).bitcast(u32)
        tif = view(B2 + 11264, 2, 16, TOPK)
        bv = view(B2 + 11776, 2, HH, TOPK)
        bp = view(B2 + 12032, 2, HH, TOPK).bitcast(u32)
        bq = view(B2 + 12288, 2, 2, HH * TOPK).bitcast(u32)
        bqf = view(B2 + 12800, 2, 2, HH * TOPK)
        assert B2 + 13312 <= 32768
        G = view(0, P, SEQ)
        uT = view(0, ST_, SEQ)
        sv = view(6144, ST_, SEQ)
        ssq = view(12288, ST_, SEQ)
        svtok = view(12288, 2, SH)
        smean = view(18432, SEQ)
        srstd = view(18688, SEQ)
        sws = view(20000, SG, P)
        sbs = view(21024, SG, P)
        tabs = view(24576, C2W)
        T2 = 24576 + C2W
        dwf = view(T2, KT, 16)
        awf = view(T2 + 128, KT, 16)
        row_rstd = arena[0:32, T2 + 256:T2 + 256 + TOK]
        dsm = view(T2 + 528, 3, 6, 16)
        assert T2 + 528 + 288 <= 32768
        fo = view(20224, KT, TOK)

        def tab(name, rows=P):
            a, w = C2O[name]
            return tabs[0:rows, a:a + w]

        aqk = view(0, 16, TOK)
        aqkv = view(0, 24, TOK)
        avT = view(4352, 8, TOK)
        aog = view(6528, 8, TOK)
        asq = view(8704, 16, TOK)
        avtok = view(13056, 3, D)
        alf = view(16528, 3, 32)
        awork = view(16640, 4, 3, 16)
        acum = arena[0:32, 16832:16832 + TOK]
        aL = view(17104, 2, TOK)
        aR = view(17648, 2, TOK)
        asm = view(18192, 2, 6)
        ap_ = view(18208, 2, 3, TOK)
        qgain = view(19840, 1)
        apT = view(8704, 2, 3, 3, P)
        ay = view(4352, 8, TOK)
        dqkv = view(0, 24, TOK)
        dog = view(6528, 8, TOK)
        dsq = view(8704, 16, TOK)
        dwork = view(8704, 2, TOK)
        (dER, ddec, dLT, dQK, dkb, dkd, dvb, dX, dXT, dMT, dT1, dqd, dW, dU, dST) = (
            view(8704 + 1024 * k, 8, P) for k in range(15))
        dOT = dqkv[:, 16:24, :]
        fact = view(0, 24, TOK)
        fconv = view(6528, 2, 4, TOK)
        cact = silu_c[:, :]
        one, two = slice(T0, TOK), slice(0, TOK)

        def heads4(bank, rows, cols):
            return ps[0:rows, bank, :].rearrange("p (g c) -> p g c", c=P)[:, :, 0:cols]

        def trin(n):
            return tab("tri")[0:n, TOK + META:TOK + META + n]

        block = ctx.enter_context(nc.Block())

        parts = [("ada", 96), ("ret_in", 48), ("ret_out", 16), ("query0", 16), ("u0", 128), ("v0", 128), ("sgu_in", 48),
                 ("sgu_out", 24), ("query1", 16), ("u1", 128), ("v1", 128), ("att_in", 32), ("att_out", 8), ("up0", 44),
                 ("down0", 24), ("dn_in", 32), ("dn_out", 8), ("up1", 44), ("down1", 24)]
        first, n = {}, 0
        for name, units in parts:
            first[name] = n
            n += units
        n_units = n
        stages = ["ada", "ret", "peer0", "sgu", "peer1", "final1", "att", "ffn0", "dn", "ffn1"]
        on = {s: until is None or stages.index(s) <= stages.index(until) for s in stages}
        last_part = {None: "down1", "ada": "ada", "ret": "ret_out", "peer0": "v0", "sgu": "sgu_out", "peer1": "v1",
                     "final1": "v1", "att": "att_out", "ffn0": "down0", "dn": "dn_out", "ffn1": "down1"}[until]

        limit = first[last_part] + dict(parts)[last_part]
        blocks_before, nb = {}, 0
        for name, units in parts:
            blocks_before[name] = nb
            if name in ("ret_in", "query0", "query1", "u0", "u1", "sgu_in", "att_in", "up0", "up1", "dn_in"):
                nb += units

        def groups_at(j, groups):
            return range(j * groups // ROUND, (j + 1) * groups // ROUND)

        def at_round(b, step, n):
            return n if b is None else b * step + n

        def meet(c, sem):
            c.engine.drain().then_inc(sem, 1)
            c.engine.wait_ge(sem, c.next(sem, 4))

        @block.sync
        def _(sp):
            sp.dma_start(params[:], t["params"]).then_inc(s_consts_in, 16)
            sp.dma_start(const1[:], t["const1"]).then_inc(s_consts_in, 16)
            sp.dma_start(x[:, :, T0:TOK], t["xT"]).then_inc(s_consts_in, 16)
            sp.dma_start(posn, t["positions"]).then_inc(s_consts_in, 16)

            def load(src, at):
                if not (at.b is None and at.unit < RAW):
                    sp.wait_ge(s_raw_free, at.number(1 - RAW) * 2)
                sp.dma_start(raw[:, at.raw, :, :], src).then_inc(full[at.raw], 16)

            def stream(src, base, count):
                done = 0
                if base == 0:
                    for k in range(ROUND):
                        load(src[k], At(k))
                    done = ROUND
                rounds = (count - done) // ROUND
                with sp.Fori(0, rounds) as b:
                    for k in range(ROUND):
                        load(src[b * ROUND + (done + k)], At(base + done + k, b))
                for k in range(done + rounds * ROUND, count):
                    load(src[k], At(base + k))

            for name, units in parts:
                stream(t[name], first[name], units)
                if name == last_part:
                    break
            sp.wait_ge(s_result_ready, 1)
            if until is None:
                sp.dma_start(out, x[:, :, T0:TOK]).then_inc(s_out_done, 16)
            else:
                sp.dma_start(out, x[:, :, :]).then_inc(s_out_done, 16)
            sp.wait_ge(s_out_done, 16)

        @block.gpsimd
        def _(pool):
            c = Counts(pool)
            pool.memset(ones[:], 1.0).then_inc(s_memsets, 1)
            pool.memset(zeros_b[:], 0.0).then_inc(s_memsets, 1)
            pool.memset(small[:, 0:1], EPS).then_inc(s_memsets, 1)
            pool.memset(small[:, 1:2], float(np.pi / 2)).then_inc(s_memsets, 1)
            pool.memset(small[:, 2:4], 1.0).then_inc(s_memsets, 1)
            pool.memset(x[:, :, 0:T0], 0.0).then_inc(s_memsets, 1)
            pool.engine_nop().then_inc(s_bank_free, 4)
            pool.engine_nop().then_inc(s_dn_silu, 2)
            pool.wait_ge(s_ada_row, c.next(s_ada_row, 24))
            pool.dma_start(t["scratch"], ada_row).then_inc(s_row_out, 16)
            pool.wait_ge(s_row_out, 16)
            pool.dma_start(ada_sq, t["scratch"].rearrange("a (b c) -> (a b) c", c=P)).then_inc(s_row_in, 16)
            meet(c, s_met)
            if on["ret"]:
                pool.dma_start(ret_dec, t["ret_dec"]).then_inc(s_ret_in, 16)
                meet(c, s_met)
                meet(c, s_met)
            for layer in range(2):
                if on["peer%d" % layer]:
                    meet(c, s_met)
                    pool.dma_start(keysT, t["keysT"][layer]).then_inc(s_keys_in, 16)
                    pool.wait_ge(s_gate_in, c.next(s_gate_in))
                    pool.memset(G[:, EARLY:P, :], 1.0).then_inc(s_g_ones, 1)
                    meet(c, s_met)
                if layer == 0 and on["sgu"]:
                    pool.dma_start(sws, t["w_s"]).then_inc(s_sgu_in, 16)
                    pool.wait_ge(s_sgu_in, 16)
                    pool.memset(sws[64:128, :, 0:64], 0.0).then_inc(s_memsets, 1)
                    pool.dma_start(sbs[0:1, :, :], t["b_s"]).then_inc(s_sgu_in, 16)
                    meet(c, s_met)
                    meet(c, s_met)
            if on["att"]:
                pool.dma_start(x[:, :, 0:T0], t["metaT"]).then_inc(s_tabs_in, 16)
                pool.dma_start(tabs, t["const2"]).then_inc(s_tabs_in, 16)
                pool.dma_start(awf, t["att_wf"]).then_inc(s_tabs_in, 16)
                for _ in range(3):
                    meet(c, s_met)
            if on["ffn0"]:
                pool.memset(fact[:, 22:24, :], 0.0).then_inc(s_memsets, 1)
                meet(c, s_met)
                meet(c, s_met)
            if on["dn"]:
                pool.dma_start(dwf, t["dn_wf"]).then_inc(s_tabs_in, 16)
                for _ in range(3):
                    meet(c, s_met)
            if on["ffn1"]:
                pool.memset(fact[:, 22:24, :], 0.0).then_inc(s_memsets, 1)
                meet(c, s_met)
                meet(c, s_met)

        @block.tensor
        def _(pe):
            c = Counts(pe)
            mm, tr = nc.tensor.matmul, nc.tensor.transpose

            def unit(at, dst, moving, opened=False, second_half=None):
                for half in range(2):
                    if half and second_half is not None:
                        pe.wait_ge(s_h_ready, second_half)
                    pe.wait_ge(s_raw_free, at.halves(2 * ADA_UNITS + half + 1))
                    for q in range(4):
                        k, slot = 4 * half + q, at.slot(half)
                        hi, lo = moving(k)
                        begin, end = opened is False and k == 0, opened or k == KT - 1
                        mm(dst(k), w_lo[:, slot, q, :], hi, start=begin, stop=opened, skip_group_check=opened)
                        mm(dst(k), w_hi[:, slot, q, :], lo, start=False, stop=opened, skip_group_check=opened)
                        last = mm(dst(k), w_hi[:, slot, q, :], hi, start=False, stop=end, skip_group_check=opened)
                    last.then_inc(s_half_used, 1)

            def project(name, cols, count=None):
                base, count = first[name], count or dict(parts)[name]
                rounds = count // ROUND
                width = cols.stop - cols.start

                def one_unit(j, b=None):
                    pe.wait_ge(s_bank_free, c.next(s_bank_free))
                    unit(At(base + j, b), lambda k: ps[:, j % 4, 0:width], lambda k: (h_hi[:, k, 0:width], h_lo[:, k, 0:width]))

                with c.loop(rounds, bank_free=ROUND) as b:
                    for j in range(ROUND):
                        one_unit(j, b)
                for j in range(rounds * ROUND, count):
                    one_unit(j)

            def zero_banks(banks):
                for bank in banks:
                    for side in range(2):
                        mm(ps[:, bank, side * SEQ:side * SEQ + SEQ], zeros_b[:, :], ones[:].bitcast(bf16), start=True,
                           stop=True)

            def project_out(name, width, signal):
                base, count = first[name], dict(parts)[name]
                zero_banks(range(8))

                def round_of(r, b=None):
                    pe.wait_ge(s_h_ready, c.next(s_h_ready))
                    for m in range(8):
                        unit(At(base + r * ROUND + m, b), lambda k: ps[:, m, 0:width],
                             lambda k: (h_hi[:, k, 0:width], h_lo[:, k, 0:width]), opened=True,
                             second_half=c.next(s_h_ready) if m == 0 else None)

                rounds = count // ROUND
                if rounds > 1:
                    with c.loop(rounds - 1, h_ready=2) as b:
                        round_of(0, b)
                round_of(rounds - 1)
                pe.drain().then_inc(signal, 1)

            def moved():
                pe.wait_ge(s_bank_free, c.n[s_bank_free.name] + 4)

            def sum_tiles(src, tiles, cols, signal=s_sums, bank=4):
                for k in range(tiles):
                    last = mm(ps[:, bank, 0:cols.stop - cols.start], ones[:], src[:, k, 0:cols.stop - cols.start], start=k == 0,
                              stop=k == tiles - 1)
                last.then_inc(signal, 1)

            def sum_x(cols, updated=True):
                if updated:
                    pe.wait_ge(s_x_tile, c.next(s_x_tile, 3))
                    c.next(s_x_tile, 5)
                for n, k in enumerate(X_ORDER):
                    pe.wait_ge(s_squares, c.next(s_squares))
                    last = mm(ps[:, 4, 0:cols.stop - cols.start], ones[:], sq[:, k, 0:cols.stop - cols.start],
                              start=n == 0, stop=n == KT - 1)
                last.then_inc(s_sums, 1)

            def norm(cols, updated=True):
                sum_x(cols, updated)
                pe.wait_ge(s_h_ready, c.next(s_h_ready))

            pe.wait_ge(s_memsets, c.next(s_memsets, 6))
            pe.wait_ge(s_c_act, c.next(s_c_act))

            def ada_unit(j, b=None):
                at = At(j, b)
                pe.wait_ge(full[at.raw], at.fill() * 16)
                for k in range(KT):
                    last = mm(ps[0:1, (j // 4) % 2, (j % 4) * P:(j % 4) * P + P], cact[:, k:k + 1], raw[:, at.raw, k, :],
                              start=k == 0, stop=k == KT - 1)
                last.then_inc(s_raw_free, 2)
            for j in range(8):
                ada_unit(j)
            with c.loop(11, ada_row=2) as b:
                for j in range(8):
                    if j % 4 == 0:
                        pe.wait_ge(s_ada_row, c.next(s_ada_row))
                    ada_unit(8 + j, b)
            pe.wait_ge(s_ada_row, c.next(s_ada_row, 2))
            pe.wait_ge(s_row_in, 16)
            pe.wait_ge(s_consts_in, c.next(s_consts_in, 64))
            tr(ps[:, 2, 0:96], ada_sq, ident[0:96, 0:96]).then_inc(s_ada_t, 1)
            meet(c, s_met)

            if on["ret"]:
                norm(one, updated=False)
                project("ret_in", one)
                meet(c, s_met)
                for n in range(8):
                    for q in range(4):
                        m, jt = 2 * n + q // 2, q % 2
                        last = tr(ps[:, n, q * P:q * P + P], vT[:, m, jt * P:jt * P + P], ident)
                    last.then_inc(s_vt_ready, 1)
                for hd in range(RH):
                    pe.wait_ge(s_vt_copied, c.next(s_vt_copied, 2))
                for hd in range(RH):
                    for jt in range(2):
                        for k in range(2):
                            last = mm(ps[:, hd, jt * SEQ:jt * SEQ + SEQ], qk[:, 8 + 2 * hd + k, jt * P:jt * P + P],
                                      qk[:, 2 * hd + k, :], start=k == 0, stop=k == 1)
                    last.then_inc(s_scores_ready, 1)
                for hd in range(RH):
                    pe.wait_ge(s_decayed, c.next(s_decayed))
                for m in range(16):
                    hd = m // 4
                    if m >= 4:
                        pe.wait_ge(s_y_copied, c.next(s_y_copied))
                    for jt in range(2):
                        last = mm(ps[:, 4 + m % 4, 0:SEQ], vtok[:, jt, m * P:m * P + P], sT[:, hd, jt, :], start=jt == 0,
                                  stop=jt == 1)
                    last.then_inc(s_y_ready, 1)
                pe.wait_ge(s_y_copied, c.next(s_y_copied, 4))
                pe.wait_ge(s_squares, c.next(s_squares))
                for hd in range(RH):
                    for k in range(4):
                        last = mm(ps[:, hd // 2, (hd % 2) * SEQ:(hd % 2) * SEQ + SEQ], ones[:], ysq[:, 4 * hd + k, :],
                                  start=k == 0, stop=k == 3)
                last.then_inc(s_sums, 1)
                meet(c, s_met)
                project_out("ret_out", SEQ, s_acc_done)

            def peer(layer):
                norm(one)
                meet(c, s_met)
                project(f"query{layer}", one)
                pe.wait_ge(s_keys_in, c.next(s_keys_in, 16))
                moved()
                for tt in range(2):
                    for m in range(16):
                        last = mm(ps[:, 4 * tt + m // 4, (m % 4) * P:(m % 4) * P + P], qT[:, m, tt * P:tt * P + P],
                                  keysT[:, m, :], start=True, stop=True)
                        if m % 4 == 3:
                            last.then_inc(s_key_scores, 1)
                pe.wait_ge(s_key_copied, c.next(s_key_copied, 8))
                project(f"u{layer}", one, EARLY)
                pe.wait_ge(s_picked_ready, c.next(s_picked_ready))
                for n in range(3):
                    for tt in range(2):
                        last = tr(ps[:, 4 + n, tt * P:tt * P + P], picked[:, tt, n, :], ident)
                last.then_inc(s_tables_ready, 1)

                for rounds, tile, group, groups in GATE_ROUNDS:
                    base = first[f"u{layer}"] + tile
                    with c.loop(rounds, bank_free=ROUND, picks_ready=groups) as b:
                        for j in range(ROUND):
                            pe.wait_ge(s_bank_free, c.next(s_bank_free))
                            unit(At(base + j, b), lambda k: ps[:, j % 4, 0:SEQ],
                                 lambda k: (h_hi[:, k, 0:SEQ], h_lo[:, k, 0:SEQ]))
                            for k in groups_at(j, groups):
                                pe.wait_ge(s_picks_ready, c.next(s_picks_ready))
                                for q in range(4):
                                    last = mm(ps[:, 4 + k % 2, q * P:q * P + P], pick[:, k % 2, 1, q, :],
                                              pick[:, k % 2, 0, q, :], start=True, stop=True)
                                last.then_inc(s_g_banks, 1)
                pe.wait_ge(s_g_applied, c.next(s_g_applied))
                zero_banks(range(4, 8))
                base = first[f"v{layer}"]
                with c.loop(P // ROUND, mix_done=ROUND) as b:
                    for j in range(ROUND):
                        pe.wait_ge(s_mix_done, c.next(s_mix_done))
                        unit(At(base + j, b), lambda m: ps[:, 4 + m // 2, (m % 2) * SEQ:(m % 2) * SEQ + SEQ],
                             lambda m: (mixed_hi[:, j % 2, :], mixed_lo[:, j % 2, :]), opened=True)
                pe.drain().then_inc(s_acc_done, 1)
                meet(c, s_met)

            if on["peer0"]:
                peer(0)

            if on["sgu"]:
                pe.wait_ge(s_memsets, c.next(s_memsets))
                norm(one)
                project("sgu_in", one)
                moved()
                sum_tiles(sv, ST_, slice(0, SEQ), s_mean_sum)
                for m in range(ST_):
                    if m % THIRD == 0:
                        pe.wait_ge(s_squares, c.next(s_squares))
                    last = mm(ps[:, 4, 0:SEQ], ones[:], ssq[:, m, :], start=m == 0, stop=m == ST_ - 1)
                last.then_inc(s_sums, 1)
                for n in range(12):
                    if 2 * n % THIRD == 0:
                        pe.wait_ge(s_sgu_ready, c.next(s_sgu_ready))
                    if n >= 4:
                        pe.wait_ge(s_vt_copied, c.next(s_vt_copied))
                    for q in range(4):
                        m, jt = 2 * n + q // 2, q % 2
                        last = tr(ps[:, n % 4, q * P:q * P + P], sv[:, m, jt * P:jt * P + P], ident)
                    last.then_inc(s_vt_ready, 1)
                pe.wait_ge(s_vt_copied, c.next(s_vt_copied, 4))
                pe.wait_ge(s_sgu_in, c.next(s_sgu_in, 32))
                for n in range(12):
                    if n >= 4:
                        pe.wait_ge(s_sgu_s, c.next(s_sgu_s))
                    for q in range(4):
                        m, jt = 2 * n + q // 2, q % 2
                        dst = ps[:, 4 + n % 4, q * P:q * P + P]
                        mm(dst, svtok[:, jt, m * P:m * P + P], sws[:, m // 3, :], start=True, stop=False)
                        last = mm(dst, ones[0:1, :], sbs[0:1, m // 3, :], start=False, stop=True)
                    last.then_inc(s_spatial_ready, 1)
                pe.wait_ge(s_sgu_s, c.next(s_sgu_s, 4))
                meet(c, s_met)
                project_out("sgu_out", SEQ, s_acc_done)
                meet(c, s_met)

            if on["peer1"]:
                peer(1)
            if on["final1"]:
                sum_x(one)

            def norm_post():
                pe.wait_ge(s_fo_copied, c.next(s_fo_copied))
                sum_tiles(sq, KT, two)

            if on["att"]:
                pe.wait_ge(s_tabs_in, c.next(s_tabs_in, 48))
                norm(two)
                project("att_in", two)
                for tt, (s, n) in enumerate(TILES):
                    for k in range(KT):
                        last = mm(ps[0:n, 5, tt * 16:tt * 16 + 16], h[:, k, s:s + n], awf[:, k, :], start=k == 0,
                                  stop=k == KT - 1)
                last.then_inc(s_scores_ready, 1)
                moved()
                pe.wait_ge(s_squares, c.next(s_squares))
                for b in range(16):
                    last = mm(ps[0:32, 6, 0:TOK], tab("colsel")[:, 32 - 2 * b:64 - 2 * b], asq[:, b, :], start=b == 0,
                              stop=b == 15)
                last.then_inc(s_sums, 1)
                pe.wait_ge(s_inv, c.next(s_inv))
                for b in range(16):
                    if b >= 4:
                        pe.wait_ge(s_scaled, c.next(s_scaled))
                    mm(ps[:, b % 4, 0:TOK], tab("rowsel", 32)[:, b * P:b * P + P], row_rstd, start=True,
                       stop=True).then_inc(s_norms, 1)
                pe.wait_ge(s_scaled, c.next(s_scaled, 4))
                for n in range(8):
                    if n >= 4:
                        pe.wait_ge(s_vt_copied, c.next(s_vt_copied))
                    for tt, (s, w) in enumerate(TILES):
                        last = tr(ps[0:w, n % 4, tt * P:tt * P + P], avT[:, n, s:s + w], ident)
                    last.then_inc(s_vt_ready, 1)
                pe.wait_ge(s_vt_copied, c.next(s_vt_copied, 4))
                pe.wait_ge(s_heads_prep, c.next(s_heads_prep))
                for tt, (s, n) in enumerate(TILES):
                    last = mm(ps[0:32, 5, 0:TOK], alf[0:n, tt, :], tab("tri")[0:n, tt * TOK:tt * TOK + TOK], start=tt == 0,
                              stop=tt == 2)
                last.then_inc(s_cum_ready, 1)
                meet(c, s_met)
                for pr in range(AH // 2):
                    for par_ in range(2):
                        lo = 64 * par_
                        pe.wait_ge(s_heads_prep, c.next(s_heads_prep))
                        for tt, (s, n) in enumerate(TILES):
                            kend = s + n
                            dst = ps[0:n, 3 * par_ + tt, 0:kend]
                            mm(dst, aqk[lo:lo + 64, pr, s:s + n], aqk[lo:lo + 64, 8 + pr, 0:kend], start=True, stop=False)
                            mm(dst, aL[0:32, par_, s:s + n], aR[0:32, par_, 0:kend], start=False,
                               stop=True).then_inc(s_att_s, 1)
                    for par_ in range(2):
                        for tt, (s, n) in enumerate(TILES):
                            pe.wait_ge(s_att_pn, c.next(s_att_pn))
                            for kt in range(tt + 1):
                                ks, kn = TILES[kt]
                                last = tr(ps[0:kn, 3 * par_ + tt, kt * P:kt * P + n], ap_[0:n, par_, tt, ks:ks + kn],
                                          ident[0:n, 0:n])
                            last.then_inc(s_att_t, 1)
                    for par_ in range(2):
                        lo = 64 * par_
                        for tt, (s, n) in enumerate(TILES):
                            pe.wait_ge(s_att_tc, c.next(s_att_tc))
                            for kt in range(tt + 1):
                                ks, kn = TILES[kt]
                                hd = 2 * pr + par_
                                last = mm(ps[lo:lo + 64, 6, s:s + n], avtok[0:kn, kt, hd * 64:hd * 64 + 64],
                                          apT[0:kn, par_, tt, kt, 0:n], start=kt == 0, stop=kt == tt)
                    last.then_inc(s_att_o, 1)
                    pe.wait_ge(s_att_od, c.next(s_att_od))
                meet(c, s_met)
                project_out("att_out", TOK, s_out_ready)
                norm_post()
                meet(c, s_met)

            def ffn(n):
                norm(two)
                project(f"up{n}", two)
                pe.wait_ge(s_memsets, c.next(s_memsets))
                meet(c, s_met)
                project_out(f"down{n}", TOK, s_out_ready)
                norm_post()
                meet(c, s_met)

            if on["ffn0"]:
                ffn(0)

            if on["dn"]:
                pe.wait_ge(s_tabs_in, c.next(s_tabs_in, 16))
                norm(two)
                project("dn_in", two)
                for tt, (s, n) in enumerate(TILES):
                    for k in range(KT):
                        last = mm(ps[0:n, 5, tt * 16:tt * 16 + 16], h[:, k, s:s + n], dwf[:, k, :], start=k == 0,
                                  stop=k == KT - 1)
                last.then_inc(s_scores_ready, 1)
                moved()
                pe.wait_ge(s_squares, c.next(s_squares))
                for b in range(16):
                    last = mm(ps[0:16, 6, 0:TOK], tab("colsel1")[:, 16 - b:32 - b], dsq[:, b, :], start=b == 0, stop=b == 15)
                last.then_inc(s_sums, 1)
                pe.wait_ge(s_inv, c.next(s_inv))
                for b in range(16):
                    if b >= 4:
                        pe.wait_ge(s_scaled, c.next(s_scaled))
                    mm(ps[:, b % 4, 0:TOK], tab("rowsel1", 16)[:, b * P:b * P + P], row_rstd[0:16, :], start=True,
                       stop=True).then_inc(s_norms, 1)
                pe.wait_ge(s_scaled, c.next(s_scaled, 4))
                meet(c, s_met)
                for ch, (s, n) in enumerate(TILES):
                    tri_n = trin(n)
                    levels = n.bit_length() - 1
                    col = lambda hd, w: slice((hd % 4) * P, (hd % 4) * P + w)
                    mm(ps[0:n, 2, 0:8], tri_n, dsm[0:n, ch, 2, 0:8], start=True, stop=True)
                    for g in range(2):
                        for hd in range(4 * g, 4 * g + 4):
                            mm(ps[:, g, col(hd, n)], dsm[0:n, ch, 2, hd:hd + 1].to_broadcast([n, P]), tri_n, start=True,
                               stop=True)
                            mm(ps[0:n, 4 + g, col(hd, n)], dqkv[:, 8 + hd, s:s + n], dqkv[:, 8 + hd, s:s + n],
                               start=True, stop=True)
                            last = mm(ps[0:n, 6 + g, col(hd, n)], dqkv[:, 8 + hd, s:s + n], dqkv[:, hd, s:s + n],
                                      start=True, stop=True)
                        last.then_inc(s_dn_p, 1)
                    for g in range(2):
                        pe.wait_ge(s_dn_v, c.next(s_dn_v))
                        for hd in range(4 * g, 4 * g + 4):
                            tr(ps[0:n, g, col(hd, P)], dqkv[:, 8 + hd, s:s + n], ident)
                            last = tr(ps[0:n, 2 + g, col(hd, P)], dqkv[:, 16 + hd, s:s + n], ident)
                        last.then_inc(s_dn_p, 1)
                    for lv in range(levels):
                        for g in range(2):
                            pe.wait_ge(s_dn_v, c.next(s_dn_v))
                            for hd in range(4 * g, 4 * g + 4):
                                last = mm(ps[0:n, g, col(hd, n)], dMT[0:n, hd, 0:n], dX[0:n, hd, 0:n], start=True, stop=True)
                            last.then_inc(s_dn_p, 1)
                        for g in range(2):
                            pe.wait_ge(s_dn_v, c.next(s_dn_v))
                            for hd in range(4 * g, 4 * g + 4):
                                mm(ps[0:n, 2 + g, col(hd, n)], dXT[0:n, hd, 0:n], dT1[0:n, hd, 0:n], start=True, stop=True)
                                last = mm(ps[0:n, 4 + g, col(hd, n)], dT1[0:n, hd, 0:n], dXT[0:n, hd, 0:n], start=True,
                                          stop=True)
                            last.then_inc(s_dn_p, 1)
                    for g in range(2):
                        pe.wait_ge(s_dn_v, c.next(s_dn_v))
                        for hd in range(4 * g, 4 * g + 4):
                            last = mm(ps[:, g, col(hd, n)], dkb[0:n, hd, :], dXT[0:n, hd, 0:n], start=True, stop=True)
                        last.then_inc(s_dn_p, 1)
                    for g in range(2):
                        pe.wait_ge(s_dn_v, c.next(s_dn_v))
                        for hd in range(4 * g, 4 * g + 4):
                            dst = ps[0:n, 2 + g, col(hd, P)]
                            mm(dst, dXT[0:n, hd, 0:n], dvb[0:n, hd, :], start=True, stop=False)
                            last = mm(dst, dW[:, hd, 0:n], dST[:, hd, :], start=False, stop=True)
                        last.then_inc(s_dn_p, 1)
                    for g in range(2):
                        pe.wait_ge(s_dn_v, c.next(s_dn_v))
                        for hd in range(4 * g, 4 * g + 4):
                            dst = ps[:, 4 + g, col(hd, n)]
                            mm(dst, dST[:, hd, :], dqd[:, hd, 0:n], start=True, stop=False)
                            mm(dst, dU[0:n, hd, :], dQK[0:n, hd, 0:n], start=False, stop=True)
                            last = mm(ps[:, 6 + g, col(hd, P)], dkd[0:n, hd, :], dU[0:n, hd, :], start=True, stop=True)
                        last.then_inc(s_dn_p, 1)
                    pe.wait_ge(s_dn_v, c.next(s_dn_v, 2))
                pe.wait_ge(s_squares, c.next(s_squares))
                for b in range(8):
                    last = mm(ps[0:16, 6, 0:TOK], tab("colsel1")[:, 16 - b:32 - b], dsq[:, b, :], start=b == 0, stop=b == 7)
                last.then_inc(s_sums, 1)
                pe.wait_ge(s_inv, c.next(s_inv))
                for b in range(8):
                    if b >= 4:
                        pe.wait_ge(s_scaled, c.next(s_scaled))
                    mm(ps[:, b % 4, 0:TOK], tab("rowsel1", 16)[:, b * P:b * P + P], row_rstd[0:16, :], start=True,
                       stop=True).then_inc(s_norms, 1)
                pe.wait_ge(s_scaled, c.next(s_scaled, 4))
                meet(c, s_met)
                project_out("dn_out", TOK, s_out_ready)
                norm_post()
                meet(c, s_met)
            if on["ffn1"]:
                ffn(1)

        @block.scalar
        def _(act):
            c = Counts(act, s_act_own)
            A = nc.scalar.activation

            def split(at):
                if at.b is None and at.unit >= limit:
                    return
                act.wait_ge(full[at.raw], at.fill() * 16)
                for half in range(2):
                    if not (at.b is None and at.unit < ADA_UNITS + 2):
                        act.wait_ge(s_half_used, at.halves(half - 3))
                    A(w_hi[:, at.slot(half)], raw[:, at.raw, 4 * half:4 * half + 4, :], ACT.Copy).then_inc(s_hi_ready, 1)

            def take(name, skip, rounds, dst, func, bias=None):
                with c.loop(rounds) as b:
                    for j in range(ROUND):
                        at = At(first[name] + skip + j, b)
                        split(at.plus(2))
                        act.wait_ge(s_half_used, at.halves(2))
                        width = dst(0).shape[-1]
                        extra = {} if bias is None else {"bias": bias(b * ROUND + j)}
                        A(dst(b * ROUND + j), ps[:, j % 4, 0:width], func, **extra).then_inc(s_bank_free, 1)

            def feed(name, src, width):
                base, rounds = first[name], dict(parts)[name] // ROUND

                def round_of(r, b=None):
                    for k in range(KT):
                        if k % 4 == 0 and not (b is None and r == 0):
                            act.wait_ge(s_half_used, At(base + r * ROUND, b).halves(0 if k else -1))
                        A(h_hi[:, k, 0:width], src[:, (r * KT + k) if b is None else b * KT + (r * KT + k), 0:width],
                          ACT.Copy).then_inc(s_act_hi, 1)
                    for m in range(ROUND):
                        split(At(base + r * ROUND + m + 2, b))

                round_of(0)
                if rounds > 2:
                    with c.loop(rounds - 2) as b:
                        round_of(1, b)
                if rounds > 1:
                    round_of(rounds - 1)

            def norm_sums(scale=1.0 / D, src=None, dst=None):
                act.wait_ge(s_sums, c.next(s_sums))
                src = ps[:, 4, 0:SEQ] if src is None else src
                dst = rstd[:, 0:SEQ] if dst is None else dst
                A(dst, src, ACT.Sqrt, bias=eps[0:dst.shape[0], :], scale=scale).then_inc(s_root, 1)

            def square_x(cols, updated=True):
                for k in X_ORDER:
                    if updated:
                        act.wait_ge(s_x_tile, c.next(s_x_tile))
                    A(sq[:, k, 0:cols.stop - cols.start], x[:, k, cols], ACT.Square).then_inc(s_squares, 1)

            def norm_one(layer, which):
                square_x(one, updated=(layer, which) != (0, 0))
                norm_sums()
                for k in range(KT):
                    act.wait_ge(s_h_scaled, c.next(s_h_scaled))
                    at = layer * 48 + (0 if which == 0 else 24) + k
                    A(h_hi[:, k, 0:SEQ], h[:, k, 0:SEQ], ACT.Identity, bias=mods[:, at:at + 1])
                    A(h[:, k, 0:SEQ], h[:, k, 0:SEQ], ACT.Identity, bias=mods[:, at:at + 1]).then_inc(s_act_hi, 1)

            def norm_two():
                square_x(two)
                norm_sums(src=ps[:, 4, 0:TOK], dst=rstd[:, :])
                for k in range(KT):
                    act.wait_ge(s_h_whole, c.next(s_h_whole))
                    A(h_hi[:, k, :], h[:, k, :], ACT.Copy).then_inc(s_act_hi, 1)

            def norm_post():
                act.wait_ge(s_out_ready, c.next(s_out_ready))
                A(fo, ps[:, :, 0:TOK], ACT.Copy)
                A(sq, ps[:, :, 0:TOK], ACT.Square).then_inc(s_fo_copied, 1)
                norm_sums(src=ps[:, 4, 0:TOK], dst=rstd[:, :])
                meet(c, s_met)

            act.wait_ge(s_consts_in, c.next(s_consts_in, 64))
            act.wait_ge(s_memsets, c.next(s_memsets, 6))
            A(cact, par("c", 0, 8), ACT.Silu).then_inc(s_c_act, 1)
            act.wait_ge(s_rope_args, c.next(s_rope_args))
            A(sinT, rope[:, 4, :], ACT.Sin)
            A(cosT, rope[:, 5, :], ACT.Sin, bias=half_pi, scale=-1.0).then_inc(s_rope_ready, 1)
            with c.loop(12, raw_free=16) as b:
                for j in range(2):
                    act.wait_ge(s_raw_free, c.next(s_raw_free, 8))
                    A(ada_row.rearrange("p (s n) -> p s n", n=BANK)[:, b * 2 + j, :], ps[0:1, j, :],
                      ACT.Copy).then_inc(s_ada_row, 1)
            split(At(ADA_UNITS))
            split(At(ADA_UNITS + 1))
            meet(c, s_met)

            if on["ret"]:
                norm_one(0, 0)
                take("ret_in", 0, 2, lambda m: qk[:, m, :], ACT.Copy)
                take("ret_in", 16, 2, lambda m: vT[:, m, :], ACT.Copy)
                take("ret_in", 32, 2, lambda m: gT[:, m, :], ACT.Silu)
                meet(c, s_met)
                for n in range(8):
                    act.wait_ge(s_vt_ready, c.next(s_vt_ready))
                    A(vtok.rearrange("p j (m f) -> p m j f", f=P)[:, 2 * n:2 * n + 2],
                      ps[:, n, :].rearrange("p (m j f) -> p m j f", m=2, j=2), ACT.Copy).then_inc(s_vt_copied, 1)
                for m in range(16):
                    act.wait_ge(s_y_ready, c.next(s_y_ready))
                    A(yT[:, m, :], ps[:, 4 + m % 4, 0:SEQ], ACT.Copy).then_inc(s_y_copied, 1)
                act.wait_ge(s_y_copied, c.next(s_y_copied, 16))
                A(ysq, yT, ACT.Square).then_inc(s_squares, 1)
                norm_sums(1.0 / RDV, ps[:, 0:2, :], yrs.rearrange("p (a b) t -> p a (b t)", a=2))
                meet(c, s_met)
                feed("ret_out", yT, SEQ)

            def peer(layer):
                norm_one(layer, 1)
                meet(c, s_met)
                take(f"query{layer}", 0, 2, lambda m: qT[:, m, :], ACT.Copy)
                for n in range(8):
                    act.wait_ge(s_key_scores, c.next(s_key_scores))
                    A(sc[:, n // 4, (n % 4) * 4:(n % 4) * 4 + 4, :], ps[:, n, :].rearrange("p (m f) -> p m f", f=P),
                      ACT.Copy).then_inc(s_key_copied, 1)
                take(f"u{layer}", 0, EARLY // ROUND, lambda m: G[:, m, :], ACT.Gelu_apprx_tanh)
                act.wait_ge(s_gate_in, c.next(s_gate_in))
                A(picked[:, :, 2, :], picked[:, :, 2, :], ACT.Exp).then_inc(s_gate_exp, 1)
                act.wait_ge(s_tables_ready, c.next(s_tables_ready))
                A(chosen[:], ps[:, 4:7, 0:SEQ], ACT.Copy).then_inc(s_chosen_ready, 1)
                act.wait_ge(s_chosen_ready, c.next(s_chosen_ready))
                gates = chosen[:, 2, :].rearrange("p (g t) -> p g t", t=4)

                def gate_picks(g, buf):
                    act.wait_ge(s_onehots, c.next(s_onehots))
                    for q in range(4):
                        last = A(pick[:, buf, 0, q, :], pick[:, buf, 0, q, :], ACT.Copy, scale=gates[:, g, q:q + 1])
                    last.then_inc(s_picks_ready, 1)

                def gate_round(b, tile, group, groups, ends=False):
                    for j in range(ROUND):
                        at = At(first[f"u{layer}"] + tile + j, b)
                        split(at.plus(2))
                        act.wait_ge(s_half_used, at.halves(2))
                        A(ps[:, j % 4, 0:SEQ], ps[:, j % 4, 0:SEQ], ACT.Gelu_apprx_tanh).then_inc(s_gelu_done, 1)
                        for k in groups_at(j, groups):
                            if not (ends and k == groups - 1):
                                gate_picks(at_round(b, groups, group + k + 1), (k + 1) % 2)

                gate_picks(0, 0)
                for rounds, tile, group, groups in GATE_ROUNDS:
                    ends = tile + rounds * ROUND == P
                    with c.loop(rounds - ends, onehots=groups) as b:
                        gate_round(b, tile, group, groups)
                    if ends:
                        gate_round(None, tile + (rounds - 1) * ROUND, group + (rounds - 1) * groups, groups, True)
                base = first[f"v{layer}"]

                def mix(i, j):
                    A(mixed_hi[:, j % 2, :], G[:, i, :], ACT.Copy).then_inc(s_act_hi, 1)

                act.wait_ge(s_g_applied, c.next(s_g_applied))
                mix(0, 0)
                mix(1, 1)
                with c.loop(P // ROUND - 1) as b:
                    for j in range(ROUND):
                        at = At(base + j, b)
                        split(at.plus(2))
                        act.wait_ge(s_half_used, at.halves(2))
                        mix(b * ROUND + (j + 2), j)
                for i in range(P - ROUND, P):
                    split(At(base + i + 2))
                    if i + 2 < P:
                        act.wait_ge(s_half_used, At(base + i).halves(2))
                        mix(i + 2, i)
                meet(c, s_met)

            if on["peer0"]:
                peer(0)

            if on["sgu"]:
                norm_one(1, 0)
                take("sgu_in", 0, 6, lambda m: view(0, 48, SEQ)[:, m, :], ACT.Gelu_apprx_tanh, bias=lambda m: par("sgu_b_in", 0, 48)[:, m:m + 1]
                     if isinstance(m, int) else par("sgu_b_in", 0, 48).unsqueeze(2)[:, m, :])
                for m in range(0, ST_, THIRD):
                    act.wait_ge(s_sgu_centred, c.next(s_sgu_centred))
                    A(ssq[:, m:m + THIRD, :], sv[:, m:m + THIRD, :], ACT.Square).then_inc(s_squares, 1)
                norm_sums(1.0 / SH, ps[:, 4, 0:SEQ], srstd)
                for n in range(12):
                    act.wait_ge(s_vt_ready, c.next(s_vt_ready))
                    A(svtok.rearrange("p j (m f) -> p m j f", f=P)[:, 2 * n:2 * n + 2],
                      ps[:, n % 4, :].rearrange("p (m j f) -> p m j f", m=2, j=2), ACT.Copy).then_inc(s_vt_copied, 1)
                meet(c, s_met)
                feed("sgu_out", uT, SEQ)
                meet(c, s_met)

            if on["peer1"]:
                peer(1)
            if on["final1"]:
                square_x(one)
                norm_sums()

            if on["att"]:
                act.wait_ge(s_tabs_in, c.next(s_tabs_in, 48))
                norm_two()
                take("att_in", 0, 3, lambda m: aqkv[:, m, :], ACT.Copy)
                take("att_in", 24, 1, lambda m: aog[:, m, :], ACT.Sigmoid)
                act.wait_ge(s_bank_free, 4 + blocks_before["att_in"] + 32)
                A(asq, aqk, ACT.Square).then_inc(s_squares, 1)
                norm_sums(1.0 / ADH, ps[0:32, 6, 0:TOK], row_rstd)
                for n in range(8):
                    act.wait_ge(s_vt_ready, c.next(s_vt_ready))
                    A(avtok[0:META, 0, n * P:n * P + P], ps[0:META, n % 4, 0:P], ACT.Copy)
                    A(avtok[:, 1:3, n * P:n * P + P], ps[:, n % 4, P:3 * P].rearrange("p (a f) -> p a f", a=2),
                      ACT.Copy).then_inc(s_vt_copied, 1)
                act.wait_ge(s_logit_in, c.next(s_logit_in))
                c.link(A(awork[:, 1], awork[:, 1], ACT.Exp))
                A(awork[:, 1], awork[:, 1], ACT.Ln, bias=1.0).then_inc(s_logit_exp, 1)
                meet(c, s_met)
                for pr in range(AH // 2):
                    for par_ in range(2):
                        for tt, (s, n) in enumerate(TILES):
                            k = 3 * par_ + tt
                            act.wait_ge(s_att_m, c.next(s_att_m))
                            A(ap_[0:n, par_, tt, 0:s + n], ps[0:n, k, 0:s + n], ACT.Exp, bias=asm[0:n, 0, k:k + 1],
                              accum_out=asm[0:n, 1, k:k + 1]).then_inc(s_att_p, 1)
                    for par_ in range(2):
                        for tt, (s, n) in enumerate(TILES):
                            k = 3 * par_ + tt
                            act.wait_ge(s_att_t, c.next(s_att_t))
                            last = A(apT[0:META, par_, tt, 0, 0:n], ps[0:META, k, 0:n], ACT.Copy)
                            if tt:
                                last = A(apT[:, par_, tt, 1:tt + 1, 0:n],
                                         ps[:, k, P:P * (tt + 1)].rearrange("p (a f) -> p a f", f=P), ACT.Copy)
                            last.then_inc(s_att_tc, 1)
                meet(c, s_met)
                feed("att_out", ay, TOK)
                norm_post()

            def ffn(n):
                norm_two()
                c.n[s_bank_free.name] = 4 + blocks_before[f"up{n}"]
                w3 = par("ffn_conv", n * 132, 132).rearrange("p (b w) -> p b w", w=3)
                with c.loop(11, bank_free=4) as b:
                    for j in range(4):
                        at = At(first[f"up{n}"] + j, b, 4)
                        split(at.plus(2))
                        act.wait_ge(s_half_used, at.halves(2))
                        A(fconv[:, 0, j, :], ps[:, j, 0:TOK], ACT.Copy, scale=w3[:, b * 4 + j, 2:3]).then_inc(s_tap_done, 1)
                        if j % 2:
                            act.wait_ge(s_bank_free, c.next(s_bank_free))
                            A(fconv[:, 1, j - 1, :], fconv[:, 0, j - 1, :], ACT.Gelu_apprx_tanh).then_inc(s_ffn_gelu, 1)
                            c.next(s_bank_free)
                meet(c, s_met)
                feed(f"down{n}", fact, TOK)
                norm_post()

            if on["ffn0"]:
                ffn(0)

            if on["dn"]:
                norm_two()
                c.n[s_bank_free.name] = 4 + blocks_before["dn_in"]
                w4 = par("dn_conv", 0, 96).rearrange("p (b w) -> p b w", w=4)
                with c.loop(3, bank_free=8) as b:
                    for j in range(8):
                        at = At(first["dn_in"] + j, b)
                        split(at.plus(2))
                        act.wait_ge(s_half_used, at.halves(2))
                        act.wait_ge(s_dn_silu, b * 8 + (j + 1))
                        A(dwork[:, j % 2, :], ps[:, j % 4, 0:TOK], ACT.Copy, scale=w4[:, b * 8 + j, 3:4]).then_inc(s_tap_done, 1)
                        for i in (j - 1, j) if j % 2 else ():
                            act.wait_ge(s_bank_free, c.next(s_bank_free))
                            A(dqkv[:, b * 8 + i, :], dwork[:, i % 2, :], ACT.Silu).then_inc(s_dn_silu, 1)
                take("dn_in", 24, 1, lambda m: dog[:, m, :], ACT.Silu)
                act.wait_ge(s_dn_silu, 2 + 24)
                A(dsq, dqkv[:, 0:16, :], ACT.Square).then_inc(s_squares, 1)
                norm_sums(1.0, ps[0:16, 6, 0:TOK], row_rstd[0:16, :])
                act.wait_ge(s_logit_in, c.next(s_logit_in))
                A(dsm[:, :, 0, 0:8], dsm[:, :, 0, 0:8], ACT.Sigmoid)
                c.link(A(dsm[:, :, 5, 0:8], dsm[:, :, 5, 0:8], ACT.Exp))
                A(dsm[:, 0, 4, 8:16], par("a_log", 0, 8), ACT.Exp)
                A(dsm[:, :, 5, 0:8], dsm[:, :, 5, 0:8], ACT.Ln, bias=1.0).then_inc(s_logit_exp, 1)
                meet(c, s_met)
                for ch, (s, n) in enumerate(TILES):
                    act.wait_ge(s_logit_in, c.next(s_logit_in))
                    A(dsm[0:n, ch, 4, 0:8], dsm[0:n, ch, 3, 0:8], ACT.Exp)
                    for g in range(2):
                        if g:
                            act.wait_ge(s_logit_in, c.next(s_logit_in))
                        here = slice(4 * g, 4 * g + 4)
                        A(ddec[0:n, here, 0:n], ddec[0:n, here, 0:n], ACT.Exp)
                        A(dER[:, here, 0:n], heads4(g, P, n), ACT.Exp).then_inc(s_logit_exp, 1)
                act.wait_ge(s_dn_v, sum(2 * (5 + 2 * (n.bit_length() - 1)) for _, n in TILES))
                A(dsq[:, 0:8, :], dOT, ACT.Square).then_inc(s_squares, 1)
                norm_sums(1.0 / P, ps[0:16, 6, 0:TOK], row_rstd[0:16, :])
                meet(c, s_met)
                feed("dn_out", dOT, TOK)
                norm_post()
            if on["ffn1"]:
                ffn(1)

        @block.vector
        def _(v):
            c = Counts(v, s_dve_own)
            V = nc.vector
            TT, TS, STT = V.tensor_tensor, V.tensor_scalar, V.scalar_tensor_tensor

            def split(at, halves=(0, 1)):
                if at.b is None and at.unit >= limit:
                    return
                for half in halves:
                    v.wait_ge(s_hi_ready, at.halves(half + 1))
                    TT(w_lo[:, at.slot(half)], raw[:, at.raw, 4 * half:4 * half + 4, :],
                       w_hi[:, at.slot(half)].bitcast(f32), SUB).then_inc(s_raw_free, 1)

            def split_all(name, skip=0, count=None):
                base = first[name] + skip
                rounds = (count or dict(parts)[name]) // ROUND
                last = base + rounds * ROUND == limit
                if rounds - last > 0:
                    with v.Fori(0, rounds - last) as b:
                        for j in range(ROUND):
                            split(At(base + j + 2, b))
                if last:
                    for j in range(ROUND):
                        split(At(base + (rounds - 1) * ROUND + j + 2))

            def low_h(width):
                for k in range(KT):
                    v.wait_ge(s_act_hi, c.next(s_act_hi))
                    last = TT(h_lo[:, k, 0:width], h[:, k, 0:width], h_hi[:, k, 0:width].bitcast(f32), SUB)
                last.then_inc(s_h_ready, 1)

            def feed(name, src, width):
                base, rounds = first[name], dict(parts)[name] // ROUND

                def round_of(r, b=None):
                    for k in range(KT):
                        v.wait_ge(s_act_hi, c.next(s_act_hi))
                        last = TT(h_lo[:, k, 0:width], src[:, (r * KT + k) if b is None else b * KT + (r * KT + k), 0:width],
                                  h_hi[:, k, 0:width].bitcast(f32), SUB)
                        if k % 4 == 3:
                            last.then_inc(s_h_ready, 1)
                    for m in range(ROUND):
                        split(At(base + r * ROUND + m + 2, b))

                round_of(0)
                if rounds > 2:
                    with c.loop(rounds - 2, act_hi=KT) as b:
                        round_of(1, b)
                if rounds > 1:
                    round_of(rounds - 1)

            def inverse_root(dst):
                v.wait_ge(s_root, c.next(s_root))
                return V.reciprocal(dst, dst)

            def norm_one(n):
                c.link(inverse_root(rstd[:, 0:SEQ]))
                for k in range(KT):
                    STT(h[:, k, 0:SEQ], x[:, k, one], gains[:, n, k:k + 1], rstd[:, 0:SEQ], MUL, MUL).then_inc(s_h_scaled, 1)
                low_h(SEQ)

            def norm_two(gain):
                c.link(inverse_root(rstd[:, :]))
                for k in range(KT):
                    STT(h[:, k, :], x[:, k, :], gain[:, k:k + 1], rstd[:, :], MUL, MUL).then_inc(s_h_whole, 1)
                low_h(TOK)

            def add_gated(src, gate):
                for k in X_ORDER:
                    STT(x[:, k, one], src(k), mods[:, gate + k:gate + k + 1], x[:, k, one], MUL, ADD).then_inc(s_x_tile, 1)

            def norm_post(gain):
                c.link(inverse_root(rstd[:, :]))
                for k in range(KT):
                    STT(fo[:, k, :], fo[:, k, :], gain[:, k:k + 1], rstd[:, :], MUL, MUL)
                meet(c, s_met)
                for k in X_ORDER:
                    TT(x[:, k, :], x[:, k, :], fo[:, k, :], ADD).then_inc(s_x_tile, 1)

            v.wait_ge(s_consts_in, c.next(s_consts_in, 64))
            v.wait_ge(s_memsets, c.next(s_memsets, 6))
            c.link(V.tensor_copy(rope[:, 0, :], posn))
            c.link(TS(rope[:, 1, :], rope[:, 0, :], inv_freq, None, MUL))
            c.link(TS(rope[:, 2, :], rope[:, 1, :], float(0.5 / np.pi), 12582912.0, MUL, ADD))
            c.link(TS(rope[:, 2, :], rope[:, 2, :], -12582912.0, None, ADD))
            for k, piece in enumerate(TWO_PI_PARTS):
                c.link(STT(rope[:, 1, :], rope[:, 2, :], -piece, rope[:, 1, :], MUL, ADD))
            c.link(TS(rope[:, 4, :], rope[:, 1, :], -3.1415925, 3.1415925, ALU.max, ALU.min))
            STT(rope[:, 5, :], rope[:, 4, :], -1.0, rope[:, 4, :], MUL, ALU.max).then_inc(s_rope_args, 1)
            v.wait_ge(s_ada_t, c.next(s_ada_t))
            c.link(TT(mods[:], ps[:, 2, 0:96], par("ada_b", 0, 96), ADD))
            for n in range(4):
                layer, which = n // 2, n % 2
                at = layer * 48 + 8 + 24 * which
                gain = par("norm_ffn" if which else "norm_mix", layer * 8, 8)
                STT(gains[:, n, :], mods[:, at:at + 8], 1.0, gain, ADD, MUL)
            split(At(ADA_UNITS))
            split(At(ADA_UNITS + 1))
            meet(c, s_met)

            if on["ret"]:
                norm_one(0)
                split_all("ret_in", 0, 16)
                v.wait_ge(s_rope_ready, c.next(s_rope_ready))
                pair = qk.rearrange("p (m two) t -> p m two t", two=2)
                x1, x2 = pair[:, :, 0, :], pair[:, :, 1, :]
                halves = (slice(0, 4), slice(4, 8))
                cosb, sinb = bc(cosT, 1, [P, 4, SEQ]), bc(sinT, 1, [P, 4, SEQ])
                prod = [ropet[:, k, :].rearrange("p (m t) -> p m t", m=8) for k in range(4)]
                steps = [(prod[k][:, m], (x1, x2, x1, x2)[k][:, m], (cosb, sinb, sinb, cosb)[k], MUL)
                         for m in halves for k in range(4)]
                steps += [(x1[:, m], prod[0][:, m], prod[1][:, m], SUB) for m in halves]
                steps += [(x2[:, m], prod[2][:, m], prod[3][:, m], ADD) for m in halves]
                for j in range(16):
                    split(At(first["ret_in"] + 16 + j + 2))
                    if j == 0:
                        v.wait_ge(s_bank_free, 4 + blocks_before["ret_in"] + 16)
                    if j < len(steps):
                        rotated, one_side, other, op = steps[j]
                        c.link(TT(rotated, one_side, other, op))
                split_all("ret_in", 32, 16)
                meet(c, s_met)
                v.wait_ge(s_ret_in, c.next(s_ret_in, 16))
                for hd in range(RH):
                    v.wait_ge(s_scores_ready, c.next(s_scores_ready))
                    TT(sT[:, hd], ps[:, hd, :].rearrange("p (j t) -> p j t", j=2), ret_dec[:, :, hd, :],
                       MUL).then_inc(s_decayed, 1)
                v.wait_ge(s_squares, c.next(s_squares, KT + 1))
                TT(yT, yT, gT, MUL)
                c.link(inverse_root(yrs))
                yv = yT.rearrange("p (g b) t -> p g b t", g=RH)
                TT(yv, yv, bc(yrs, 2, [P, RH, 4, SEQ]), MUL)
                meet(c, s_met)
                feed("ret_out", yT, SEQ)
                v.wait_ge(s_acc_done, c.next(s_acc_done))
                add_gated(lambda k: ps[:, k, 0:SEQ], 16)

            def top16(src, rest, vals, idx, rows, ahead):
                for r in rows:
                    last = V.max(vals(r)[:, 0:8], src(r))
                    if r != rows[-1]:
                        ahead(r)
                c.link(last)
                for r in rows:
                    V.max_index(idx(r)[:, 0:8], vals(r)[:, 0:8], src(r))
                    last = V.match_replace(rest(r), vals(r)[:, 0:8], src(r), -3e38)
                    if r != rows[-1]:
                        ahead(r)
                c.link(last)
                for r in rows:
                    last = V.max(vals(r)[:, 8:16], rest(r))
                    if r != rows[-1]:
                        ahead(r)
                c.link(last)
                for r in rows:
                    last = V.max_index(idx(r)[:, 8:16], vals(r)[:, 8:16], rest(r))
                    if r != rows[-1]:
                        ahead(r)
                c.link(last)

            def peer(layer):
                norm_one(2 * layer + 1)
                meet(c, s_met)
                split_all(f"query{layer}")
                base = first[f"u{layer}"]
                split_next = [0]

                def ahead(every, r):
                    if r % every == 0 and split_next[0] < EARLY:
                        split(At(base + split_next[0] + 2))
                        split_next[0] += 1

                v.wait_ge(s_key_copied, c.next(s_key_copied, 8))
                for tt in range(2):
                    top16(lambda m: sc[:, tt, m, :], lambda m: sc2[:, m, :], lambda m: tv[:, tt, m, :],
                          lambda m: ti[:, tt, m, :], range(16), lambda r: ahead(4, r))
                    V.tensor_copy(tif[:, tt], ti[:, tt])
                    first_k = tv[:, tt].rearrange("p (g two) k -> p g two k", two=2)
                    c.link(TT(cand.rearrange("p g (a b) -> p g a b", a=TOPK),
                              first_k[:, :, 0, :].unsqueeze(3).to_broadcast([P, HH, TOPK, TOPK]),
                              first_k[:, :, 1, :].unsqueeze(2).to_broadcast([P, HH, TOPK, TOPK]), ADD))
                    ahead(1, 0)
                    top16(lambda g: cand[:, g, :], lambda g: cand2[:, g, :], lambda g: bv[:, tt, g, :],
                          lambda g: bp[:, tt, g, :], range(HH), lambda r: ahead(4, r))
                    flat = bp[:, tt].rearrange("p g k -> p (g k)")
                    TS(bq[:, tt, 0, :], flat, 4, None, ALU.logical_shift_right)
                    c.link(TS(bq[:, tt, 1, :], flat, 15, None, ALU.bitwise_and))
                    c.link(V.tensor_copy(bqf[:, tt], bq[:, tt]))
                    for n in range(2):
                        ahead(1, 0)
                        hot = cand2.rearrange("p g (k a) -> p (g k) a", a=TOPK)
                        c.link(TT(hot, bqf[:, tt, n, :].unsqueeze(2).to_broadcast([P, P, TOPK]),
                                  bc(iota[:, 0:TOPK], 1, [P, P, TOPK]), ALU.is_equal))
                        ahead(1, 0)
                        hot4 = cand2.rearrange("p g (k a) -> p g k a", a=TOPK)
                        index = tif[:, tt].rearrange("p (g two) a -> p g two a", two=2)[:, :, n, :]
                        c.link(TT(hot4, hot4, index.unsqueeze(2).to_broadcast([P, HH, TOPK, TOPK]), MUL))
                        ahead(1, 0)
                        c.link(V.tensor_reduce(picked[:, tt, n, :], hot, op=ADD, axis=AX))
                    last = TT(picked[:, tt, 2, :].rearrange("p (g k) -> p g k", k=TOPK), bv[:, tt],
                              bv[:, tt, :, 0:1].to_broadcast([P, HH, TOPK]), SUB)
                last.then_inc(s_gate_in, 1)
                while split_next[0] < EARLY:
                    ahead(1, 0)
                v.wait_ge(s_gate_exp, c.next(s_gate_exp))
                gates = picked[:, :, 2, :].rearrange("p t (g k) -> p t g k", k=TOPK)
                c.link(V.tensor_reduce(gsum, gates, op=ADD, axis=AX))
                c.link(V.reciprocal(gsum, gsum))
                TT(gates, gates, gsum.unsqueeze(3).to_broadcast([P, 2, HH, TOPK]), MUL).then_inc(s_picked_ready, 1)
                v.wait_ge(s_chosen_ready, c.next(s_chosen_ready))

                keys4 = chosen[:, 0:2, :].rearrange("p n (g t) -> p g n t", t=4)
                by_token = G.rearrange("p i (g t) -> p g t i", t=4)

                def onehots(g, buf):
                    TT(pick[:, buf], iota.unsqueeze(1).unsqueeze(1).to_broadcast([P, 2, 4, P]),
                       keys4[:, g].unsqueeze(3).to_broadcast([P, 2, 4, P]), ALU.is_equal).then_inc(s_onehots, 1)

                def gate_round(b, tile, group, groups, ends=False):
                    for j in range(ROUND):
                        split(At(base + tile + j + 2, b))
                        i = at_round(b, ROUND, tile + j)
                        v.wait_ge(s_gelu_done, c.next(s_gelu_done))
                        v.wait_ge(s_dve_own, c.value(s_dve_own))
                        TT(G[:, i, :], ps[:, j % 4, 0:SEQ], G[:, i, :], MUL).then_inc(s_bank_free, 1)
                        for n, k in enumerate(groups_at(j, groups)):
                            g = at_round(b, groups, group + k)
                            if n == 0:
                                v.wait_ge(s_bank_free, c.next(s_bank_free))
                            v.wait_ge(s_g_banks, c.next(s_g_banks))
                            TT(by_token[:, g], ps[:, 4 + k % 2, :].rearrange("p (t i) -> p t i", t=4), by_token[:, g],
                               MUL).then_inc(s_dve_own, 1)
                            c.next(s_dve_own)
                            if not (ends and k >= groups - 2):
                                onehots(at_round(b, groups, group + k + 2), k % 2)

                onehots(0, 0)
                onehots(1, 1)
                c.n[s_bank_free.name] = 4 + blocks_before[f"u{layer}"] + EARLY
                v.wait_ge(s_bank_free, c.value(s_bank_free))
                v.wait_ge(s_g_ones, c.next(s_g_ones))
                for rounds, tile, group, groups in GATE_ROUNDS:
                    ends = tile + rounds * ROUND == P
                    with c.loop(rounds - ends, gelu_done=ROUND, bank_free=ROUND, g_banks=groups, dve_own=groups) as b:
                        gate_round(b, tile, group, groups)
                    if ends:
                        gate_round(None, tile + (rounds - 1) * ROUND, group + (rounds - 1) * groups, groups, True)
                v.wait_ge(s_dve_own, c.value(s_dve_own))
                v.engine_nop().then_inc(s_g_applied, 1)
                base = first[f"v{layer}"]

                def mix(i, j):
                    v.wait_ge(s_act_hi, c.next(s_act_hi))
                    TT(mixed_lo[:, j % 2, :], G[:, i, :], mixed_hi[:, j % 2, :].bitcast(f32), SUB).then_inc(s_mix_done, 1)

                mix(0, 0)
                mix(1, 1)
                with c.loop(P // ROUND - 1, act_hi=ROUND) as b:
                    for j in range(ROUND):
                        split(At(base + j + 2, b))
                        mix(b * ROUND + (j + 2), j)
                for i in range(P - ROUND, P):
                    split(At(base + i + 2))
                    if i + 2 < P:
                        mix(i + 2, i)
                v.wait_ge(s_acc_done, c.next(s_acc_done))
                meet(c, s_met)
                add_gated(lambda k: ps[:, 4 + k // 2, (k % 2) * SEQ:(k % 2) * SEQ + SEQ], 48 * layer + 40)

            if on["peer0"]:
                peer(0)

            if on["sgu"]:
                norm_one(2)
                split_all("sgu_in")
                v.wait_ge(s_mean_sum, c.next(s_mean_sum))
                c.link(TS(smean, ps[:, 4, 0:SEQ], 1.0 / SH, None, MUL))
                for m in range(0, ST_, THIRD):
                    TT(sv[:, m:m + THIRD, :], sv[:, m:m + THIRD, :], bc(smean, 1, [P, THIRD, SEQ]),
                       SUB).then_inc(s_sgu_centred, 1)
                c.link(inverse_root(srstd))

                def scale(m):
                    TT(sv[:, m:m + THIRD, :], sv[:, m:m + THIRD, :], bc(srstd, 1, [P, THIRD, SEQ]), MUL).then_inc(s_dve_own, 1)

                scale(0)
                for third in range(3):
                    if third < 2:
                        scale((third + 1) * THIRD)
                    v.wait_ge(s_dve_own, c.next(s_dve_own))
                    for m in range(third * THIRD, (third + 1) * THIRD):
                        last = TS(sv[:, m, :], sv[:, m, :], par("sgu_ln_g", m), par("sgu_ln_b", m), MUL, ADD)
                    last.then_inc(s_sgu_ready, 1)
                for n in range(12):
                    v.wait_ge(s_spatial_ready, c.next(s_spatial_ready))
                    TT(uT[:, 2 * n:2 * n + 2, :], ps[:, 4 + n % 4, :].rearrange("p (m t) -> p m t", m=2),
                       uT[:, 2 * n:2 * n + 2, :], MUL).then_inc(s_sgu_s, 1)
                meet(c, s_met)
                feed("sgu_out", uT, SEQ)
                v.wait_ge(s_acc_done, c.next(s_acc_done))
                meet(c, s_met)
                add_gated(lambda k: ps[:, k, 0:SEQ], 48 + 16)

            if on["peer1"]:
                peer(1)
            if on["final1"]:
                c.link(inverse_root(rstd[:, 0:SEQ]))
                for k in X_ORDER:
                    STT(x[:, k, one], x[:, k, one], par("norm_final", k), rstd[:, 0:SEQ], MUL, MUL).then_inc(s_x_tile, 1)

            if on["att"]:
                v.wait_ge(s_tabs_in, c.next(s_tabs_in, 48))
                norm_two(par("mix_pre", 0, 8))
                split_all("att_in")
                TS(qgain, par("q_gain"), ADH ** -0.5, None, MUL)
                c.link(V.memset(awork[:, 0:2], 0.0))
                v.wait_ge(s_scores_ready, c.next(s_scores_ready))
                for tt, (s, n) in enumerate(TILES):
                    last = TT(awork[0:n, 0, tt, :], ps[0:n, 5, tt * 16:tt * 16 + 16], par("b_forget", 0, 16)[0:n, :], ADD)
                c.link(last)
                STT(awork[:, 1], awork[:, 0], -1.0, awork[:, 0], MUL, ALU.min).then_inc(s_logit_in, 1)
                v.wait_ge(s_root, c.next(s_root))
                V.reciprocal(row_rstd, row_rstd).then_inc(s_inv, 1)
                for b in range(16):
                    v.wait_ge(s_norms, c.next(s_norms))
                    STT(aqk[:, b, :], aqk[:, b, :], qgain if b < 8 else par("k_gain"), ps[:, b % 4, 0:TOK], MUL,
                        MUL).then_inc(s_scaled, 1)
                v.wait_ge(s_logit_exp, c.next(s_logit_exp))
                c.link(STT(alf[:, :, 0:16], awork[:, 0], 0.0, awork[:, 1], ALU.min, SUB))
                TS(alf[:, :, 16:32], alf[:, :, 0:16], -1.0, None, MUL).then_inc(s_heads_prep, 1)
                v.wait_ge(s_cum_ready, c.next(s_cum_ready))
                V.tensor_copy(acum, ps[0:32, 5, 0:TOK])
                meet(c, s_met)
                half = tab("half", 32)
                for pr in range(AH // 2):
                    for par_ in range(2):
                        hd = 2 * pr + par_
                        TS(aL[0:32, par_, :], acum, half[:, 0:1], tab("selbot", 32)[:, hd:hd + 1], MUL, ADD)
                        TS(aR[0:32, par_, :], acum, half[:, 1:2], tab("seltop", 32)[:, hd:hd + 1], MUL,
                           ADD).then_inc(s_heads_prep, 1)
                    for par_ in range(2):
                        for tt, (s, n) in enumerate(TILES):
                            k = 3 * par_ + tt
                            v.wait_ge(s_att_s, c.next(s_att_s))
                            c.link(TT(ps[0:n, k, s:s + n], ps[0:n, k, s:s + n], tab("causal")[0:n, 0:n], ADD))
                            V.tensor_reduce(asm[0:n, 0, k:k + 1], ps[0:n, k, 0:s + n], op=ALU.max, axis=AX,
                                            negate=True).then_inc(s_att_m, 1)
                    for par_ in range(2):
                        for tt, (s, n) in enumerate(TILES):
                            k = 3 * par_ + tt
                            v.wait_ge(s_att_p, c.next(s_att_p))
                            c.link(V.reciprocal(asm[0:n, 1, k:k + 1], asm[0:n, 1, k:k + 1]))
                            TS(ap_[0:n, par_, tt, 0:s + n], ap_[0:n, par_, tt, 0:s + n], asm[0:n, 1, k:k + 1], None,
                               MUL).then_inc(s_att_pn, 1)
                    v.wait_ge(s_att_o, c.next(s_att_o))
                    TT(ay[:, pr, :], ps[:, 6, 0:TOK], aog[:, pr, :], MUL).then_inc(s_att_od, 1)
                meet(c, s_met)
                feed("att_out", ay, TOK)
                norm_post(par("mix_post", 0, 8))

            def conv(at, dst, src, w, taps):
                split(at, (0,))
                v.wait_ge(s_tap_done, c.next(s_tap_done))
                for back in range(1, taps):
                    last = STT(dst[:, back:TOK], src[:, 0:TOK - back], w(taps - 1 - back), dst[:, back:TOK], MUL, ADD)
                    if back < taps - 1:
                        last.then_inc(s_dve_own, 1)
                        if back == 1:
                            split(at, (1,))
                        v.wait_ge(s_dve_own, c.next(s_dve_own))
                last.then_inc(s_bank_free, 1)

            def ffn(n):
                norm_two(par("ffn_pre", 8 * n, 8))
                c.n[s_bank_free.name] = 4 + blocks_before[f"up{n}"]
                w3 = par("ffn_conv", n * 132, 132).rearrange("p (b w) -> p b w", w=3)
                with c.loop(11, tap_done=4, bank_free=4, ffn_gelu=2, dve_own=4) as b:
                    for q in range(2):
                        for j in (2 * q, 2 * q + 1):
                            conv(At(first[f"up{n}"] + j + 2, b, 4), fconv[:, 0, j, :], ps[:, j, 0:TOK],
                                 lambda k: w3[:, b * 4 + j, k:k + 1], 3)
                        v.wait_ge(s_bank_free, c.next(s_bank_free, 2))
                        v.wait_ge(s_ffn_gelu, c.next(s_ffn_gelu))
                        TT(fact[:, b * 2 + q, :], fconv[:, 1, 2 * q, :], fconv[:, 0, 2 * q + 1, :], MUL)
                meet(c, s_met)
                feed(f"down{n}", fact, TOK)
                norm_post(par("ffn_post", 8 * n, 8))

            if on["ffn0"]:
                ffn(0)

            if on["dn"]:
                v.wait_ge(s_tabs_in, c.next(s_tabs_in, 16))
                norm_two(par("mix_pre", 8, 8))
                w4 = par("dn_conv", 0, 96).rearrange("p (b w) -> p b w", w=4)
                with c.loop(3, tap_done=8, dve_own=16) as b:
                    for j in range(8):
                        conv(At(first["dn_in"] + j + 2, b), dwork[:, j % 2, :], ps[:, j % 4, 0:TOK],
                             lambda k: w4[:, b * 8 + j, k:k + 1], 4)
                split_all("dn_in", 24, 8)
                c.link(V.memset(dsm, 0.0))
                v.wait_ge(s_scores_ready, c.next(s_scores_ready))
                for tt, (s, n) in enumerate(TILES):
                    V.tensor_copy(dsm[0:n, tt, 0, 0:8], ps[0:n, 5, tt * 16:tt * 16 + 8])
                    last = TT(dsm[0:n, tt, 1, 0:8], ps[0:n, 5, tt * 16 + 8:tt * 16 + 16], par("dt_bias", 0, 8)[0:n, :], ADD)
                c.link(last)
                STT(dsm[:, :, 5, 0:8], dsm[:, :, 1, 0:8], -1.0, dsm[:, :, 1, 0:8], MUL, ALU.min).then_inc(s_logit_in, 1)
                v.wait_ge(s_root, c.next(s_root))
                V.reciprocal(row_rstd[0:16, :], row_rstd[0:16, :]).then_inc(s_inv, 1)
                for b in range(16):
                    v.wait_ge(s_norms, c.next(s_norms))
                    STT(dqkv[:, b, :], dqkv[:, b, :], P ** -0.5 if b < 8 else 1.0, ps[:, b % 4, 0:TOK], MUL,
                        MUL).then_inc(s_scaled, 1)
                v.wait_ge(s_logit_exp, c.next(s_logit_exp))
                c.link(STT(dsm[:, :, 1, 0:8], dsm[:, :, 1, 0:8], 0.0, dsm[:, :, 5, 0:8], ALU.max, ADD))
                STT(dsm[:, :, 2, 0:8], dsm[:, :, 1, 0:8], -1.0, bc(dsm[:, 0, 4, 8:16], 1, [P, 3, 8]), MUL, MUL)
                V.memset(dST, 0.0)
                meet(c, s_met)
                for ch, (s, n) in enumerate(TILES):
                    beta = dsm[0:n, ch, 0, 0:8]
                    beta_n = lambda here: beta[:, here].unsqueeze(2).to_broadcast([n, 4, n])
                    levels = n.bit_length() - 1
                    groups = (slice(0, 4), slice(4, 8))
                    mask = tab("levels").rearrange("p (l c) -> p l c", l=LEVELS)

                    def masked(lv, here):
                        return TT(dMT[0:n, here, 0:n], dLT[0:n, here, 0:n], bc(mask[0:n, lv, 0:n], 1, [n, 4, n]), MUL)

                    for g, here in enumerate(groups):
                        v.wait_ge(s_dn_p, c.next(s_dn_p))
                        if g == 0:
                            c.link(V.tensor_copy(dsm[0:n, ch, 3, 0:8], ps[0:n, 2, 0:8]))
                        c.link(TT(ddec[0:n, here, 0:n], heads4(g, n, n),
                                  dsm[0:n, ch, 3, 0:8][:, here].unsqueeze(2).to_broadcast([n, 4, n]), SUB))
                        TT(ddec[0:n, here, 0:n], ddec[0:n, here, 0:n], bc(tab("mneg")[0:n, 0:n], 1, [n, 4, n]),
                           ADD).then_inc(s_logit_in, 1)
                    V.tensor_copy(dX[0:n, :, 0:n], bc(ident[0:n, 0:n], 1, [n, 8, n]))
                    V.tensor_copy(dXT[0:n, :, 0:n], bc(ident[0:n, 0:n], 1, [n, 8, n]))
                    for g, here in enumerate(groups):
                        v.wait_ge(s_logit_exp, c.next(s_logit_exp))
                        TT(dLT[0:n, here, 0:n], heads4(4 + g, n, n), ddec[0:n, here, 0:n], MUL)
                        TT(dqd[:, here, 0:n], dqkv[:, here, s:s + n], dER[:, here, 0:n], MUL)
                        if g == 0:
                            TT(dsm[0:n, ch, 4, 0:8], dsm[0:n, ch, 4, 0:8], beta, MUL)
                        TT(dQK[0:n, here, 0:n], heads4(6 + g, n, n), ddec[0:n, here, 0:n], MUL).then_inc(s_dn_v, 1)
                    for g, here in enumerate(groups):
                        v.wait_ge(s_dn_p, c.next(s_dn_p))
                        masked(0, here)
                        TT(dkb[0:n, here], heads4(g, n, P), dsm[0:n, ch, 4, 0:8][:, here].unsqueeze(2).to_broadcast([n, 4, P]), MUL)
                        TT(dkd[0:n, here], heads4(g, n, P), ddec[0:n, here, n - 1:n].to_broadcast([n, 4, P]), MUL)
                        TT(dvb[0:n, here], heads4(2 + g, n, P), beta[:, here].unsqueeze(2).to_broadcast([n, 4, P]),
                           MUL).then_inc(s_dn_v, 1)
                    for lv in range(levels):
                        for g, here in enumerate(groups):
                            v.wait_ge(s_dn_p, c.next(s_dn_p))
                            TT(dT1[0:n, here, 0:n], heads4(g, n, n), beta_n(here), MUL).then_inc(s_dn_v, 1)
                            if lv < levels - 1:
                                masked(lv + 1, here)
                        for g, here in enumerate(groups):
                            v.wait_ge(s_dn_p, c.next(s_dn_p))
                            TT(dX[0:n, here, 0:n], dX[0:n, here, 0:n], heads4(2 + g, n, n), SUB)
                            TT(dXT[0:n, here, 0:n], dXT[0:n, here, 0:n], heads4(4 + g, n, n), SUB).then_inc(s_dn_v, 1)
                    for g, here in enumerate(groups):
                        v.wait_ge(s_dn_p, c.next(s_dn_p))
                        TS(dW[:, here, 0:n], heads4(g, P, n), -1.0, None, MUL).then_inc(s_dn_v, 1)
                    for g, here in enumerate(groups):
                        v.wait_ge(s_dn_p, c.next(s_dn_p))
                        V.tensor_copy(dU[0:n, here], heads4(2 + g, n, P)).then_inc(s_dn_v, 1)
                    for g, here in enumerate(groups):
                        v.wait_ge(s_dn_p, c.next(s_dn_p))
                        c.link(TT(dST[:, here], dST[:, here], dER[:, here, n - 1:n].to_broadcast([P, 4, P]), MUL))
                        V.tensor_copy(dOT[:, here, s:s + n], heads4(4 + g, P, n))
                        TT(dST[:, here], dST[:, here], heads4(6 + g, P, P), ADD).then_inc(s_dn_v, 1)
                v.wait_ge(s_root, c.next(s_root))
                V.reciprocal(row_rstd[0:16, :], row_rstd[0:16, :]).then_inc(s_inv, 1)
                for b in range(8):
                    v.wait_ge(s_norms, c.next(s_norms))
                    last = STT(dOT[:, b, :], dOT[:, b, :], par("o_gain"), ps[:, b % 4, 0:TOK], MUL, MUL)
                    last.then_inc(s_scaled, 1)
                v.wait_ge(s_scaled, 16 + 16 + 8)
                TT(dOT, dOT, dog, MUL)
                meet(c, s_met)
                feed("dn_out", dOT, TOK)
                norm_post(par("mix_post", 8, 8))
            if on["ffn1"]:
                ffn(1)
            v.drain().then_inc(s_result_ready, 1)


def columns(a):
    a = np.asarray(a)
    return np.ascontiguousarray(a.reshape(-1, P).T)


def units_k(w):
    K, N = w.shape
    return np.ascontiguousarray(w.reshape(KT, P, N // P, P).transpose(2, 1, 0, 3))


def units_out(w):
    K = w.shape[0]
    rounds = -(-K // D)
    full = np.zeros((rounds * D, D), w.dtype)
    full[:K] = w
    return np.ascontiguousarray(full.reshape(rounds, KT, P, KT, P).transpose(0, 3, 2, 1, 4)).reshape(-1, P, KT, P)


def kernel(_until=None, **inputs):
    import concourse.bacc as bacc
    from concourse import mybir
    from concourse.bass_utils import run_bass_kernel_spmd

    a = {k: np.asarray(v) for k, v in inputs.items()}
    f32 = np.float32
    c1, c2, ret_dec = shape_constants()
    rows = lambda v: np.broadcast_to(v.reshape(1, -1), (P, v.size))
    conv = lambda w: w.T.reshape(-1, P, w.shape[0]).transpose(1, 0, 2).reshape(P, -1)
    pairs = lambda w: w.reshape(w.shape[0], 2, FFT, P).transpose(0, 2, 1, 3).reshape(w.shape[0], -1)
    twice = lambda g: np.concatenate([g, g]).reshape(P, 1)
    pieces = {
        "c": columns(a["c"]), "ada_b": columns(a["ada_b"]), "norm_mix": columns(a["norm_mix"]),
        "norm_ffn": columns(a["norm_ffn"]), "norm_final": columns(a["norm_final"]), "sgu_b_in": columns(a["sgu_b_in"]),
        "sgu_ln_g": columns(a["sgu_ln_g"]), "sgu_ln_b": columns(a["sgu_ln_b"]), "mix_pre": columns(a["norm_mix_pre_2"]),
        "mix_post": columns(a["norm_mix_post_2"]), "ffn_pre": columns(a["norm_ffn_pre_2"]),
        "ffn_post": columns(a["norm_ffn_post_2"]), "q_gain": twice(a["attn_q_norm_2"][0]),
        "k_gain": twice(a["attn_k_norm_2"][0]), "o_gain": a["dn_o_norm_2"].reshape(P, 1),
        "ffn_conv": np.concatenate([conv(pairs(w)) for w in a["ffn_conv_2"]], 1), "dn_conv": conv(a["dn_conv_2"][0]),
        "b_forget": rows(a["attn_b_forget_2"]), "a_log": rows(a["dn_a_log_2"]), "dt_bias": rows(a["dn_dt_bias_2"]),
    }
    params = np.concatenate([pieces[n] for n, _ in PCOLS], 1)
    assert params.shape == (P, PW), params.shape
    ada = a["ada_w"]
    aw, dw = a["attn_w_in_2"][0], a["dn_w_in_2"][0]
    tail = lambda w: np.ascontiguousarray(w[:, -16:].reshape(KT, P, 16).transpose(1, 0, 2))
    feed = {
        "params": params, "const1": c1, "const2": c2, "ret_dec": ret_dec,
        "xT": np.ascontiguousarray(a["x"][0].T.reshape(KT, P, SEQ).transpose(1, 0, 2)),
        "metaT": np.ascontiguousarray(a["meta_tokens_2"].T.reshape(KT, P, META).transpose(1, 0, 2)),
        "positions": np.ascontiguousarray(np.broadcast_to(a["positions"][0][None, :], (P, SEQ))),
        "ada": np.concatenate([units_k(ada[0]), units_k(ada[1])]),
        "ret_in": units_k(a["ret_w_in"][0]), "ret_out": units_out(a["ret_w_out"][0]),
        "query0": units_k(a["peer_w_query"][0]), "query1": units_k(a["peer_w_query"][1]),
        "keysT": np.ascontiguousarray(a["peer_sub_keys"].reshape(2, 16, NKEYS, P).transpose(0, 3, 1, 2)),
        "sgu_in": units_k(a["sgu_w_in"][0]), "sgu_out": units_out(a["sgu_w_out"][0]),
        "w_s": np.ascontiguousarray(a["sgu_w_s"][0].transpose(2, 0, 1)), "b_s": a["sgu_b_s"],
        "att_in": units_k(np.ascontiguousarray(aw[:, :4096])), "att_wf": tail(aw), "att_out": units_out(a["attn_w_out_2"][0]),
        "dn_in": units_k(np.ascontiguousarray(dw[:, :4096])), "dn_wf": tail(dw), "dn_out": units_out(a["dn_w_out_2"][0]),
    }
    for n in range(2):
        feed[f"u{n}"] = np.ascontiguousarray(a["peer_u"][n].reshape(P, P, KT, P).transpose(0, 3, 2, 1))
        feed[f"v{n}"] = a["peer_v"][n].reshape(P, P, KT, P)
        feed[f"up{n}"] = units_k(pairs(a["ffn_w_up_2"][n]))
        feed[f"down{n}"] = units_out(a["ffn_w_down_2"][n])

    nc = bacc.Bacc("TRN2", target_bir_lowering=False, num_devices=1)
    t = {k: nc.dram_tensor(f"in_{k}", v.shape, mybir.dt.from_np(v.dtype), kind="ExternalInput").ap()
         for k, v in feed.items()}
    t["scratch"] = nc.dram_tensor("ada_scratch", (1, 12288), mybir.dt.float32, kind="Internal").ap()
    width = SEQ if _until is None else TOK
    out = nc.dram_tensor("out_xT", (P, KT, width), mybir.dt.float32, kind="ExternalOutput").ap()
    build_program(nc, t, out, _until)
    r = run_bass_kernel_spmd(nc, [{f"in_{k}": v for k, v in feed.items()}], core_ids=[0])
    got = r.results[0]["out_xT"]
    if _until is not None:
        return got
    return np.ascontiguousarray(got.transpose(2, 1, 0)).reshape(1, SEQ, D)
```
